# Optimizing a Trainium2 kernel written in Bass

```python
import jax, jax.numpy as jnp
from jax import lax
import numpy as np

D_MODEL = 1024
BATCH = 1
SEQ = 512
DEPTH = 1

GRID_W = 64
CTX_LEN = 256

RET_HEADS = 4
RET_QK_DIM = 128
RET_V_DIM = 256
RET_CHUNK = 128
ROPE_THETA = 10000.0
RET_QK_W = RET_HEADS * RET_QK_DIM
RET_V_W = RET_HEADS * RET_V_DIM

SGU_GROUPS = 4
SGU_CHUNK = 128
SGU_WIDTH = 1024

N_EXPERTS = 16
EC_CAPACITY_FACTOR = 2
D_EXPERT = 1024

LN_EPS = 1e-6
DEEPNORM_ALPHA = (2.0 * DEPTH) ** 0.25
DEEPNORM_BETA = (8.0 * DEPTH) ** -0.25

IN_WIDTHS = (RET_QK_W, RET_QK_W, RET_V_W, RET_V_W, SGU_WIDTH, SGU_WIDTH, D_MODEL, D_MODEL)
IN_OFFSETS = tuple(sum(IN_WIDTHS[:i + 1]) for i in range(len(IN_WIDTHS) - 1))
D_IN = sum(IN_WIDTHS)

kernel_name = "hybrid_retention_sgu_ecmoe_dit"

def layer_norm(x, w=None, b=None):
    xf = x.astype(jnp.float32)
    mu = jnp.mean(xf, axis=-1, keepdims=True)
    var = jnp.mean(jnp.square(xf - mu), axis=-1, keepdims=True)
    y = (xf - mu) * lax.rsqrt(var + LN_EPS)
    if w is not None:
        y = y * w.astype(jnp.float32) + b.astype(jnp.float32)
    return y.astype(x.dtype)

def modulate(x, shift, scale):
    return layer_norm(x) * (1.0 + scale) + shift

def axial_rope_tables(n_tokens, dtype):
    rows = n_tokens // GRID_W
    r, col = jnp.meshgrid(jnp.arange(rows), jnp.arange(GRID_W), indexing="ij")
    n_freq = RET_QK_DIM // 4
    inv = ROPE_THETA ** (-jnp.arange(n_freq, dtype=jnp.float32) / n_freq)
    pos = jnp.stack([r.reshape(-1), col.reshape(-1)], axis=-1).astype(jnp.float32)
    ang = pos[..., None] * inv
    return jnp.cos(ang).astype(dtype), jnp.sin(ang).astype(dtype)

def apply_axial_rope(x, cos, sin):
    bsz, t, nh, dk = x.shape
    xs = x.reshape(bsz, t, nh, 2, 2, dk // 4)
    x1, x2 = xs[..., 0, :], xs[..., 1, :]
    c, s = cos[:, None], sin[:, None]
    return jnp.stack([x1 * c - x2 * s, x2 * c + x1 * s], axis=-2).reshape(bsz, t, nh, dk)

def split_heads(z, nh):
    bsz, t, _ = z.shape
    return z.reshape(bsz, t, nh, -1).transpose(0, 2, 1, 3)

def retention_chunked(q, k, v, log_gamma, state0):
    bsz, nh, t, dk = q.shape
    dv = v.shape[-1]
    n = t // RET_CHUNK
    q = q.reshape(bsz, nh, n, RET_CHUNK, dk)
    k = k.reshape(bsz, nh, n, RET_CHUNK, dk)
    v = v.reshape(bsz, nh, n, RET_CHUNK, dv)
    idx = jnp.arange(RET_CHUNK, dtype=jnp.float32)
    diff = idx[:, None] - idx[None, :]
    decay_mask = jnp.where(diff[None] >= 0, jnp.exp(diff[None] * log_gamma[:, None, None]), 0.0)
    scores = jnp.einsum("bhnld,bhnmd->bhnlm", q, k) * decay_mask[None, :, None].astype(q.dtype)
    intra = jnp.einsum("bhnlm,bhnmv->bhnlv", scores, v)
    zeta = jnp.exp((RET_CHUNK - 1 - idx)[None] * log_gamma[:, None])
    xi = jnp.exp((idx + 1.0)[None] * log_gamma[:, None])
    chunk_kv = jnp.einsum("bhnld,bhnlv->nbhdv", k * zeta[None, :, None, :, None], v).astype(jnp.float32)
    chunk_decay = jnp.exp(RET_CHUNK * log_gamma)[None, :, None, None]

    def step(state, kv):
        return chunk_decay * state + kv, state

    state_final, state_prev = lax.scan(step, state0, chunk_kv)
    cross = jnp.einsum("bhnld,nbhdv->bhnlv", q * xi[None, :, None, :, None], state_prev)
    out = (intra + cross).reshape(bsz, nh, t, dv)
    return out, state_final

def retention_final_state(k, v, log_gamma):
    t = k.shape[2]
    w = jnp.exp((t - 1 - jnp.arange(t, dtype=jnp.float32))[None] * log_gamma[:, None])
    return jnp.einsum("bhtd,bhtv->bhdv", k * w[None, :, :, None], v).astype(jnp.float32)

def context_retention_states(hc, w_in, b_in, decay_f, decay_b):
    lo, hi = RET_QK_W, 2 * RET_QK_W + RET_V_W
    kv = hc @ w_in[:, lo:hi] + b_in[lo:hi]
    k, v = jnp.split(kv, [RET_QK_W], axis=-1)
    k = split_heads(k, RET_HEADS) * (RET_QK_DIM ** -0.5)
    v = split_heads(v, RET_HEADS)
    sf = retention_final_state(k, v, jax.nn.log_sigmoid(decay_f.astype(jnp.float32)))
    sb = retention_final_state(jnp.flip(k, axis=2), jnp.flip(v, axis=2),
                               jax.nn.log_sigmoid(decay_b.astype(jnp.float32)))
    return sf, sb

def token_mixer(h, rope, s0f, s0b, w_in, b_in, decay_f, decay_b, gn_w, gn_b,
                sgu_ln_w, sgu_ln_b, sgu_w, sgu_b, w_pa, w_pb, w_o, b_o):
    bsz, t, _ = h.shape
    z = h @ w_in + b_in
    q, k, v, g, u, vs, ga, gb = jnp.split(z, IN_OFFSETS, axis=-1)

    q = q.reshape(bsz, t, RET_HEADS, RET_QK_DIM)
    k = k.reshape(bsz, t, RET_HEADS, RET_QK_DIM) * (RET_QK_DIM ** -0.5)
    if rope is not None:
        q = apply_axial_rope(q, *rope)
        k = apply_axial_rope(k, *rope)
    q = q.transpose(0, 2, 1, 3)
    k = k.transpose(0, 2, 1, 3)
    v = split_heads(v, RET_HEADS)
    lgf = jax.nn.log_sigmoid(decay_f.astype(jnp.float32))
    lgb = jax.nn.log_sigmoid(decay_b.astype(jnp.float32))
    o_f, sf = retention_chunked(q, k, v, lgf, s0f)
    o_b, sb = retention_chunked(jnp.flip(q, axis=2), jnp.flip(k, axis=2), jnp.flip(v, axis=2), lgb, s0b)
    o = (o_f + jnp.flip(o_b, axis=2)).transpose(0, 2, 1, 3)
    o = layer_norm(o).reshape(bsz, t, RET_V_W) * gn_w + gn_b
    ret = o.astype(h.dtype) * jax.nn.silu(g)

    u = jax.nn.gelu(u)
    vs = layer_norm(jax.nn.gelu(vs), sgu_ln_w, sgu_ln_b)
    vs = vs.reshape(bsz, t // SGU_CHUNK, SGU_CHUNK, SGU_GROUPS, SGU_WIDTH // SGU_GROUPS)
    spatial = jnp.einsum("gpq,bnqgc->bnpgc", sgu_w, vs) + sgu_b.T[None, None, :, :, None]
    sgu = u * spatial.reshape(bsz, t, SGU_WIDTH)

    y = jax.nn.sigmoid(ga) * (ret @ w_pa) + jax.nn.sigmoid(gb) * (sgu @ w_pb)
    return y @ w_o + b_o, sf, sb

def expert_choice_ffn(h, w_router, b_router, w_gate, w_up, w_down):
    bsz, t, d = h.shape
    cap = EC_CAPACITY_FACTOR * t // N_EXPERTS
    logits = (h @ w_router + b_router).astype(jnp.float32)
    affinity = jax.nn.softmax(logits, axis=-1)
    gates, idx = lax.top_k(affinity.transpose(0, 2, 1), cap)
    xs = jax.vmap(lambda hb, ib: hb[ib])(h, idx)
    hidden = jax.nn.silu(jnp.einsum("becd,edf->becf", xs, w_gate)) * jnp.einsum("becd,edf->becf", xs, w_up)
    ye = jnp.einsum("becf,efd->becd", hidden, w_down) * gates[..., None].astype(h.dtype)
    return jax.vmap(lambda yb, ib: jnp.zeros((t, d), yb.dtype).at[ib.reshape(-1)].add(yb.reshape(-1, d)))(ye, idx)

def setup_inputs(seed: int = 0) -> dict:
    key = jax.random.key(seed)
    ks = jax.random.split(key, 32)
    f32 = jnp.float32
    L, D = DEPTH, D_MODEL

    def nrm(k, shape, scale):
        return jax.random.normal(k, shape, f32) * scale

    base_decay = jnp.log(2.0 ** (5.0 + jnp.arange(RET_HEADS, dtype=f32)) - 1.0)
    return {
        "x": nrm(ks[0], (BATCH, SEQ, D), 1.0),
        "c": nrm(ks[1], (BATCH, D), 1.0),
        "ctx": nrm(ks[2], (BATCH, CTX_LEN, D), 1.0),
        "c_ctx": nrm(ks[3], (D,), 1.0),
        "w_ada": nrm(ks[4], (L, D, 6 * D), 0.5 * D ** -0.5),
        "b_ada": nrm(ks[5], (L, 6 * D), 0.02),
        "w_in": nrm(ks[6], (L, D, D_IN), D ** -0.5),
        "b_in": nrm(ks[7], (L, D_IN), 0.02),
        "ret_decay_f": base_decay[None] + nrm(ks[8], (L, RET_HEADS), 0.1),
        "ret_decay_b": base_decay[None] + nrm(ks[9], (L, RET_HEADS), 0.1),
        "ret_gn_w": 1.0 + nrm(ks[10], (L, RET_V_W), 0.02),
        "ret_gn_b": nrm(ks[11], (L, RET_V_W), 0.02),
        "sgu_ln_w": 1.0 + nrm(ks[12], (L, SGU_WIDTH), 0.02),
        "sgu_ln_b": nrm(ks[13], (L, SGU_WIDTH), 0.02),
        "sgu_w": nrm(ks[14], (L, SGU_GROUPS, SGU_CHUNK, SGU_CHUNK), SGU_CHUNK ** -0.5),
        "sgu_b": 1.0 + nrm(ks[15], (L, SGU_GROUPS, SGU_CHUNK), 0.02),
        "w_pa": nrm(ks[16], (L, RET_V_W, D), DEEPNORM_BETA * RET_V_W ** -0.5),
        "w_pb": nrm(ks[17], (L, SGU_WIDTH, D), DEEPNORM_BETA * SGU_WIDTH ** -0.5),
        "w_o": nrm(ks[18], (L, D, D), DEEPNORM_BETA * D ** -0.5),
        "b_o": nrm(ks[19], (L, D), 0.02),
        "ln1_w": 1.0 + nrm(ks[20], (L, D), 0.02),
        "ln1_b": nrm(ks[21], (L, D), 0.02),
        "w_router": nrm(ks[22], (L, D, N_EXPERTS), D ** -0.5),
        "b_router": nrm(ks[23], (L, N_EXPERTS), 0.01),
        "w_gate": nrm(ks[24], (L, N_EXPERTS, D, D_EXPERT), D ** -0.5),
        "w_up": nrm(ks[25], (L, N_EXPERTS, D, D_EXPERT), D ** -0.5),
        "w_down": nrm(ks[26], (L, N_EXPERTS, D_EXPERT, D), DEEPNORM_BETA * D_EXPERT ** -0.5),
        "ln2_w": 1.0 + nrm(ks[27], (L, D), 0.02),
        "ln2_b": nrm(ks[28], (L, D), 0.02),
    }

def reference(x, c, ctx, c_ctx, w_ada, b_ada, w_in, b_in, ret_decay_f, ret_decay_b, ret_gn_w, ret_gn_b,
              sgu_ln_w, sgu_ln_b, sgu_w, sgu_b, w_pa, w_pb, w_o, b_o, ln1_w, ln1_b,
              w_router, b_router, w_gate, w_up, w_down, ln2_w, ln2_b):
    bsz, n_tok, _ = x.shape
    rope = axial_rope_tables(n_tok, x.dtype)
    zero_state = jnp.zeros((bsz, RET_HEADS, RET_QK_DIM, RET_V_DIM), jnp.float32)

    for l in range(DEPTH):
        mod = jax.nn.silu(c) @ w_ada[l] + b_ada[l]
        mod_ctx = jax.nn.silu(c_ctx) @ w_ada[l] + b_ada[l]
        sh1, sc1, g1, sh2, sc2, g2 = jnp.split(mod[:, None, :], 6, axis=-1)
        csh1, csc1, cg1, csh2, csc2, cg2 = jnp.split(mod_ctx[None, None, :], 6, axis=-1)
        mixer_params = (w_in[l], b_in[l], ret_decay_f[l], ret_decay_b[l], ret_gn_w[l], ret_gn_b[l],
                        sgu_ln_w[l], sgu_ln_b[l], sgu_w[l], sgu_b[l], w_pa[l], w_pb[l], w_o[l], b_o[l])
        moe_params = (w_router[l], b_router[l], w_gate[l], w_up[l], w_down[l])
        last = (l + 1 == DEPTH)

        hc = modulate(ctx, csh1, csc1)
        if last:
            sf, sb = context_retention_states(hc, w_in[l], b_in[l], ret_decay_f[l], ret_decay_b[l])
        else:
            mix_c, sf, sb = token_mixer(hc, None, zero_state, zero_state, *mixer_params)

        h = modulate(x, sh1, sc1)
        mix, _, _ = token_mixer(h, rope, sf, sb, *mixer_params)
        x = layer_norm(DEEPNORM_ALPHA * x + g1 * mix, ln1_w[l], ln1_b[l])
        x = layer_norm(DEEPNORM_ALPHA * x + g2 * expert_choice_ffn(modulate(x, sh2, sc2), *moe_params),
                       ln2_w[l], ln2_b[l])

        if not last:
            ctx = layer_norm(DEEPNORM_ALPHA * ctx + cg1 * mix_c, ln1_w[l], ln1_b[l])
            ctx = layer_norm(DEEPNORM_ALPHA * ctx + cg2 * expert_choice_ffn(modulate(ctx, csh2, csc2), *moe_params),
                             ln2_w[l], ln2_b[l])
    return x


_drawn_inputs = setup_inputs


def setup_inputs(seed=0):
    import zlib

    import numpy as np

    out = dict(_drawn_inputs(seed))
    spreads = {}
    factors = {'ctx': 7.137,
     'c_ctx': 6.712,
     'b_ada': 8.0,
     'b_in': 8.0,
     'ret_decay_f': 41.296,
     'ret_decay_b': 43.368,
     'ret_gn_w': 64.0,
     'ret_gn_b': 64.0,
     'sgu_ln_w': 64.0,
     'sgu_ln_b': 64.0,
     'sgu_b': 64.0,
     'b_o': 8.0,
     'ln1_w': 8.608,
     'ln1_b': 8.0,
     'b_router': 64.0,
     'ln2_w': 9.693,
     'ln2_b': 8.544,
     'w_router': 3.928,
     'w_gate': 4.069,
     'w_up': 3.779,
     'w_down': 3.772}
    for name, (base, spread) in spreads.items():
        noise = np.random.default_rng([zlib.crc32(name.encode()), seed]).standard_normal(out[name].shape)
        drawn = base * np.exp(spread * noise) if base else spread * noise
        out[name] = __import__('jax').numpy.asarray(drawn.astype(out[name].dtype))
    for name, factor in factors.items():
        out[name] = (out[name] * factor).astype(out[name].dtype)
    return out
```

```python
from contextlib import ExitStack

import numpy as np

import concourse.bass as bass
from concourse import mybir

F32 = mybir.dt.float32
F32R = mybir.dt.float32r
ALU = mybir.AluOpType
ACT = mybir.ActivationFunctionType
AX_X = mybir.AxisListType.X

P = 128
BANKS = 8
BANK = 512
GRID_W = 64
ROPE_THETA = 10000.0
LN_EPS = 1e-6
DEPTH = 1
ALPHA = (2.0 * DEPTH) ** 0.25
CAPACITY_FACTOR = 2

SBUF_START = 16512
AREA = 7680


def place(kib):
    return SBUF_START + AREA + int((kib - 8) * 1024)


class Jobs:

    def __init__(self):
        self.number, self.bank, self.drainer = {}, {}, {}
        self.names, self.turn = [], 0

    def add(self, name, drainer, bank=None, banks=BANKS):
        if bank is None:
            bank = self.turn % banks
            self.turn = bank + 1
        self.number[name] = len(self.names) + 1
        self.bank[name], self.drainer[name] = bank, drainer
        self.names.append(name)

    def full(self, name):
        return self.number[name]

    def drained(self, name):
        return sum(self.drainer[n] == self.drainer[name] for n in self.names[:self.number[name]])

    def before(self, name):
        found = [n for n in self.names[:self.number[name] - 1] if self.bank[n] == self.bank[name]]
        return found[-1] if found else None


def shape_constants(seq, heads_dim):
    m, l = np.meshgrid(np.arange(P), np.arange(P), indexing="ij")
    p = np.arange(P)[:, None]
    ramps = np.concatenate([P - 1 - p, p, 2 * P - 1 - p, P + p], 1)
    slots = np.broadcast_to(np.arange(64)[None], (P, 64))
    table = np.concatenate([np.eye(P), slots, ramps, np.maximum(l - m, 0), np.maximum(m - l, 0),
                            l >= m, m >= l, l + 1, P - l], 1).astype(np.float32)
    t = np.arange(seq)
    n_freq = heads_dim // 4
    inv = (np.float32(ROPE_THETA) ** (-np.arange(n_freq, dtype=np.float32) / np.float32(n_freq))).astype(np.float32)
    pos = np.stack([t // GRID_W, t % GRID_W], -1).astype(np.float32)
    ang = (pos[..., None] * inv).astype(np.float32)
    cos, sin = np.cos(ang).astype(np.float32), np.sin(ang).astype(np.float32)
    both = np.stack([cos, cos], 2).reshape(seq, heads_dim)
    turn = np.stack([-sin, sin], 2).reshape(seq, heads_dim)
    scale = np.float32(heads_dim ** -0.5)
    rope = np.stack([both, turn, both * scale, turn * scale], 1).astype(np.float32)
    return table, np.ascontiguousarray(rope.reshape(seq // P, P, 4, heads_dim))


def mixer_and_experts(nc, t):
    x_d, ctx_d, out_d = t["x"], t["ctx"], t["out"]
    _, SEQ, D = x_d.shape
    CTX = ctx_d.shape[1]
    HEADS = t["ret_decay_f"].shape[1]
    D_IN = t["w_in"].shape[2]
    NE = t["w_gate"].shape[1]
    FE = t["w_gate"].shape[3]
    DK = 128
    DV = t["ret_gn_w"].shape[1] // HEADS
    QW, VW = HEADS * DK, HEADS * DV
    GROUPS = t["sgu_w"].shape[1]
    T, C, K = SEQ // P, CTX // P, D // P
    CAP = CAPACITY_FACTOR * SEQ // NE
    PAIRS = NE // 2
    assert (T, C, K, CAP, QW, VW, FE) == (4, 2, 8, 64, 512, 1024, 1024)
    OFF_Q, OFF_K, OFF_V = 0, QW, 2 * QW
    OFF_G = OFF_V + VW
    OFF_U, OFF_VS, OFF_GA, OFF_GB = OFF_G + VW, OFF_G + VW + D, OFF_G + VW + 2 * D, OFF_G + VW + 3 * D
    assert OFF_GB + D == D_IN

    w_in, w_pa, w_pb, w_o = (t[n][0] for n in ("w_in", "w_pa", "w_pb", "w_o"))
    GROUP_LIST = [("k", w_in, OFF_K), ("q", w_in, OFF_Q), ("v0", w_in, OFF_V), ("v1", w_in, OFF_V + 512),
                  ("g0", w_in, OFF_G), ("g1", w_in, OFF_G + 512),
                  ("pa0", w_pa, 0), ("ga0", w_in, OFF_GA), ("pa1", w_pa, 512), ("ga1", w_in, OFF_GA + 512),
                  ("vs0", w_in, OFF_VS), ("vs1", w_in, OFF_VS + 512), ("u0", w_in, OFF_U), ("u1", w_in, OFF_U + 512),
                  ("pb0", w_pb, 0), ("gb0", w_in, OFF_GB), ("pb1", w_pb, 512), ("gb1", w_in, OFF_GB + 512),
                  ("wo0", w_o, 0), ("wo1", w_o, 512)]
    ORDER = [g[0] for g in GROUP_LIST]
    number_of = {name: i for i, name in enumerate(ORDER)}
    WITH_CTX = {"k", "v0", "v1"}
    WIDE = {"g0", "g1", "pa0", "ga0", "pa1", "ga1", "u0", "u1", "pb0", "gb0", "pb1", "gb1"}
    ROW_CHUNKS_AFTER = {"pa0": 4, "ga0": 4, "pa1": 4, "ga1": 4}

    J = Jobs()
    J.add("cols", "act", banks=7)
    for i in range(T + C):
        for h in range(2):
            J.add(("xT", i, h), "act", banks=7)
    J.add("modrow", "act", bank=7)
    J.add("mod", "dve", bank=6)
    J.turn = 0

    def group_jobs(g):
        who = "act" if g.rstrip("01") in ("g", "pa", "ga", "pb", "gb", "u") else "dve"
        for j in range(4):
            J.add((g, j), who)
        if g in WITH_CTX:
            for j in range(C):
                J.add((g, T + j), who)

    def state_jobs(h):
        J.add(("kv0", h), "act")
        for j in range(T - 1):
            J.add(("kv", h, j), "dve")
        J.add(("sc", h), "dve")

    for g in ("k", "q", "v0", "v1"):
        group_jobs(g)
    J.add(("qT", 0), "act")
    J.add(("kT", 0), "act")
    state_jobs(0)
    for h in range(HEADS):
        if h + 1 < HEADS:
            J.add(("qT", h + 1), "act")
            J.add(("kT", h + 1), "act")
        J.add(("o", h, 0), "act")
        J.add(("o", h, 1), "act")
        if h + 1 < HEADS:
            state_jobs(h + 1)
    for half in range(2):
        group_jobs(f"g{half}")
        for c in range(4 * half, 4 * half + 4):
            J.add(("oT", c), "dve")
    for g in ("pa0", "ga0", "pa1", "ga1"):
        group_jobs(g)
    J.add("swT", "act")
    group_jobs("vs0")
    group_jobs("vs1")
    for half in range(2):
        group_jobs(f"u{half}")
        for c in range(4 * half, 4 * half + 4):
            J.add(("sp", c), "dve")
    for i in range(8):
        J.add(("row", i), "act")
    for g in ("pb0", "gb0", "pb1", "gb1", "wo0", "wo1"):
        group_jobs(g)
    for i in range(T):
        for h in range(2):
            J.add(("h2T", i, h), "act")
        J.add(("lg", i), "dve")
    J.add("affT", "act")
    J.add("posT", "dve")

    RAW = 3
    raw_uses = [("ada", k) for k in range(K)]
    rows_left = [("row", n) for n in range(2 * K)]
    raw_uses += [(ORDER[0], 0), (ORDER[0], 1)]
    for gi, g in enumerate(ORDER):
        if gi + 1 < len(ORDER):
            raw_uses += [(ORDER[gi + 1], 0), (ORDER[gi + 1], 1)]
        for _ in range(ROW_CHUNKS_AFTER.get(g, 0)):
            raw_uses.append(rows_left.pop(0))
    assert not rows_left
    raw_at = {u: n for n, u in enumerate(raw_uses)}

    with ExitStack() as ctx:
        small_at = [SBUF_START]

        def small(name, shape, dt=F32):
            n = int(np.prod(shape[1:])) * 4
            a = nc.alloc_sbuf_tensor_at(name, list(shape), dt, offset=small_at[0])
            small_at[0] += (n + 31) // 32 * 32
            assert small_at[0] <= SBUF_START + AREA
            return a

        def at(kib, name, shape, dt=F32):
            return nc.alloc_sbuf_tensor_at(name, list(shape), dt, offset=place(kib))

        def sem(name):
            return ctx.enter_context(nc.semaphore(name))

        ps = ctx.enter_context(nc.psum_tensor("banks", [P, BANKS, BANK], F32))

        ident_slots = small("ident_slots", [P, P + 64 + 4])
        ident = ident_slots[:, 0:P]
        slot_ramp = ident_slots[:, P:P + 64]
        ramps = ident_slots[:, P + 64:P + 68]
        ones = small("ones", [P, P])
        vec_rows = small("vec_rows", [80, P])
        cols = small("cols", [P, 80])
        c_wide = small("c_wide", [P, K, 32])
        mod = small("mod", [P, 16, 2])
        stats = small("stats", [P, 6, 2, 6])
        moments = small("moments", [P, 6, 2])
        rstd = small("rstd", [P, 6])
        o_stats = small("o_stats", [P, T * HEADS, 6])
        o_moments = small("o_moments", [P, T * HEADS, 2])
        o_rstd = small("o_rstd", [P, T * HEADS])
        v_stats = small("v_stats", [P, T, 2, 6])
        v_moments = small("v_moments", [P, T, 2])
        v_rstd = small("v_rstd", [P, T])
        l_stats = small("l_stats", [P, 3 * T, 2, 6])
        l_moments = small("l_moments", [P, 3 * T, 2])
        l_rstd = small("l_rstd", [P, 3 * T])
        l_nmr = small("l_nmr", [P, 3 * T])
        powers = small("powers", [P, 16])
        decay = small("decay", [P, 2 * HEADS])
        decay_w = small("decay_w", [P, 4, 2 * HEADS])
        log_gamma = small("log_gamma", [P, 2 * HEADS])
        zeta_arg = small("zeta_arg", [P, 6, HEADS])
        zeta = small("zeta", [P, 6, HEADS])
        zeta_ctx = small("zeta_ctx", [P, 4, HEADS])
        w_router = small("w_router_s", [P, K, NE])
        b_router = small("b_router_s", [P, NE])
        logits = small("logits", [P, T, NE])
        aff = small("aff", [P, T, NE])
        soft = small("soft", [P, 3, T])
        pos_t = small("pos_t", [P, T, NE])
        top8 = small("top8", [NE, 2, 8])
        gate_col = small("gate_col", [P, 1])

        raw = at(8, "raw", [P, RAW, 2048])
        w_hi = at(32, "w_hi", [P, 2, 2048], F32R)
        w_lo = at(48, "w_lo", [P, 2, 2048], F32R)
        h_hi = at(64, "h_hi", [P, K, SEQ], F32R)
        h_lo = at(80, "h_lo", [P, K, SEQ], F32R)
        x_in = at(96, "x_in", [P, T + C, D])
        xn_t = at(120, "xn_t", [P, K, SEQ + CTX])
        mod_t = at(188, "mod_t", [P, 512])
        hc_hi = at(144, "hc_hi", [P, K, CTX], F32R)
        hc_lo = at(152, "hc_lo", [P, K, CTX], F32R)
        h_tmp = at(182, "h_tmp", [P, 2, SEQ + CTX])
        tables = at(202, "tables", [P, 6 * P])
        k_s = at(96, "k_s", [P, T, QW])
        q_s = at(104, "q_s", [P, T, QW])
        v_s = at(112, "v_s", [P, T, VW])
        kc_s = at(128, "kc_s", [P, C, QW])
        vc_s = at(132, "vc_s", [P, C, VW])
        b_row = at(160, "b_row", [P, 2 * QW + VW])
        rope = at(168, "rope", [P, T, 4, DK])
        rope_tmp = at(176, "rope_tmp", [P, 2, QW])
        mask = at(180, "mask", [P, HEADS, P])
        q_t = at(152, "q_t", [P, 2, SEQ])
        k_t = at(156, "k_t", [P, 2, SEQ])
        q_f = at(160, "q_f", [P, 2, SEQ])
        q_b = at(164, "q_b", [P, 2, SEQ])
        kz = at(168, "kz", [P, 2, 2, T - 1, DK])
        kcz = at(140, "kcz", [P, 2, 2, C, DK])
        sm = at(176, "sm", [P, 2, SEQ])
        state = at(144, "state", [P, 2, T, DV])
        xi = at(182, "xi_rows", [P, 2, HEADS, P])
        o_s = at(186, "o_s", [P, T, VW])
        g_t = at(96, "g_t", [P, K, SEQ])
        r_hi = at(112, "r_hi", [P, K, SEQ], F32R)
        r_lo = at(128, "r_lo", [P, K, SEQ], F32R)
        prod = at(144, "prod", [P, 2, SEQ])
        ya = at(96, "ya", [P, K, SEQ])
        gate_s = at(148, "gate_s", [P, 2, SEQ])
        mod_rows = at(152, "mod_rows", [P, 4 * D])
        vs_s = at(168, "vs_s", [P, T, D])
        vs_rows = at(184, "vs_rows", [P, 3, D])
        u_t = at(196, "u_t", [P, 4, SEQ])
        sw_in = at(204, "sw_in", [P, GROUPS, P])
        sw_t = at(206, "sw_t", [P, GROUPS, P])
        sgu_b = at(184, "sgu_b_s", [P, GROUPS, P])
        s_hi = at(112, "s_hi", [P, K, SEQ], F32R)
        s_lo = at(128, "s_lo", [P, K, SEQ], F32R)
        pb_s = at(200, "pb_s", [P, 4, SEQ])
        y_hi = at(168, "y_hi", [P, K, SEQ], F32R)
        y_lo = at(184, "y_lo", [P, K, SEQ], F32R)
        xa = at(96, "xa", [P, T, D])
        b_o = at(112, "b_o_s", [P, D])
        ln_rows = at(200, "ln_rows", [P, 2, D])
        ln_tmp = at(144, "ln_tmp", [P, 2, D])
        h2 = at(112, "h2", [P, T, D])
        h2_hi = at(8, "h2_hi", [P, T, D], F32R)
        h2_lo = at(32, "h2_lo", [P, T, D], F32R)
        h2_t = at(24, "h2_t", [P, 2, K, P])
        aff_t = at(24, "aff_t", [NE, SEQ])
        work = at(26, "work", [NE, SEQ])
        picked = at(28, "picked", [NE, SEQ])
        rank = at(30, "rank", [NE, SEQ])
        RING = 6
        ring_at = (64, 80, 128, 168, 184, 48)
        ring = [at(kib, f"ring{n}", [P, 2, 2, FE]) for n, kib in enumerate(ring_at)]
        x_rows = at(152, "x_rows", [P, D])
        xs = at(112, "xs", [P, K, P])
        hid = at(116, "hid", [P, FE])
        hid_t = at(120, "hid_t", [P, K, P])
        ye = at(124, "ye", [P, D])
        sel = at(24, "sel", [P, T, P], F32R)
        sel_t = at(26, "sel_t", [P, SEQ], F32R)
        ye_hi = at(28, "ye_hi", [P, D], F32R)
        ye_lo = at(144, "ye_lo", [P, D], F32R)
        silu_s = at(148, "silu_s", [P, FE])


        raw_landed = [sem(f"raw_landed{i}") for i in range(RAW)]
        ring_landed = [sem(f"ring_landed{i}") for i in range(RING)]
        vec_landed = sem("vec_landed")
        x_landed = [sem(f"x_landed{i}") for i in range(T + C)]
        ident_landed = sem("ident_landed")
        tables_landed = sem("tables_landed")
        decay_landed = sem("decay_landed")
        b_row_landed = sem("b_row_landed")
        rope_landed = sem("rope_landed")
        router_landed = sem("router_landed")
        vs_rows_landed = sem("vs_rows_landed")
        sw_landed = sem("sw_landed")
        sgu_b_landed = sem("sgu_b_landed")
        rows_zeroed = sem("rows_zeroed")
        rows_started = sem("rows_started")
        xa_landed = sem("xa_landed")
        b_o_landed = sem("b_o_landed")
        ln1_landed = sem("ln1_landed")
        ln2_landed = sem("ln2_landed")
        stored = sem("stored")
        bank_full = sem("bank_full")
        act_drained = sem("act_drained")
        dve_drained = sem("dve_drained")
        set_up = sem("set_up")
        silu_c = sem("silu_c")
        var_ready = sem("var_ready")
        rstd_ready = sem("rstd_ready")
        eps_added = sem("eps_added")
        x_normed = sem("x_normed")
        ada_used = sem("ada_used")
        c_spread = sem("c_spread")
        h_made = sem("h_made")
        h_split = sem("h_split")
        hi_made = sem("hi_made")
        lo_made = sem("lo_made")
        half_used = sem("half_used")
        exp_in = sem("exp_in")
        exp_out = sem("exp_out")
        masks_made = sem("masks_made")
        roped = sem("roped")
        kz_made = sem("kz_made")
        q_made = sem("q_made")
        o_normed = sem("o_normed")
        ret_made = sem("ret_made")
        gated = sem("gated")
        gelu_done = sem("gelu_done")
        vs_scaled = sem("vs_scaled")
        vs_made = sem("vs_made")
        sgu_made = sem("sgu_made")
        y_made = sem("y_made")
        rows_summed = sem("rows_summed")
        w_applied = sem("w_applied")
        b_applied = sem("b_applied")
        sc_applied = sem("sc_applied")
        h2_made = sem("h2_made")
        nmr_made = sem("nmr_made")
        normed = sem("normed")
        h2_copied = sem("h2_copied")
        acc_scaled = sem("acc_scaled")
        h2_split = sem("h2_split")
        out_ready = sem("out_ready")
        dve_step = sem("dve_step")
        act_step = sem("act_step")
        chunk_used = sem("chunk_used")
        pair_full = sem("pair_full")
        pair_act = sem("pair_act")
        pair_dve = sem("pair_dve")

        LATE = [0] + [n for i in range(1, T) for n in (2 * i, 2 * i - 1)] + [2 * T - 1] + [2 * T + i for i in range(T)]
        SCATTER_BANK = (0, 1, 2, 3, 4, 5, 0, 1)
        drained_by = {"act": act_drained, "dve": dve_drained}

        def wait_full(eng, job):
            eng.wait_ge(bank_full, J.full(job))

        def wait_drained(eng, job):
            eng.wait_ge(drained_by[J.drainer[job]], J.drained(job))

        def bank(job):
            return ps[:, J.bank[job], :]

        def last_job(g):
            return (g, T + C - 1) if g in WITH_CTX else (g, 3)

        def wait_raw(eng, use):
            n = raw_at[use]
            eng.wait_ge(raw_landed[n % RAW], 16 * (n // RAW + 1))

        def raw_slot(use):
            return raw[:, raw_at[use] % RAW, :]

        def wait_weights_free(eng, gi, half):
            if gi == 0:
                return
            if half == 0:
                eng.wait_ge(half_used, gi)
            else:
                wait_full(eng, last_job(ORDER[gi - 1]))

        vec = nc.vector
        act_e = nc.scalar
        pool_e = nc.gpsimd
        block = ctx.enter_context(nc.Block())

        expert_w = [t[n].rearrange("l e (c k p) f -> (l e) c p k f", k=2, p=P) for n in ("w_gate", "w_up", "w_down")]

        @block.sync
        def _(sp):
            w_ada = t["w_ada"][0]
            for n, use in enumerate(raw_uses):
                kind, part = use
                if n >= RAW:
                    was, was_part = raw_uses[n - RAW]
                    if was == "ada":
                        sp.wait_ge(ada_used, was_part + 1)
                    elif was == "row":
                        sp.wait_ge(rows_summed, was_part + 1)
                    else:
                        sp.wait_ge(lo_made, 2 * number_of[was] + was_part + 1)
                slot = raw_slot(use)
                if kind == "ada":
                    sp.dma_start(slot, w_ada[part * P:(part + 1) * P, 0:2 * D]).then_inc(raw_landed[n % RAW], 16)
                elif kind == "row":
                    k, side = part % K, part // K
                    sp.dma_start(slot, w_ada[k * P:(k + 1) * P, 2 * D * (1 + side):2 * D * (2 + side)])\
                        .then_inc(raw_landed[n % RAW], 16)
                else:
                    _, w, first = GROUP_LIST[number_of[kind]]
                    rows = w[part * 4 * P:(part + 1) * 4 * P, first:first + 512].rearrange("(k p) n -> p k n", p=P)
                    sp.dma_start(slot.rearrange("p (k n) -> p k n", k=4), rows).then_inc(raw_landed[n % RAW], 16)

            def load_chunk(i, c):
                for e in range(2):
                    sp.dma_start(ring[c % RING][:, e, :, :], expert_w[c // 4][2 * i + e, c % 4])\
                        .then_inc(ring_landed[c % RING], 16)

            for c in range(12):
                if c == 0:
                    wait_full(sp, ("gb1", 3))
                if c == 3:
                    wait_full(sp, ("wo1", 3))
                if c >= RING:
                    sp.wait_ge(chunk_used, c - RING + 1)
                load_chunk(0, c)
            with sp.Fori(1, PAIRS) as i:
                for c in range(12):
                    sp.wait_ge(chunk_used, 12 * i + (c - RING + 1))
                    load_chunk(i, c)
            out_v = out_d.rearrange("b (t p) d -> (b t) p d", p=P)
            for i in range(T):
                sp.wait_ge(out_ready, i + 1)
                sp.dma_start(out_v[i], xa[:, i, :]).then_inc(stored, 16)
            sp.wait_ge(stored, 16 * T)

        @block.gpsimd
        def _(pool):
            pool_e.memset(ones[:, :], 1.0).then_inc(set_up, 1)
            pool_e.memset(powers[:, :], -0.5).then_inc(set_up, 1)
            pool.wait_ge(set_up, 2)
            turn = [0]

            def rsqrt(out, var, n):
                turn[0] += 1
                pool.wait_ge(var_ready, turn[0])
                pool_e.tensor_scalar(out, var, LN_EPS, None, ALU.add).then_inc(eps_added, 1)
                pool.wait_ge(eps_added, turn[0])
                pool_e.tensor_tensor(out, out, powers[:, 0:n], ALU.pow).then_inc(rstd_ready, 1)

            for i in range(T + C):
                rsqrt(rstd[:, i:i + 1], moments[:, i, 1:2], 1)
            rsqrt(o_rstd[:, :], o_moments[:, :, 1], T * HEADS)
            wait_full(pool, ("oT", 3))
            pool_e.memset(mod_rows[:, :], 0.0).then_inc(rows_zeroed, 1)
            pool.wait_ge(rows_zeroed, 1)
            pool.dma_start(mod_rows[0:1, :], t["b_ada"][:, 2 * D:6 * D]).then_inc(rows_started, 16)
            wait_full(pool, ("oT", 7))
            for j, row in enumerate((t["b_in"][0, OFF_VS:OFF_VS + D], t["sgu_ln_w"][0], t["sgu_ln_b"][0])):
                pool.dma_start(vs_rows[:, j, :], row.partition_broadcast(P)).then_inc(vs_rows_landed, 16)
            pool.dma_start(sw_in[:, :, :], t["sgu_w"][0].rearrange("g p q -> p g q")).then_inc(sw_landed, 16)
            pool.wait_ge(vs_rows_landed, 48)
            for i in range(T + 1):
                if i < T:
                    rsqrt(v_rstd[:, i:i + 1], v_moments[:, i, 1:2], 1)
                if i >= 1:
                    pool.wait_ge(vs_scaled, i)
                    pool_e.tensor_tensor(vs_s[:, i - 1, :], vs_s[:, i - 1, :], vs_rows[:, 2, :], ALU.add)\
                        .then_inc(vs_made, 1)
            pool.wait_ge(vs_made, T)
            pool.dma_start(sgu_b[:, :, :].rearrange("p g q -> p (g q)"),
                           t["sgu_b"][0].rearrange("g q -> (g q)").partition_broadcast(P)).then_inc(sgu_b_landed, 16)
            pool.wait_ge(y_made, K)
            pool.dma_start(xa[:, :, :], x_d[0].rearrange("(t p) d -> p t d", p=P)).then_inc(xa_landed, 16)
            pool.dma_start(b_o[:, :], t["b_o"][0].partition_broadcast(P)).then_inc(b_o_landed, 16)
            for j, row in enumerate((t["ln1_w"][0], t["ln1_b"][0])):
                pool.dma_start(ln_rows[:, j, :], row.partition_broadcast(P)).then_inc(ln1_landed, 16)

            def ln1_rsqrt(i):
                rsqrt(l_rstd[:, 2 * i:2 * i + 1], l_moments[:, 2 * i, 1:2], 1)

            def h2_rsqrt(i):
                rsqrt(l_rstd[:, 2 * i + 1:2 * i + 2], l_moments[:, 2 * i + 1, 1:2], 1)

            def ln1_bias(i):
                pool.wait_ge(w_applied, i + 1)
                pool_e.tensor_tensor(xa[:, i, :], xa[:, i, :], ln_rows[:, 1, :], ALU.add).then_inc(b_applied, 1)

            def h2_shift(i):
                pool.wait_ge(sc_applied, i + 1)
                pool_e.tensor_tensor(h2[:, i, :], h2[:, i, :], mod_rows[:, D:2 * D], ALU.add).then_inc(h2_made, 1)

            pool.wait_ge(ln1_landed, 32)
            for i in range(T + 1):
                if i < T:
                    ln1_rsqrt(i)
                if i >= 1:
                    h2_rsqrt(i - 1)
                if i < T:
                    ln1_bias(i)
                if i >= 1:
                    h2_shift(i - 1)
            for j, row in enumerate((t["ln2_w"][0], t["ln2_b"][0])):
                pool.dma_start(ln_rows[:, j, :], row.partition_broadcast(P)).then_inc(ln2_landed, 16)
            wait_full(pool, ("wo1", 3))
            for i in range(T):
                pool.wait_ge(h2_copied, i + 1)
                pool_e.tensor_tensor(h2_lo[:, i, :], h2[:, i, :], h2_hi[:, i, :], ALU.subtract).then_inc(h2_split, 1)
            for i in range(T + 1):
                if i < T:
                    rsqrt(l_rstd[:, 2 * T + i:2 * T + i + 1], l_moments[:, 2 * T + i, 1:2], 1)
                if i >= 1:
                    pool.wait_ge(w_applied, T + i)
                    pool_e.tensor_tensor(xa[:, i - 1, :], xa[:, i - 1, :], ln_rows[:, 1, :], ALU.add)\
                        .then_inc(out_ready, 1)

        @block.scalar
        def _(act):
            pieces = ((0, t["c"][0]), (8, t["c_ctx"]), (16, t["b_ada"][0, 0:2 * D]), (32, t["b_in"][0, OFF_G:OFF_G + 2 * D]),
                      (48, t["b_in"][0, OFF_GA:OFF_GA + 2 * D]), (64, t["ret_gn_w"][0]), (72, t["ret_gn_b"][0]))
            for first, v in pieces:
                n = v.shape[0] // P
                act.dma_start(vec_rows[first:first + n, :], v.rearrange("(r n) -> r n", n=P)).then_inc(vec_landed, 16)
            act.dma_start(x_in[:, 0, :], x_d[0, 0:P, :]).then_inc(x_landed[0], 16)
            act.dma_start(ident_slots[:, :], t["shape_table"][:, 0:P + 68]).then_inc(ident_landed, 16)
            for i in range(1, T + C):
                src = x_d[0, i * P:(i + 1) * P, :] if i < T else ctx_d[0, (i - T) * P:(i - T + 1) * P, :]
                act.dma_start(x_in[:, i, :], src).then_inc(x_landed[i], 16)
            act.dma_start(tables[:, :], t["shape_table"][:, P + 68:]).then_inc(tables_landed, 16)
            act.dma_start(decay[:, 0:HEADS], t["ret_decay_f"][0].partition_broadcast(P)).then_inc(decay_landed, 16)
            act.dma_start(decay[:, HEADS:], t["ret_decay_b"][0].partition_broadcast(P)).then_inc(decay_landed, 16)
            act.dma_start(b_row[:, :], t["b_in"][0, 0:OFF_G].partition_broadcast(P)).then_inc(b_row_landed, 16)
            act.dma_start(rope[:, :, :, :].rearrange("p t a d -> p t (a d)"),
                          t["rope"].rearrange("t p a d -> p t (a d)")).then_inc(rope_landed, 16)
            act.dma_start(w_router[:, :, :], t["w_router"][0].rearrange("(k p) e -> p k e", p=P)).then_inc(router_landed, 16)
            act.dma_start(b_router[:, :], t["b_router"][0].partition_broadcast(P)).then_inc(router_landed, 16)

            act.wait_ge(vec_landed, 16 * len(pieces))
            act_e.activation(vec_rows[0:16, :], vec_rows[0:16, :], ACT.Silu).then_inc(silu_c, 1)
            wait_full(act, "cols")
            act_e.activation(cols[:, :], bank("cols")[:, 0:80], ACT.Copy).then_inc(act_drained, 1)
            for i in range(T + C):
                for h in range(2):
                    wait_full(act, ("xT", i, h))
                    act_e.activation(xn_t[:, 4 * h:4 * h + 4, i * P:(i + 1) * P],
                                     bank(("xT", i, h)).rearrange("p (k n) -> p k n", k=4), ACT.Copy)\
                        .then_inc(act_drained, 1)

            def high_part(gi, half):
                use = (ORDER[gi], half)
                wait_raw(act, use)
                wait_weights_free(act, gi, half)
                act_e.activation(w_hi[:, half, :], raw_slot(use), ACT.Copy).then_inc(hi_made, 1)

            wait_full(act, "modrow")
            act_e.activation(mod_t[:, :], bank("modrow"), ACT.Copy).then_inc(act_drained, 1)
            wait_drained(act, "mod")
            wait_drained(act, ("xT", T + C - 1, 1))
            for k in range(K):
                if k >= 2:
                    act.wait_ge(h_split, k - 1)
                for j, (lo, hi) in enumerate(((0, SEQ), (SEQ, SEQ + CTX))):
                    act_e.activation(h_tmp[:, k % 2, lo:hi], xn_t[:, k, lo:hi], ACT.Identity,
                                     scale=mod[:, 8 + k, j:j + 1], bias=mod[:, k, j:j + 1]).then_inc(h_made, 1)
                if k == 2:
                    high_part(0, 0)
            high_part(0, 1)

            def exps():
                act.wait_ge(exp_in, 1)
                act_e.activation(decay_w[:, 1, :], decay_w[:, 0, :], ACT.Exp).then_inc(exp_out, 1)
                act.wait_ge(exp_in, 2)
                act_e.activation(zeta[:, :, :], zeta_arg[:, :, :], ACT.Exp).then_inc(exp_out, 1)
                act.wait_ge(tables_landed, 16)
                for s in range(2):
                    for h in range(HEADS):
                        act_e.activation(xi[:, s, h, :], tables[:, (4 + s) * P:(5 + s) * P], ACT.Exp,
                                         scale=log_gamma[:, s * HEADS + h:s * HEADS + h + 1]).then_inc(exp_out, 1)
                for h in range(HEADS):
                    act_e.activation(mask[:, h, :], tables[:, 0:P], ACT.Exp,
                                     scale=log_gamma[:, h:h + 1]).then_inc(exp_out, 1)
                    act_e.activation(o_s[:, 0, h * P:(h + 1) * P], tables[:, P:2 * P], ACT.Exp,
                                     scale=log_gamma[:, HEADS + h:HEADS + h + 1]).then_inc(exp_out, 1)

            def retention():
                def transposed(h):
                    for name, dst in (("qT", q_t), ("kT", k_t)):
                        wait_full(act, (name, h))
                        act_e.activation(dst[:, h % 2, :], bank((name, h)), ACT.Copy).then_inc(act_drained, 1)

                def first_state(h):
                    wait_full(act, ("kv0", h))
                    act_e.activation(state[:, :, 0, :], bank(("kv0", h)).rearrange("p (s v) -> p s v", s=2),
                                     ACT.Copy).then_inc(act_drained, 1)

                transposed(0)
                first_state(0)
                high_part(number_of["g0"], 1)
                for h in range(HEADS):
                    if h + 1 < HEADS:
                        transposed(h + 1)
                    if h == 0:
                        act.wait_ge(masks_made, 1)
                    for j in range(2):
                        wait_full(act, ("o", h, j))
                        act_e.activation(o_s[:, 2 * j:2 * j + 2, h * DV:(h + 1) * DV],
                                         bank(("o", h, j)).rearrange("p (n v) -> p n v", n=2),
                                         ACT.Copy).then_inc(act_drained, 1)
                    if h + 1 < HEADS:
                        first_state(h + 1)

            gates_seen = [0]

            def drain(g):
                half = int(g[-1])
                for j in range(4):
                    c = 4 * half + j
                    wait_full(act, (g, j))
                    if g in ("g0", "g1"):
                        act_e.activation(g_t[:, c, :], bank((g, j)), ACT.Silu,
                                         bias=cols[:, 32 + c:33 + c]).then_inc(act_drained, 1)
                    elif g in ("pa0", "pa1"):
                        act_e.activation(ya[:, c, :], bank((g, j)), ACT.Copy).then_inc(act_drained, 1)
                    elif g in ("pb0", "pb1"):
                        if half:
                            act.wait_ge(y_made, j + 1)
                        else:
                            act.wait_ge(sgu_made, K)
                        act_e.activation(pb_s[:, j, :], bank((g, j)), ACT.Copy).then_inc(act_drained, 1)
                    elif g in ("u0", "u1"):
                        if half:
                            act.wait_ge(sgu_made, c - 3)
                        act_e.activation(u_t[:, j, :], bank((g, j)), ACT.Gelu_apprx_tanh,
                                         bias=cols[:, 40 + c:41 + c]).then_inc(act_drained, 1)
                    else:
                        n = gates_seen[0]
                        gates_seen[0] += 1
                        if n >= 2:
                            act.wait_ge(gated, n - 1)
                        first = 48 if g.startswith("ga") else 56
                        act_e.activation(gate_s[:, n % 2, :], bank((g, j)), ACT.Sigmoid,
                                         bias=cols[:, first + c:first + c + 1]).then_inc(act_drained, 1)

            def gelu_vs(half):
                for i in range(T):
                    wait_drained(act, (f"vs{half}", i))
                    v = vs_s[:, i, half * 512:(half + 1) * 512]
                    act_e.activation(v, v, ACT.Gelu_apprx_tanh).then_inc(gelu_done, 1)

            for gi, g in enumerate(ORDER):
                if gi + 1 < len(ORDER):
                    high_part(gi + 1, 0)
                if J.drainer[(g, 0)] == "act":
                    drain(g)
                if gi + 1 < len(ORDER) and g != "v1":
                    high_part(gi + 1, 1)
                if g == "k":
                    exps()
                if g == "v1":
                    retention()
                if g == "ga1":
                    wait_full(act, "swT")
                    act_e.activation(sw_t[:, :, :], bank("swT").rearrange("p (g q) -> p g q", g=GROUPS),
                                     ACT.Copy).then_inc(act_drained, 1)
                if g in ("vs0", "vs1"):
                    gelu_vs(int(g[-1]))
                if g == "u1":
                    for i in range(8):
                        wait_full(act, ("row", i))
                        act_e.activation(mod_rows[:, i * 512:(i + 1) * 512], bank(("row", i)), ACT.Copy,
                                         bias=1.0 if i in (4, 5) else 0.0).then_inc(act_drained, 1)

            def normalise(n, dst, src):
                act.wait_ge(nmr_made, LATE.index(n) + 1)
                act_e.activation(dst, src, ACT.Identity, scale=l_rstd[:, n:n + 1], bias=l_nmr[:, n:n + 1])\
                    .then_inc(normed, 1)

            def router_operand(i):
                for h in range(2):
                    wait_full(act, ("h2T", i, h))
                    act_e.activation(h2_t[:, i % 2, 4 * h:4 * h + 4, :],
                                     bank(("h2T", i, h)).rearrange("p (k n) -> p k n", k=4), ACT.Copy)\
                        .then_inc(act_drained, 1)
                act_e.activation(h2_hi[:, i, :], h2[:, i, :], ACT.Copy).then_inc(h2_copied, 1)
                act_e.activation(xa[:, i, :], xa[:, i, :], ACT.Copy, scale=ALPHA).then_inc(acc_scaled, 1)

            for i in range(T + 2):
                if i < T:
                    normalise(2 * i, xa[:, i, :], xa[:, i, :])
                if 1 <= i <= T:
                    normalise(2 * i - 1, h2[:, i - 1, :], xa[:, i - 1, :])
                if i >= 2:
                    router_operand(i - 2)
            act.wait_ge(exp_in, 3)
            act_e.activation(logits[:, :, :], logits[:, :, :], ACT.Exp).then_inc(exp_out, 1)
            wait_full(act, "affT")
            act_e.activation(aff_t[:, :], bank("affT")[0:NE, :], ACT.Copy).then_inc(act_drained, 1)

            with act.Fori(0, PAIRS) as i:
                for h in range(2):
                    act.wait_ge(pair_full, 16 * i + (1 + h))
                    act_e.activation(x_rows[:, h * 512:(h + 1) * 512], ps[:, 4 + h, :], ACT.Copy)\
                        .then_inc(pair_act, 1)
                for h in range(2):
                    act.wait_ge(pair_full, 16 * i + (3 + h))
                    act_e.activation(xs[:, 4 * h:4 * h + 4, :], ps[:, 2 + h, :].rearrange("p (k n) -> p k n", k=4),
                                     ACT.Copy).then_inc(pair_act, 1)
                act.wait_ge(pair_full, 16 * i + 5)
                act_e.activation(sel_t[:, :], ps[:, 6, :], ACT.Copy).then_inc(pair_act, 1)
                act.wait_ge(chunk_used, 12 * i + 4)
                for h in range(2):
                    act_e.activation(silu_s[:, h * 512:(h + 1) * 512], ps[:, h, :], ACT.Silu).then_inc(pair_act, 1)
                for h in range(2):
                    act.wait_ge(pair_full, 16 * i + (7 + h))
                    act_e.activation(hid_t[:, 4 * h:4 * h + 4, :], ps[:, 4 + h, :].rearrange("p (k n) -> p k n", k=4),
                                     ACT.Copy).then_inc(pair_act, 1)
            for i in range(T):
                normalise(2 * T + i, xa[:, i, :], xa[:, i, :])

        @block.vector
        def _(dve):
            steps = [0]

            def step(ins):
                steps[0] += 1
                ins.then_inc(dve_step, 1)
                dve.wait_ge(dve_step, steps[0])

            def moments_of(src, st, mo):
                n = src.shape[1] // 512 or 1
                for j in range(n):
                    ins = vec.bn_stats(st[:, j, :] if n > 1 else st, src[:, j * 512:(j + 1) * 512])
                step(ins)
                vec.bn_aggr(mo, st.rearrange("p a b -> p (a b)") if n > 1 else st).then_inc(var_ready, 1)

            groups_of_var = [0]

            def normalise(dst, src, mo, rs):
                groups_of_var[0] += 1
                dve.wait_ge(rstd_ready, groups_of_var[0])
                return vec.tensor_scalar(dst, src, mo[:, 0:1], rs, ALU.subtract, ALU.mult)

            wait_drained(dve, "cols")
            vec.tensor_copy(c_wide[:, :, :].rearrange("p k (x n) -> p k x n", x=2),
                            cols[:, 0:16].rearrange("p (x k) -> p k x", x=2).unsqueeze(3)
                            .broadcast_to([P, K, 2, 16])).then_inc(c_spread, 1)
            for i in range(T + C + 1):
                if i < T + C:
                    dve.wait_ge(x_landed[i], 16)
                    moments_of(x_in[:, i, :], stats[:, i, :, :], moments[:, i, :])
                if i >= 1:
                    normalise(x_in[:, i - 1, :], x_in[:, i - 1, :], moments[:, i - 1, :],
                              rstd[:, i - 1:i]).then_inc(x_normed, 1)

            dve.wait_ge(decay_landed, 32)
            step(vec.tensor_scalar(decay_w[:, 2, :], decay[:, :], -1.0, None, ALU.mult))
            vec.tensor_tensor(decay_w[:, 0, :], decay[:, :], decay_w[:, 2, :], ALU.min).then_inc(exp_in, 1)

            def log_gammas():
                dve.wait_ge(exp_out, 1)
                y, s, s2, q = (decay_w[:, j, :] for j in (1, 2, 3, 0))
                step(vec.tensor_scalar(s, y, 2.0, None, ALU.add))
                step(vec.reciprocal(s2, s))
                step(vec.tensor_tensor(s, y, s2, ALU.mult))
                step(vec.tensor_tensor(s2, s, s, ALU.mult))
                step(vec.tensor_scalar(q, s2, 1.0 / 17.0, None, ALU.mult))
                for n in (15, 13, 11, 9, 7, 5, 3):
                    step(vec.scalar_tensor_tensor(q, q, 1.0 / n, s2, ALU.add, ALU.mult))
                step(vec.scalar_tensor_tensor(q, q, 1.0, s, ALU.add, ALU.mult))
                step(vec.tensor_scalar(s, decay[:, :], 0.0, None, ALU.min))
                step(vec.scalar_tensor_tensor(log_gamma[:, :], q, -2.0, s, ALU.mult, ALU.add))
                f, b = log_gamma[:, 0:HEADS], log_gamma[:, HEADS:]
                for j, (g, by) in enumerate(((f, ramps[:, 0:1]), (b, ramps[:, 1:2]), (f, ramps[:, 2:3]),
                                             (b, ramps[:, 3:4]), (f, float(P)), (b, float(P)))):
                    ins = vec.tensor_scalar(zeta_arg[:, j, :], g, by, None, ALU.mult)
                ins.then_inc(exp_in, 1)
                dve.wait_ge(exp_out, 2)
                for j, s in enumerate((2, 0, 1, 3)):
                    step(vec.tensor_scalar(zeta_ctx[:, j, :], zeta[:, s, :], float(DK) ** -0.5, None, ALU.mult))

            def masks():
                dve.wait_ge(exp_out, 2 + 4 * HEADS)
                back = o_s[:, 0, 0:HEADS * P].rearrange("p (h n) -> p h n", h=HEADS)
                tri_f = tables[:, 2 * P:3 * P].unsqueeze(1).broadcast_to([P, HEADS, P])
                tri_b = tables[:, 3 * P:4 * P].unsqueeze(1).broadcast_to([P, HEADS, P])
                step(vec.tensor_tensor(mask[:, :, :], mask[:, :, :], tri_f, ALU.mult))
                step(vec.tensor_tensor(back, back, tri_b, ALU.mult))
                vec.tensor_tensor(mask[:, :, :], mask[:, :, :], back, ALU.add).then_inc(masks_made, 1)

            wait_full(dve, "mod")
            step(vec.tensor_tensor(mod[:, :, :].rearrange("p (j b) x -> p b j x", b=4),
                                   bank("mod").rearrange("p (b j x n) -> p b j x n", b=4, j=4, x=2)[:, :, :, :, 0],
                                   cols[:, 16:32].rearrange("p (j b) -> p b j", b=4).unsqueeze(3)
                                   .broadcast_to([P, 4, 4, 2]), ALU.add))
            vec.tensor_scalar(mod[:, 8:16, :], mod[:, 8:16, :], 1.0, None, ALU.add).then_inc(dve_drained, 1)

            def low_part(gi, half):
                use = (ORDER[gi], half)
                wait_raw(dve, use)
                wait_weights_free(dve, gi, half)
                dve.wait_ge(hi_made, 2 * gi + half + 1)
                vec.tensor_tensor(w_lo[:, half, :], raw_slot(use), w_hi[:, half, :], ALU.subtract).then_inc(lo_made, 1)

            def split(hi, lo, src):
                step(vec.tensor_copy(hi, src))
                return vec.tensor_tensor(lo, src, hi, ALU.subtract)

            for k in range(K):
                dve.wait_ge(h_made, 2 * k + 2)
                vec.tensor_copy(h_hi[:, k, :], h_tmp[:, k % 2, 0:SEQ])
                step(vec.tensor_copy(hc_hi[:, k, :], h_tmp[:, k % 2, SEQ:]))
                vec.tensor_tensor(h_lo[:, k, :], h_tmp[:, k % 2, 0:SEQ], h_hi[:, k, :], ALU.subtract)
                vec.tensor_tensor(hc_lo[:, k, :], h_tmp[:, k % 2, SEQ:], hc_hi[:, k, :], ALU.subtract)\
                    .then_inc(h_split, 1)
                if k == 2:
                    low_part(0, 0)
            low_part(0, 1)

            def add_bias(g):
                dve.wait_ge(b_row_landed, 16)
                for j in range(T + (C if g in WITH_CTX else 0)):
                    if g == "k":
                        dst = k_s[:, j, :] if j < T else kc_s[:, j - T, :]
                        row = b_row[:, OFF_K:OFF_K + QW]
                    elif g == "q":
                        dst, row = q_s[:, j, :], b_row[:, OFF_Q:OFF_Q + QW]
                    else:
                        lo = 512 * int(g[1])
                        dst = v_s[:, j, lo:lo + 512] if j < T else vc_s[:, j - T, lo:lo + 512]
                        row = b_row[:, OFF_V + lo:OFF_V + lo + 512]
                    wait_full(dve, (g, j))
                    vec.tensor_tensor(dst, bank((g, j)), row, ALU.add).then_inc(dve_drained, 1)

            def turn(z, which, g):
                dve.wait_ge(rope_landed, 16)
                wait_drained(dve, last_job(g))
                for i in range(T):
                    if i:
                        dve.wait_ge(roped, (0 if g == "k" else T) + i)
                    c = rope[:, i, 2 * which, :].unsqueeze(1).broadcast_to([P, HEADS, DK])
                    s = rope[:, i, 2 * which + 1, :].rearrange("p (a j n) -> p j a n", a=2, j=2)
                    x = z[:, i, :].rearrange("p (h d) -> p h d", h=HEADS)
                    halves = z[:, i, :].rearrange("p (h a j n) -> p j h a n", h=HEADS, a=2, j=2)
                    turned = rope_tmp[:, 1, :].rearrange("p (h a j n) -> p j h a n", h=HEADS, a=2, j=2)
                    for j in range(2):
                        vec.tensor_tensor(turned[:, j], halves[:, 1 - j],
                                          s[:, j].unsqueeze(1).broadcast_to([P, HEADS, 2, DK // 4]), ALU.mult)
                    step(vec.tensor_tensor(rope_tmp[:, 0, :].rearrange("p (h d) -> p h d", h=HEADS), x, c, ALU.mult))
                    vec.tensor_tensor(z[:, i, :], rope_tmp[:, 0, :], rope_tmp[:, 1, :], ALU.add).then_inc(roped, 1)

            def weigh_keys(h):
                cut = slice(h * DK, (h + 1) * DK)
                if h == 0:
                    dve.wait_ge(roped, 2 * T)
                    dve.wait_ge(masks_made, 1)
                vec.tensor_scalar(kz[:, h % 2, 0], k_s[:, 0:T - 1, cut], zeta[:, 0, h:h + 1], None, ALU.mult)
                vec.tensor_scalar(kz[:, h % 2, 1], k_s[:, 1:T, cut], zeta[:, 1, h:h + 1], None, ALU.mult)
                for s in range(2):
                    for i in range(C):
                        ins = vec.tensor_scalar(kcz[:, h % 2, s, i], kc_s[:, i, cut],
                                                zeta_ctx[:, 2 * s + i, h:h + 1], None, ALU.mult)
                ins.then_inc(kz_made, 1)

            def retention():
                def weigh_queries(h):
                    wait_drained(dve, ("qT", h))
                    q = q_t[:, h % 2, :].rearrange("p (n l) -> p n l", n=T)
                    for s, dst in ((0, q_f), (1, q_b)):
                        ins = vec.tensor_tensor(dst[:, h % 2, :].rearrange("p (n l) -> p n l", n=T), q,
                                                xi[:, s, h, :].unsqueeze(1).broadcast_to([P, T, P]), ALU.mult)
                    ins.then_inc(q_made, 1)

                def states(h):
                    wait_drained(dve, ("kv0", h))
                    for j in range(T - 1):
                        if j:
                            wait_drained(dve, ("kv", h, j - 1))
                        wait_full(dve, ("kv", h, j))
                        for s in range(2):
                            ins = vec.scalar_tensor_tensor(
                                state[:, s, j + 1, :], state[:, s, j, :], zeta[:, 4 + s, h:h + 1],
                                bank(("kv", h, j))[:, s * DV:(s + 1) * DV], ALU.mult, ALU.add)
                        ins.then_inc(dve_drained, 1)
                    wait_full(dve, ("sc", h))
                    vec.tensor_tensor(sm[:, h % 2, :].rearrange("p (n l) -> p n l", n=T),
                                      bank(("sc", h)).rearrange("p (n l) -> p n l", n=T),
                                      mask[:, h, :].unsqueeze(1).broadcast_to([P, T, P]), ALU.mult)\
                        .then_inc(dve_drained, 1)

                weigh_queries(0)
                states(0)
                low_part(number_of["g0"], 1)
                for h in range(1, HEADS):
                    weigh_keys(h)
                    weigh_queries(h)
                    states(h)

            def o_moments_made():
                wait_drained(dve, ("o", HEADS - 1, 1))
                for i in range(T):
                    for h in range(HEADS):
                        ins = vec.bn_stats(o_stats[:, i * HEADS + h, :], o_s[:, i, h * DV:(h + 1) * DV])
                step(ins)
                for n in range(T * HEADS):
                    ins = vec.bn_aggr(o_moments[:, n, :], o_stats[:, n, :])
                ins.then_inc(var_ready, 1)

            def o_normalised():
                groups_of_var[0] += 1
                dve.wait_ge(rstd_ready, groups_of_var[0])
                for i in range(T):
                    for h in range(HEADS):
                        n = i * HEADS + h
                        o = o_s[:, i, h * DV:(h + 1) * DV]
                        ins = vec.tensor_scalar(o, o, o_moments[:, n, 0:1], o_rstd[:, n:n + 1],
                                                ALU.subtract, ALU.mult)
                ins.then_inc(o_normed, 1)

            def gated_retention(c):
                if c >= 2:
                    dve.wait_ge(ret_made, c - 1)
                wait_full(dve, ("oT", c))
                vec.tensor_scalar(prod[:, c % 2, :], bank(("oT", c)), cols[:, 64 + c:65 + c], cols[:, 72 + c:73 + c],
                                  ALU.mult, ALU.add).then_inc(dve_drained, 1)
                wait_drained(dve, ("oT", c))
                wait_drained(dve, (f"g{c // 4}", c % 4))
                step(vec.tensor_tensor(prod[:, c % 2, :], prod[:, c % 2, :], g_t[:, c, :], ALU.mult))
                split(r_hi[:, c, :], r_lo[:, c, :], prod[:, c % 2, :]).then_inc(ret_made, 1)

            def row_chunks(first, n):
                for m in range(first, first + n):
                    k, side = m % K, m // K
                    acc = mod_rows[:, 2 * D * side:2 * D * (side + 1)]
                    if m == 0:
                        dve.wait_ge(rows_started, 16)
                    else:
                        dve.wait_ge(rows_summed, m)
                    wait_raw(dve, ("row", m))
                    vec.scalar_tensor_tensor(acc, raw_slot(("row", m)), cols[:, k:k + 1], acc,
                                             ALU.mult, ALU.add).then_inc(rows_summed, 1)

            def gate_retention(half):
                for j in range(4):
                    wait_drained(dve, (f"ga{half}", j))
                    wait_drained(dve, (f"pa{half}", j))
                    c = 4 * half + j
                    vec.tensor_tensor(ya[:, c, :], ya[:, c, :], gate_s[:, c % 2, :], ALU.mult).then_inc(gated, 1)

            def vs_biased(half):
                dve.wait_ge(vs_rows_landed, 48)
                for i in range(T):
                    wait_full(dve, (f"vs{half}", i))
                    vec.tensor_tensor(vs_s[:, i, half * 512:(half + 1) * 512], bank((f"vs{half}", i)),
                                      vs_rows[:, 0, half * 512:(half + 1) * 512], ALU.add).then_inc(dve_drained, 1)

            def vs_normalised():
                for i in range(T + 1):
                    if i < T:
                        dve.wait_ge(gelu_done, T + i + 1)
                        moments_of(vs_s[:, i, :], v_stats[:, i, :, :], v_moments[:, i, :])
                    if i >= 1:
                        v = vs_s[:, i - 1, :]
                        step(normalise(v, v, v_moments[:, i - 1, :], v_rstd[:, i - 1:i]))
                        vec.tensor_tensor(v, v, vs_rows[:, 1, :], ALU.mult).then_inc(vs_scaled, 1)

            def gated_spatial(c):
                if c == 0:
                    dve.wait_ge(sgu_b_landed, 16)
                if c >= 2:
                    dve.wait_ge(sgu_made, c - 1)
                wait_full(dve, ("sp", c))
                vec.tensor_tensor(prod[:, c % 2, :].rearrange("p (n l) -> p n l", n=T),
                                  bank(("sp", c)).rearrange("p (n l) -> p n l", n=T),
                                  sgu_b[:, c // 2, :].unsqueeze(1).broadcast_to([P, T, P]), ALU.add)\
                    .then_inc(dve_drained, 1)
                wait_drained(dve, ("sp", c))
                wait_drained(dve, (f"u{c // 4}", c % 4))
                step(vec.tensor_tensor(prod[:, c % 2, :], prod[:, c % 2, :], u_t[:, c % 4, :], ALU.mult))
                split(s_hi[:, c, :], s_lo[:, c, :], prod[:, c % 2, :]).then_inc(sgu_made, 1)

            def mixed(half):
                for j in range(4):
                    c = 4 * half + j
                    if c >= 2:
                        dve.wait_ge(y_made, c - 1)
                    wait_drained(dve, (f"gb{half}", j))
                    wait_drained(dve, (f"pb{half}", j))
                    step(vec.tensor_tensor(prod[:, c % 2, :], pb_s[:, j, :], gate_s[:, c % 2, :], ALU.mult))
                    step(vec.tensor_tensor(prod[:, c % 2, :], prod[:, c % 2, :], ya[:, c, :], ALU.add))
                    vec.tensor_copy(y_hi[:, c, :], prod[:, c % 2, :]).then_inc(gated, 1)
                    dve.wait_ge(gated, K + c + 1)
                    vec.tensor_tensor(y_lo[:, c, :], prod[:, c % 2, :], y_hi[:, c, :], ALU.subtract).then_inc(y_made, 1)

            def residual():
                dve.wait_ge(b_o_landed, 16)
                wait_drained(dve, ("row", 7))
                step(vec.tensor_tensor(b_o[:, :], b_o[:, :], mod_rows[:, 0:D], ALU.mult))
                dve.wait_ge(xa_landed, 16)
                for i in range(T):
                    ins = vec.scalar_tensor_tensor(xa[:, i, :], xa[:, i, :], ALPHA, b_o[:, :], ALU.mult, ALU.add)
                step(ins)

            def mixed_out(g, i):
                half = int(g[-1])
                cut = slice(half * 512, (half + 1) * 512)
                wait_full(dve, (g, i))
                vec.tensor_tensor(ln_tmp[:, i % 2, cut], bank((g, i)), mod_rows[:, cut], ALU.mult)\
                    .then_inc(dve_drained, 1)
                wait_drained(dve, (g, i))
                step(vec.tensor_tensor(xa[:, i, cut], xa[:, i, cut], ln_tmp[:, i % 2, cut], ALU.add))

            def ln_stats(n, src):
                moments_of(src, l_stats[:, n, :, :], l_moments[:, n, :])

            def ln_bias(n):
                groups_of_var[0] += 1
                dve.wait_ge(rstd_ready, groups_of_var[0])
                vec.scalar_tensor_tensor(l_nmr[:, n:n + 1], l_moments[:, n, 0:1], -1.0, l_rstd[:, n:n + 1],
                                         ALU.mult, ALU.mult).then_inc(nmr_made, 1)

            def ln1_scaled(i):
                dve.wait_ge(ln1_landed, 32)
                dve.wait_ge(normed, LATE.index(2 * i) + 1)
                vec.tensor_tensor(xa[:, i, :], xa[:, i, :], ln_rows[:, 0, :], ALU.mult).then_inc(w_applied, 1)

            def h2_scaled(i):
                dve.wait_ge(normed, LATE.index(2 * i + 1) + 1)
                vec.tensor_tensor(h2[:, i, :], h2[:, i, :], mod_rows[:, 2 * D:3 * D], ALU.mult).then_inc(sc_applied, 1)

            for gi, g in enumerate(ORDER):
                if g == "g0":
                    o_moments_made()
                if gi + 1 < len(ORDER):
                    low_part(gi + 1, 0)
                if g == "g0":
                    o_normalised()
                if g == "v1":
                    weigh_keys(0)
                if g in ("k", "q", "v0", "v1"):
                    add_bias(g)
                if g in ("vs0", "vs1"):
                    vs_biased(int(g[-1]))
                if g in ("ga0", "ga1"):
                    gate_retention(int(g[-1]))
                if g in ("gb0", "gb1"):
                    mixed(int(g[-1]))
                if gi + 1 < len(ORDER) and g != "v1":
                    low_part(gi + 1, 1)
                if g == "k":
                    log_gammas()
                    turn(k_s, 1, "k")
                if g == "q":
                    turn(q_s, 0, "q")
                    masks()
                if g == "v1":
                    retention()
                if g in ("g0", "g1"):
                    for c in range(4 * int(g[1]), 4 * int(g[1]) + 4):
                        gated_retention(c)
                if g in ROW_CHUNKS_AFTER:
                    row_chunks(4 * list(ROW_CHUNKS_AFTER).index(g), 4)
                if g == "vs1":
                    vs_normalised()
                if g in ("u0", "u1"):
                    for c in range(4 * int(g[1]), 4 * int(g[1]) + 4):
                        gated_spatial(c)
                if g == "gb1":
                    residual()
                if g == "wo0":
                    for i in range(T):
                        mixed_out(g, i)
            for i in range(T + 1):
                if i < T:
                    mixed_out("wo1", i)
                    ln_stats(2 * i, xa[:, i, :])
                if i >= 1:
                    dve.wait_ge(b_applied, i)
                    ln_stats(2 * i - 1, xa[:, i - 1, :])
                if i < T:
                    ln_bias(2 * i)
                    ln1_scaled(i)
                if i >= 1:
                    ln_bias(2 * i - 1)
                    h2_scaled(i - 1)

            dve.wait_ge(router_landed, 32)
            for i in range(T):
                wait_full(dve, ("lg", i))
                vec.tensor_tensor(logits[:, i, :], bank(("lg", i))[:, 0:NE], b_router[:, :], ALU.add)\
                    .then_inc(dve_drained, 1)
            wait_drained(dve, ("lg", T - 1))
            step(vec.tensor_reduce(soft[:, 0, :], logits[:, :, :], AX_X, ALU.max))
            vec.tensor_tensor(logits[:, :, :], logits[:, :, :], soft[:, 0, :].unsqueeze(2).broadcast_to([P, T, NE]),
                              ALU.subtract).then_inc(exp_in, 1)
            dve.wait_ge(exp_out, 3 + 4 * HEADS)
            step(vec.tensor_reduce(soft[:, 1, :], logits[:, :, :], AX_X, ALU.add))
            step(vec.reciprocal(soft[:, 2, :], soft[:, 1, :]))
            vec.tensor_tensor(aff[:, :, :], logits[:, :, :], soft[:, 2, :].unsqueeze(2).broadcast_to([P, T, NE]),
                              ALU.mult).then_inc(exp_in, 1)
            wait_drained(dve, "affT")
            for n in range(CAP // 8):
                src = aff_t if n == 0 else work
                step(vec.max(top8[:, n % 2, :], src[:, :]))
                step(vec.match_replace(work[:, :], top8[:, n % 2, :], src[:, :], -1.0))
            step(vec.tensor_scalar(picked[:, :], work[:, :], 0.0, None, ALU.is_lt))
            step(vec.tensor_tensor_scan(rank[:, :], picked[:, :], picked[:, :], 0.0, ALU.add, ALU.max))
            step(vec.tensor_tensor(rank[:, :], rank[:, :], picked[:, :], ALU.mult))
            vec.tensor_scalar(rank[:, :], rank[:, :], -1.0, None, ALU.add).then_inc(exp_in, 1)
            wait_full(dve, "posT")
            vec.tensor_copy(pos_t[:, :, :], bank("posT")[:, 0:T * NE].rearrange("p (t e) -> p t e", t=T))\
                .then_inc(dve_drained, 1)
            wait_drained(dve, "posT")
            dve.wait_ge(acc_scaled, T)

            with dve.Fori(0, PAIRS) as i:
                vec.tensor_tensor(sel[:, :, :].rearrange("p t (j s) -> p t j s", j=2),
                                  slot_ramp.unsqueeze(1).unsqueeze(1).broadcast_to([P, T, 2, CAP]),
                                  pos_t[:, :, bass.ds(2 * i, 2)].unsqueeze(3).broadcast_to([P, T, 2, CAP]),
                                  ALU.is_equal).then_inc(pair_dve, 1)
                dve.wait_ge(pair_full, 16 * i + 6)
                dve.wait_ge(pair_dve, 16 * i + 1)
                vec.tensor_copy(gate_col[0:CAP, :], ps[0:CAP, 7, 0:1])
                vec.tensor_copy(gate_col[CAP:P, :], ps[CAP:P, 7, 1:2]).then_inc(pair_dve, 1)
                dve.wait_ge(chunk_used, 12 * i + 8)
                for h in range(2):
                    dve.wait_ge(pair_act, 9 * i + (6 + h))
                    vec.tensor_tensor(hid[:, h * 512:(h + 1) * 512], ps[:, 2 + h, :],
                                      silu_s[:, h * 512:(h + 1) * 512], ALU.mult).then_inc(pair_dve, 1)
                dve.wait_ge(chunk_used, 12 * i + 12)
                for h in range(2):
                    cut = slice(h * 512, (h + 1) * 512)
                    vec.scalar_tensor_tensor(ye[:, cut], ps[:, 6 + h, :], gate_col[:, 0:1],
                                             mod_rows[:, 3 * D + h * 512:3 * D + (h + 1) * 512],
                                             ALU.mult, ALU.mult).then_inc(pair_dve, 1)
                dve.wait_ge(pair_dve, 16 * i + 6)
                vec.tensor_copy(ye_hi[:, :], ye[:, :]).then_inc(pair_dve, 1)
                dve.wait_ge(pair_dve, 16 * i + 7)
                vec.tensor_tensor(ye_lo[:, :], ye[:, :], ye_hi[:, :], ALU.subtract).then_inc(pair_dve, 1)
                for s in range(8):
                    dst = xa[:, s // 2, (s % 2) * 512:(s % 2 + 1) * 512]
                    dve.wait_ge(pair_full, 16 * i + (9 + s))
                    vec.tensor_tensor(dst, dst, ps[:, SCATTER_BANK[s], :], ALU.add).then_inc(pair_dve, 1)

            dve.wait_ge(pair_dve, 16 * PAIRS)
            dve.wait_ge(ln2_landed, 32)
            for i in range(T + 1):
                if i < T:
                    ln_stats(2 * T + i, xa[:, i, :])
                if i >= 1:
                    dve.wait_ge(normed, 2 * T + i)
                    vec.tensor_tensor(xa[:, i - 1, :], xa[:, i - 1, :], ln_rows[:, 0, :], ALU.mult).then_inc(w_applied, 1)
                if i < T:
                    ln_bias(2 * T + i)

        @block.tensor
        def _(pe):
            mm, flip = nc.tensor.matmul, nc.tensor.transpose

            def begin(job):
                if J.before(job):
                    wait_drained(pe, J.before(job))

            pe.wait_ge(ident_landed, 16)
            pe.wait_ge(vec_landed, 16 * 7)
            pe.wait_ge(silu_c, 1)
            begin("cols")
            flip(bank("cols")[:, 0:80], vec_rows[:, :], ident[0:80, 0:80]).then_inc(bank_full, 1)
            wait_drained(pe, "cols")
            pe.wait_ge(c_spread, 1)
            def modulation(k):
                wait_raw(pe, ("ada", k))
                w = raw_slot(("ada", k))
                for c in range(4):
                    ins = mm(bank("modrow")[32 * c:32 * c + 32, :], c_wide[:, k, :], w[:, c * 512:(c + 1) * 512],
                             start=(k == 0), stop=(k == K - 1))
                ins.then_inc(ada_used, 1)

            pe.wait_ge(set_up, 2)
            for i in range(T + C):
                pe.wait_ge(x_normed, i + 1)
                for h in range(2):
                    begin(("xT", i, h))
                    for k in range(4):
                        ins = flip(bank(("xT", i, h))[:, k * P:(k + 1) * P],
                                   x_in[:, i, (4 * h + k) * P:(4 * h + k + 1) * P], ident)
                    ins.then_inc(bank_full, 1)
                modulation(i)
            for k in range(T + C, K):
                modulation(k)
            pe.wait_ge(ada_used, K)
            pe.nop().then_inc(bank_full, 1)
            begin("mod")
            wait_drained(pe, "modrow")
            for c in range(4):
                ins = flip(bank("mod")[:, c * P:(c + 1) * P], mod_t[:, c * P:(c + 1) * P], ident)
            ins.then_inc(bank_full, 1)

            def product(job, a_hi, a_lo, b_hi, b_lo, first, last):
                o = bank(job)
                mm(o, a_hi, b_hi, start=first, stop=False)
                mm(o, a_hi, b_lo, start=False, stop=False)
                return mm(o, a_lo, b_hi, start=False, stop=last)

            def group(g, hi, lo, ready=None):
                gi = number_of[g]
                jobs = [(g, j) for j in range(4 + (C if g in WITH_CTX else 0))]
                for half in range(2):
                    pe.wait_ge(lo_made, 2 * gi + half + 1)
                    for kk in range(4):
                        k = 4 * half + kk
                        if ready:
                            ready(k)
                        w = [x[:, half, kk * 512:(kk + 1) * 512] for x in (w_hi, w_lo)]
                        for j, job in enumerate(jobs):
                            if k == 0:
                                begin(job)
                            cut = slice(j * P, (j + 1) * P)
                            if g in WIDE:
                                ins = product(job, w[0][:, cut], w[1][:, cut], hi[:, k, :], lo[:, k, :],
                                              k == 0, k == K - 1)
                            elif j < T:
                                ins = product(job, hi[:, k, cut], lo[:, k, cut], w[0], w[1], k == 0, k == K - 1)
                            else:
                                cut = slice((j - T) * P, (j - T + 1) * P)
                                ins = product(job, hc_hi[:, k, cut], hc_lo[:, k, cut], w[0], w[1],
                                              k == 0, k == K - 1)
                            if k == K - 1:
                                ins.then_inc(bank_full, 1)
                        if k == 3:
                            ins.then_inc(half_used, 1)

            def h_ready(k):
                pe.wait_ge(h_split, k + 1)

            group("k", h_hi, h_lo, h_ready)
            group("q", h_hi, h_lo)
            group("v0", h_hi, h_lo)
            group("v1", h_hi, h_lo)

            pe.wait_ge(roped, 2 * T)

            def turn_heads(h):
                for name, src in (("qT", q_s), ("kT", k_s)):
                    begin((name, h))
                    for n in range(T):
                        ins = flip(bank((name, h))[:, n * P:(n + 1) * P], src[:, n, h * DK:(h + 1) * DK], ident)
                    ins.then_inc(bank_full, 1)

            def states(h):
                pe.wait_ge(kz_made, h + 1)
                wait_drained(pe, ("v1", T + C - 1))
                cut = slice(h * DV, (h + 1) * DV)
                begin(("kv0", h))
                for s in range(2):
                    for i in range(C):
                        ins = mm(bank(("kv0", h))[:, s * DV:(s + 1) * DV], kcz[:, h % 2, s, i, :], vc_s[:, i, cut],
                                 start=(i == 0), stop=(i == C - 1))
                ins.then_inc(bank_full, 1)
                for j in range(T - 1):
                    begin(("kv", h, j))
                    o = bank(("kv", h, j))
                    mm(o[:, 0:DV], kz[:, h % 2, 0, j, :], v_s[:, j, cut], start=True, stop=True)
                    mm(o[:, DV:2 * DV], kz[:, h % 2, 1, T - 2 - j, :], v_s[:, T - 1 - j, cut],
                       start=True, stop=True).then_inc(bank_full, 1)
                begin(("sc", h))
                wait_drained(pe, ("kT", h))
                for n in range(T):
                    cut = slice(n * P, (n + 1) * P)
                    ins = mm(bank(("sc", h))[:, cut], k_t[:, h % 2, cut], q_t[:, h % 2, cut], start=True, stop=True)
                ins.then_inc(bank_full, 1)

            def outputs(h):
                wait_drained(pe, ("sc", h))
                pe.wait_ge(q_made, h + 1)
                for j in range(2):
                    begin(("o", h, j))
                    for n in (2 * j, 2 * j + 1):
                        o = bank(("o", h, j))[:, (n % 2) * DV:(n % 2 + 1) * DV]
                        cut = slice(n * P, (n + 1) * P)
                        mm(o, sm[:, h % 2, cut], v_s[:, n, h * DV:(h + 1) * DV], start=True, stop=False)
                        mm(o, q_f[:, h % 2, cut], state[:, 0, n, :], start=False, stop=False)
                        ins = mm(o, q_b[:, h % 2, cut], state[:, 1, T - 1 - n, :], start=False, stop=True)
                    ins.then_inc(bank_full, 1)

            turn_heads(0)
            states(0)
            for h in range(HEADS):
                if h + 1 < HEADS:
                    turn_heads(h + 1)
                outputs(h)
                if h + 1 < HEADS:
                    states(h + 1)

            for half in range(2):
                group(f"g{half}", h_hi, h_lo)
                pe.wait_ge(o_normed, 1)
                for c in range(4 * half, 4 * half + 4):
                    begin(("oT", c))
                    for n in range(T):
                        ins = flip(bank(("oT", c))[:, n * P:(n + 1) * P], o_s[:, n, c * P:(c + 1) * P], ident)
                    ins.then_inc(bank_full, 1)

            def ret_ready(k):
                pe.wait_ge(ret_made, k + 1)

            group("pa0", r_hi, r_lo, ret_ready)
            group("ga0", h_hi, h_lo)
            group("pa1", r_hi, r_lo)
            group("ga1", h_hi, h_lo)
            begin("swT")
            pe.wait_ge(sw_landed, 16)
            for g in range(GROUPS):
                ins = flip(bank("swT")[:, g * P:(g + 1) * P], sw_in[:, g, :], ident)
            ins.then_inc(bank_full, 1)
            group("vs0", h_hi, h_lo)
            group("vs1", h_hi, h_lo)
            for half in range(2):
                group(f"u{half}", h_hi, h_lo)
                if half == 0:
                    pe.wait_ge(vs_made, T)
                    wait_drained(pe, "swT")
                for c in range(4 * half, 4 * half + 4):
                    begin(("sp", c))
                    for n in range(T):
                        ins = mm(bank(("sp", c))[:, n * P:(n + 1) * P], vs_s[:, n, c * P:(c + 1) * P],
                                 sw_t[:, c // 2, :], start=True, stop=True)
                    ins.then_inc(bank_full, 1)

            def sgu_ready(k):
                pe.wait_ge(sgu_made, k + 1)

            pe.wait_ge(rows_summed, 2 * K)
            for i in range(8):
                begin(("row", i))
                mm(bank(("row", i)), ones[:, :], mod_rows[:, i * 512:(i + 1) * 512], start=True, stop=True)\
                    .then_inc(bank_full, 1)
            group("pb0", s_hi, s_lo, sgu_ready)
            group("gb0", h_hi, h_lo)
            group("pb1", s_hi, s_lo)
            group("gb1", h_hi, h_lo)

            def y_ready(k):
                pe.wait_ge(y_made, k + 1)

            group("wo0", y_hi, y_lo, y_ready)
            for half in range(2):
                pe.wait_ge(lo_made, 2 * len(ORDER) - 1 + half)
                for j in range(T):
                    if half == 0:
                        begin(("wo1", j))
                    cut = slice(j * P, (j + 1) * P)
                    for k in range(4 * half, 4 * half + 4):
                        w = [x[:, half, (k % 4) * 512:(k % 4 + 1) * 512] for x in (w_hi, w_lo)]
                        ins = product(("wo1", j), y_hi[:, k, cut], y_lo[:, k, cut], w[0], w[1], k == 0, k == K - 1)
                    if half:
                        ins.then_inc(bank_full, 1)

            pe.wait_ge(router_landed, 32)
            for i in range(T):
                pe.wait_ge(h2_made, i + 1)
                for h in range(2):
                    begin(("h2T", i, h))
                    for k in range(4):
                        ins = flip(bank(("h2T", i, h))[:, k * P:(k + 1) * P],
                                   h2[:, i, (4 * h + k) * P:(4 * h + k + 1) * P], ident)
                    ins.then_inc(bank_full, 1)
                begin(("lg", i))
                wait_drained(pe, ("h2T", i, 1))
                for k in range(K):
                    ins = mm(bank(("lg", i))[:, 0:NE], h2_t[:, i % 2, k, :], w_router[:, k, :],
                             start=(k == 0), stop=(k == K - 1))
                ins.then_inc(bank_full, 1)
            begin("affT")
            pe.wait_ge(exp_in, 4)
            for i in range(T):
                ins = mm(bank("affT")[0:NE, i * P:(i + 1) * P], aff[:, i, :], ident, start=True, stop=True)
            ins.then_inc(bank_full, 1)
            begin("posT")
            pe.wait_ge(exp_in, 5)
            for i in range(T):
                ins = flip(bank("posT")[:, i * NE:(i + 1) * NE], rank[:, i * P:(i + 1) * P], ident[0:NE, 0:NE])
            ins.then_inc(bank_full, 1)

            pe.wait_ge(h2_split, T)
            with pe.Fori(0, PAIRS) as i:
                pe.wait_ge(pair_dve, 16 * i + 1)
                for h in range(2):
                    for n in range(T):
                        for part in (h2_hi, h2_lo):
                            ins = mm(ps[:, 4 + h, :], sel[:, n, :], part[:, n, h * 512:(h + 1) * 512],
                                     start=(n == 0 and part is h2_hi), stop=(n == T - 1 and part is h2_lo))
                    ins.then_inc(pair_full, 1)
                for h in range(2):
                    pe.wait_ge(pair_act, 9 * i + (1 + h))
                    for k in range(4 * h, 4 * h + 4):
                        ins = flip(ps[:, 2 + h, (k % 4) * P:(k % 4 + 1) * P], x_rows[:, k * P:(k + 1) * P], ident)
                    ins.then_inc(pair_full, 1)
                for n in range(T):
                    ins = flip(ps[:, 6, n * P:(n + 1) * P], sel[:, n, :].bitcast(F32), ident)
                ins.then_inc(pair_full, 1)
                for n in range(T):
                    ins = mm(ps[:, 7, 0:2], sel[:, n, :].bitcast(F32), aff[:, n, bass.ds(2 * i, 2)],
                             start=(n == 0), stop=(n == T - 1))
                ins.then_inc(pair_full, 1)

                def expert_product(first_chunk, first_bank, operand, ready):
                    for c in range(first_chunk, first_chunk + 4):
                        pe.wait_ge(ring_landed[c % RING], 64 * i + 32 * (c // RING + 1))
                        for kk in range(2):
                            k = 2 * (c % 4) + kk
                            if k % 4 == 0:
                                pe.wait_ge(pair_act, 9 * i + ready[k // 4])
                            for f in range(2):
                                for e in range(2):
                                    ins = mm(ps[e * CAP:(e + 1) * CAP, first_bank + f, :],
                                             operand[:, k, e * CAP:(e + 1) * CAP],
                                             ring[c % RING][:, e, kk, f * 512:(f + 1) * 512],
                                             start=(k == 0), stop=(k == K - 1))
                        ins.then_inc(chunk_used, 1)

                expert_product(0, 0, xs, (3, 4))
                expert_product(4, 2, xs, (3, 4))
                for h in range(2):
                    pe.wait_ge(pair_dve, 16 * i + (3 + h))
                    for k in range(4 * h, 4 * h + 4):
                        ins = flip(ps[:, 4 + h, (k % 4) * P:(k % 4 + 1) * P], hid[:, k * P:(k + 1) * P], ident)
                    ins.then_inc(pair_full, 1)
                expert_product(8, 6, hid_t, (8, 9))
                pe.wait_ge(pair_dve, 16 * i + 8)
                for s in range(8):
                    n, h = s // 2, s % 2
                    if s >= 6:
                        pe.wait_ge(pair_dve, 16 * i + (9 + s - 6))
                    mm(ps[:, SCATTER_BANK[s], :], sel_t[:, n * P:(n + 1) * P], ye_hi[:, h * 512:(h + 1) * 512],
                       start=True, stop=False)
                    mm(ps[:, SCATTER_BANK[s], :], sel_t[:, n * P:(n + 1) * P], ye_lo[:, h * 512:(h + 1) * 512],
                       start=False, stop=True).then_inc(pair_full, 1)


_INS = ["x", "c", "ctx", "c_ctx", "w_ada", "b_ada", "w_in", "b_in", "ret_decay_f", "ret_decay_b", "ret_gn_w",
        "ret_gn_b", "sgu_ln_w", "sgu_ln_b", "sgu_w", "sgu_b", "w_pa", "w_pb", "w_o", "b_o", "ln1_w", "ln1_b",
        "w_router", "b_router", "w_gate", "w_up", "w_down", "ln2_w", "ln2_b"]


def kernel(**inputs):
    import concourse.bacc as _bacc
    from concourse.bass_utils import run_bass_kernel_spmd as _run

    nc = _bacc.Bacc("TRN2", target_bir_lowering=False, num_devices=1)
    arrays, tensors = {}, {}
    for name in _INS:
        a = np.ascontiguousarray(inputs[name])
        arrays[f"in_{name}"] = a
        tensors[name] = nc.dram_tensor(f"in_{name}", a.shape, mybir.dt.from_np(a.dtype), kind="ExternalInput").ap()
    seq, d_model = inputs["x"].shape[1:]
    shape_table, rope = shape_constants(seq, 128)
    for name, a in (("shape_table", shape_table), ("rope", rope)):
        arrays[f"in_{name}"] = a
        tensors[name] = nc.dram_tensor(f"in_{name}", a.shape, F32, kind="ExternalInput").ap()
    tensors["out"] = nc.dram_tensor("out_0", (1, seq, d_model), F32, kind="ExternalOutput").ap()
    mixer_and_experts(nc, tensors)
    r = _run(nc, [arrays], core_ids=[0])
    return r.results[0]["out_0"]
```

```python
from contextlib import ExitStack

import numpy as np

import concourse.bass as bass
from concourse import mybir

F32 = mybir.dt.float32
F32R = mybir.dt.float32r
ALU = mybir.AluOpType
ACT = mybir.ActivationFunctionType
AX_X = mybir.AxisListType.X

P = 128
BANKS = 8
BANK = 512
GRID_W = 64
ROPE_THETA = 10000.0
LN_EPS = 1e-6
DEPTH = 1
ALPHA = (2.0 * DEPTH) ** 0.25
CAPACITY_FACTOR = 2

SBUF_START = 16512
AREA = 7680


def place(kib):
    return SBUF_START + AREA + int((kib - 8) * 1024)


class Jobs:

    def __init__(self):
        self.number, self.bank, self.drainer = {}, {}, {}
        self.names, self.turn = [], 0

    def add(self, name, drainer, bank=None, banks=BANKS):
        if bank is None:
            bank = self.turn % banks
            self.turn = bank + 1
        self.number[name] = len(self.names) + 1
        self.bank[name], self.drainer[name] = bank, drainer
        self.names.append(name)

    def full(self, name):
        return self.number[name]

    def drained(self, name):
        return sum(self.drainer[n] == self.drainer[name] for n in self.names[:self.number[name]])

    def before(self, name):
        found = [n for n in self.names[:self.number[name] - 1] if self.bank[n] == self.bank[name]]
        return found[-1] if found else None


def shape_constants(seq, heads_dim):
    m, l = np.meshgrid(np.arange(P), np.arange(P), indexing="ij")
    p = np.arange(P)[:, None]
    ramps = np.concatenate([P - 1 - p, p, 2 * P - 1 - p, P + p], 1)
    slots = np.broadcast_to(np.arange(64)[None], (P, 64))
    table = np.concatenate([np.eye(P), slots, ramps, np.maximum(l - m, 0), np.maximum(m - l, 0),
                            l >= m, m >= l, l + 1, P - l], 1).astype(np.float32)
    t = np.arange(seq)
    n_freq = heads_dim // 4
    inv = (np.float32(ROPE_THETA) ** (-np.arange(n_freq, dtype=np.float32) / np.float32(n_freq))).astype(np.float32)
    pos = np.stack([t // GRID_W, t % GRID_W], -1).astype(np.float32)
    ang = (pos[..., None] * inv).astype(np.float32)
    cos, sin = np.cos(ang).astype(np.float32), np.sin(ang).astype(np.float32)
    both = np.stack([cos, cos], 2).reshape(seq, heads_dim)
    turn = np.stack([-sin, sin], 2).reshape(seq, heads_dim)
    scale = np.float32(heads_dim ** -0.5)
    rope = np.stack([both, turn, both * scale, turn * scale], 1).astype(np.float32)
    return table, np.ascontiguousarray(rope.reshape(seq // P, P, 4, heads_dim))


def mixer_and_experts(nc, t):
    x_d, ctx_d, out_d = t["x"], t["ctx"], t["out"]
    _, SEQ, D = x_d.shape
    CTX = ctx_d.shape[1]
    HEADS = t["ret_decay_f"].shape[1]
    D_IN = t["w_in"].shape[2]
    NE = t["w_gate"].shape[1]
    FE = t["w_gate"].shape[3]
    DK = 128
    DV = t["ret_gn_w"].shape[1] // HEADS
    QW, VW = HEADS * DK, HEADS * DV
    GROUPS = t["sgu_w"].shape[1]
    T, C, K = SEQ // P, CTX // P, D // P
    CAP = CAPACITY_FACTOR * SEQ // NE
    PAIRS = NE // 2
    CHUNKS = 12
    assert (T, C, K, CAP, QW, VW, FE) == (4, 2, 8, 64, 512, 1024, 1024)
    OFF_Q, OFF_K, OFF_V = 0, QW, 2 * QW
    OFF_G = OFF_V + VW
    OFF_U, OFF_VS, OFF_GA, OFF_GB = OFF_G + VW, OFF_G + VW + D, OFF_G + VW + 2 * D, OFF_G + VW + 3 * D
    assert OFF_GB + D == D_IN

    w_in, w_pa, w_pb, w_o = (t[n][0] for n in ("w_in", "w_pa", "w_pb", "w_o"))
    GROUP_LIST = [("k", w_in, OFF_K), ("q", w_in, OFF_Q), ("v0", w_in, OFF_V), ("v1", w_in, OFF_V + 512),
                  ("g0", w_in, OFF_G), ("g1", w_in, OFF_G + 512),
                  ("pa0", w_pa, 0), ("ga0", w_in, OFF_GA), ("pa1", w_pa, 512), ("ga1", w_in, OFF_GA + 512),
                  ("vs0", w_in, OFF_VS), ("vs1", w_in, OFF_VS + 512), ("u0", w_in, OFF_U), ("u1", w_in, OFF_U + 512),
                  ("pb0", w_pb, 0), ("gb0", w_in, OFF_GB), ("pb1", w_pb, 512), ("gb1", w_in, OFF_GB + 512),
                  ("wo0", w_o, 0), ("wo1", w_o, 512)]
    ORDER = [g[0] for g in GROUP_LIST]
    number_of = {name: i for i, name in enumerate(ORDER)}
    WITH_CTX = {"k", "v0", "v1"}
    WIDE = {"g0", "g1", "pa0", "ga0", "pa1", "ga1", "u0", "u1", "pb0", "gb0", "pb1", "gb1"}
    ROW_CHUNKS_AFTER = {"pa0": 4, "ga0": 4, "pa1": 4, "ga1": 4}

    J = Jobs()
    J.add("cols", "act", banks=7)
    for i in range(T + C):
        for h in range(2):
            J.add(("xT", i, h), "act", banks=7)
    J.add("modrow", "act", bank=7)
    J.add("mod", "dve", bank=6)
    J.turn = 0

    def group_jobs(g):
        who = "act" if g.rstrip("01") in ("g", "pa", "ga", "pb", "gb", "u") else "dve"
        for j in range(4):
            J.add((g, j), who)
        if g in WITH_CTX:
            for j in range(C):
                J.add((g, T + j), who)

    def state_jobs(h):
        J.add(("kv0", h), "act")
        for j in range(T - 1):
            J.add(("kv", h, j), "dve")
        J.add(("sc", h), "dve")

    for g in ("k", "q", "v0", "v1"):
        group_jobs(g)
    J.add(("qT", 0), "act")
    J.add(("kT", 0), "act")
    state_jobs(0)
    for h in range(HEADS):
        if h + 1 < HEADS:
            J.add(("qT", h + 1), "act")
            J.add(("kT", h + 1), "act")
        J.add(("o", h, 0), "act")
        J.add(("o", h, 1), "act")
        if h + 1 < HEADS:
            state_jobs(h + 1)
    for half in range(2):
        group_jobs(f"g{half}")
        for c in range(4 * half, 4 * half + 4):
            J.add(("oT", c), "dve")
    for g in ("pa0", "ga0", "pa1", "ga1"):
        group_jobs(g)
    J.add("swT", "act")
    group_jobs("vs0")
    group_jobs("vs1")
    for half in range(2):
        group_jobs(f"u{half}")
        for c in range(4 * half, 4 * half + 4):
            J.add(("sp", c), "dve")
    for i in range(8):
        J.add(("row", i), "act")
    for g in ("pb0", "gb0", "pb1", "gb1", "wo0", "wo1"):
        group_jobs(g)
    early = [J.bank["wo0", j] for j in range(T)]
    for i in range(T):
        for h in range(2):
            J.add(("h2T", i, h), "act", bank=early[h])
        J.add(("lg", i), "act", bank=early[2 + i % 2])
    J.add("lgT", "dve", bank=early[0])
    J.add("affT", "act")
    J.add("posT", "dve")

    RAW = 3
    raw_uses = [("ada", k) for k in range(K)]
    rows_left = [("row", n) for n in range(2 * K)]
    raw_uses += [(ORDER[0], 0), (ORDER[0], 1)]
    for gi, g in enumerate(ORDER):
        if gi + 1 < len(ORDER):
            raw_uses += [(ORDER[gi + 1], 0), (ORDER[gi + 1], 1)]
        for _ in range(ROW_CHUNKS_AFTER.get(g, 0)):
            raw_uses.append(rows_left.pop(0))
    assert not rows_left
    raw_at = {u: n for n, u in enumerate(raw_uses)}

    with ExitStack() as ctx:
        small_at = [SBUF_START]

        def small(name, shape, dt=F32):
            n = int(np.prod(shape[1:])) * 4
            a = nc.alloc_sbuf_tensor_at(name, list(shape), dt, offset=small_at[0])
            small_at[0] += (n + 31) // 32 * 32
            assert small_at[0] <= SBUF_START + AREA
            return a

        def at(kib, name, shape, dt=F32):
            return nc.alloc_sbuf_tensor_at(name, list(shape), dt, offset=place(kib))

        def sem(name):
            return ctx.enter_context(nc.semaphore(name))

        ps = ctx.enter_context(nc.psum_tensor("banks", [P, BANKS, BANK], F32))

        ident_slots = small("ident_slots", [P, P + 64 + 4])
        ident = ident_slots[:, 0:P]
        slot_ramp = ident_slots[:, P:P + 64]
        ramps = ident_slots[:, P + 64:P + 68]
        ones = small("ones", [P, P])
        vec_rows = small("vec_rows", [80, P])
        cols = small("cols", [P, 80])
        c_wide = small("c_wide", [P, K, 32])
        mod = small("mod", [P, 16, 2])
        stats = small("stats", [P, 6, 2, 6])
        moments = small("moments", [P, 6, 2])
        rstd = small("rstd", [P, 6])
        o_stats = small("o_stats", [P, T * HEADS, 6])
        o_moments = small("o_moments", [P, T * HEADS, 2])
        o_rstd = small("o_rstd", [P, T * HEADS])
        v_stats = small("v_stats", [P, T, 2, 6])
        v_moments = small("v_moments", [P, T, 2])
        v_rstd = small("v_rstd", [P, T])
        l_stats = small("l_stats", [P, 3 * T, 2, 6])
        l_moments = small("l_moments", [P, 3 * T, 2])
        l_rstd = small("l_rstd", [P, 3 * T])
        l_nmr = small("l_nmr", [P, 3 * T])
        powers = small("powers", [P, 16])
        decay = small("decay", [P, 2 * HEADS])
        decay_w = small("decay_w", [P, 4, 2 * HEADS])
        log_gamma = small("log_gamma", [P, 2 * HEADS])
        zeta_arg = small("zeta_arg", [P, 6, HEADS])
        zeta = small("zeta", [P, 6, HEADS])
        zeta_ctx = small("zeta_ctx", [P, 4, HEADS])
        w_router = small("w_router_s", [P, K, NE])
        b_router = small("b_router_s", [NE, 1])
        logits = small("logits", [P, T, NE])
        aff = small("aff", [P, T, NE])
        soft = small("soft", [P, 3, T])
        pos_t = small("pos_t", [P, T, NE])
        top8 = small("top8", [NE, 2, 8])
        gate_col = small("gate_col", [P, 1])

        raw = at(8, "raw", [P, RAW, 2048])
        w_hi = at(32, "w_hi", [P, 2, 2048], F32R)
        w_lo = at(48, "w_lo", [P, 2, 2048], F32R)
        h_hi = at(64, "h_hi", [P, K, SEQ], F32R)
        h_lo = at(80, "h_lo", [P, K, SEQ], F32R)
        x_in = at(96, "x_in", [P, T + C, D])
        xn_t = at(120, "xn_t", [P, K, SEQ + CTX])
        mod_t = at(188, "mod_t", [P, 512])
        hc_hi = at(144, "hc_hi", [P, K, CTX], F32R)
        hc_lo = at(152, "hc_lo", [P, K, CTX], F32R)
        h_tmp = at(182, "h_tmp", [P, 2, SEQ + CTX])
        tables = at(202, "tables", [P, 6 * P])
        k_s = at(96, "k_s", [P, T, QW])
        q_s = at(104, "q_s", [P, T, QW])
        v_s = at(112, "v_s", [P, T, VW])
        kc_s = at(128, "kc_s", [P, C, QW])
        vc_s = at(132, "vc_s", [P, C, VW])
        b_row = at(160, "b_row", [P, 2 * QW + VW])
        rope = at(168, "rope", [P, T, 4, DK])
        rope_tmp = at(176, "rope_tmp", [P, 2, QW])
        mask = at(180, "mask", [P, HEADS, P])
        q_t = at(152, "q_t", [P, 2, SEQ])
        k_t = at(156, "k_t", [P, 2, SEQ])
        q_f = at(160, "q_f", [P, 2, SEQ])
        q_b = at(164, "q_b", [P, 2, SEQ])
        kz = at(168, "kz", [P, 2, 2, T - 1, DK])
        kcz = at(140, "kcz", [P, 2, 2, C, DK])
        sm = at(176, "sm", [P, 2, SEQ])
        state = at(144, "state", [P, 2, T, DV])
        xi = at(182, "xi_rows", [P, 2, HEADS, P])
        o_s = at(186, "o_s", [P, T, VW])
        g_t = at(96, "g_t", [P, K, SEQ])
        r_hi = at(112, "r_hi", [P, K, SEQ], F32R)
        r_lo = at(128, "r_lo", [P, K, SEQ], F32R)
        prod = at(144, "prod", [P, 2, SEQ])
        ya = at(96, "ya", [P, K, SEQ])
        gate_s = at(148, "gate_s", [P, 2, SEQ])
        mod_rows = at(152, "mod_rows", [P, 4 * D])
        vs_s = at(168, "vs_s", [P, T, D])
        vs_rows = at(184, "vs_rows", [P, 3, D])
        u_t = at(196, "u_t", [P, 4, SEQ])
        sw_in = at(204, "sw_in", [P, GROUPS, P])
        sw_t = at(206, "sw_t", [P, GROUPS, P])
        sgu_b = at(184, "sgu_b_s", [P, GROUPS, P])
        s_hi = at(112, "s_hi", [P, K, SEQ], F32R)
        s_lo = at(128, "s_lo", [P, K, SEQ], F32R)
        pb_s = at(200, "pb_s", [P, 4, SEQ])
        y_hi = at(168, "y_hi", [P, K, SEQ], F32R)
        y_lo = at(184, "y_lo", [P, K, SEQ], F32R)
        xa = at(96, "xa", [P, T, D])
        b_o = at(112, "b_o_s", [P, D])
        ln_rows = at(200, "ln_rows", [P, 2, D])
        ln_tmp = at(144, "ln_tmp", [P, 2, D])
        h2 = at(112, "h2", [P, T, D])
        h2_hi = at(8, "h2_hi", [P, T, D], F32R)
        h2_lo = at(32, "h2_lo", [P, T, D], F32R)
        h2_t = at(24, "h2_t", [P, 2, K, P])
        logits_t = at(32, "logits_t", [NE, SEQ])
        aff_t = at(24, "aff_t", [NE, SEQ])
        work = at(26, "work", [NE, SEQ])
        picked = at(28, "picked", [NE, SEQ])
        rank = at(30, "rank", [NE, SEQ])
        RING = 8
        ring_at = (64, 80, 128, 48, 168, 184, 144, 112)
        ring = [at(kib, f"ring{n}", [P, 2, 2, FE]) for n, kib in enumerate(ring_at)]
        sel = at(24, "sel", [P, T, P], F32R)
        sel_t = at(26, "sel_t", [P, SEQ], F32R)
        silu_s = at(28, "silu_s", [P, FE])
        ye = at(28, "ye", [P, D])
        x_rows = at(160, "x_rows", [P, D])
        hid = at(160, "hid", [P, FE])
        ye_hi = at(160, "ye_hi", [P, D], F32R)
        xs = at(200, "xs", [P, K, P])
        hid_t = at(200, "hid_t", [P, K, P])
        ye_lo = at(200, "ye_lo", [P, D], F32R)
        ln2_rows = at(64, "ln2_rows", [P, 2, D])

        raw_landed = [sem(f"raw_landed{i}") for i in range(RAW)]
        ring_landed = [sem(f"ring_landed{i}") for i in range(RING)]
        vec_landed = sem("vec_landed")
        x_landed = [sem(f"x_landed{i}") for i in range(T + C)]
        ident_landed = sem("ident_landed")
        tables_landed = sem("tables_landed")
        decay_landed = sem("decay_landed")
        b_row_landed = sem("b_row_landed")
        rope_landed = sem("rope_landed")
        router_landed = sem("router_landed")
        vs_rows_landed = sem("vs_rows_landed")
        sw_landed = sem("sw_landed")
        sgu_b_landed = sem("sgu_b_landed")
        rows_zeroed = sem("rows_zeroed")
        rows_started = sem("rows_started")
        xa_landed = sem("xa_landed")
        b_o_landed = sem("b_o_landed")
        ln1_landed = sem("ln1_landed")
        ln2_landed = sem("ln2_landed")
        stored = sem("stored")
        bank_full = sem("bank_full")
        act_drained = sem("act_drained")
        dve_drained = sem("dve_drained")
        set_up = sem("set_up")
        silu_c = sem("silu_c")
        var_ready = sem("var_ready")
        rstd_ready = sem("rstd_ready")
        eps_added = sem("eps_added")
        x_normed = sem("x_normed")
        ada_used = sem("ada_used")
        c_spread = sem("c_spread")
        h_made = sem("h_made")
        h_split = sem("h_split")
        hi_made = sem("hi_made")
        lo_made = sem("lo_made")
        half_used = sem("half_used")
        exp_in = sem("exp_in")
        exp_out = sem("exp_out")
        masks_made = sem("masks_made")
        roped = sem("roped")
        kz_made = sem("kz_made")
        q_made = sem("q_made")
        o_normed = sem("o_normed")
        ret_made = sem("ret_made")
        gated = sem("gated")
        gelu_done = sem("gelu_done")
        vs_scaled = sem("vs_scaled")
        vs_made = sem("vs_made")
        sgu_made = sem("sgu_made")
        y_made = sem("y_made")
        rows_summed = sem("rows_summed")
        w_applied = sem("w_applied")
        b_applied = sem("b_applied")
        sc_applied = sem("sc_applied")
        h2_made = sem("h2_made")
        h2_last = sem("h2_last")
        nmr_made = sem("nmr_made")
        normed = sem("normed")
        h2_copied = sem("h2_copied")
        acc_scaled = sem("acc_scaled")
        h2_split = sem("h2_split")
        out_ready = sem("out_ready")
        last_ready = sem("last_ready")
        dve_step = sem("dve_step")
        act_step = sem("act_step")
        chunk_used = sem("chunk_used")
        pair_full = sem("pair_full")
        pair_act = sem("pair_act")
        pair_dve = sem("pair_dve")

        LATE = [0] + [n for i in range(1, T) for n in (2 * i, 2 * i - 1)] + [2 * T - 1] + [2 * T + i for i in range(T)]
        SCATTER_BANK = (0, 1, 2, 3, 4, 5, 0, 1)
        drained_by = {"act": act_drained, "dve": dve_drained}

        def wait_full(eng, job):
            eng.wait_ge(bank_full, J.full(job))

        def wait_drained(eng, job):
            eng.wait_ge(drained_by[J.drainer[job]], J.drained(job))

        def bank(job):
            return ps[:, J.bank[job], :]

        def last_job(g):
            return (g, T + C - 1) if g in WITH_CTX else (g, 3)

        def wait_raw(eng, use):
            n = raw_at[use]
            eng.wait_ge(raw_landed[n % RAW], 16 * (n // RAW + 1))

        def raw_slot(use):
            return raw[:, raw_at[use] % RAW, :]

        def parts(gi, half):
            return 4 * (half + 1) if gi == 0 else K + 2 * (gi - 1) + half + 1

        def wait_weights_free(eng, gi, half):
            if gi == 0:
                return
            if half == 0:
                eng.wait_ge(half_used, gi)
            else:
                wait_full(eng, last_job(ORDER[gi - 1]))

        vec = nc.vector
        act_e = nc.scalar
        pool_e = nc.gpsimd
        block = ctx.enter_context(nc.Block())

        expert_w = [t[n].rearrange("l e (c k p) f -> (l e) c p k f", k=2, p=P) for n in ("w_gate", "w_up", "w_down")]

        VECTORS = ((0, t["c"][0]), (8, t["c_ctx"]), (16, t["b_ada"][0, 0:2 * D]), (32, t["b_in"][0, OFF_G:OFF_G + 2 * D]),
                   (48, t["b_in"][0, OFF_GA:OFF_GA + 2 * D]), (64, t["ret_gn_w"][0]), (72, t["ret_gn_b"][0]))

        def load_vectors(eng, vectors):
            for first, v in vectors:
                n = v.shape[0] // P
                eng.dma_start(vec_rows[first:first + n, :], v.rearrange("(r n) -> r n", n=P)).then_inc(vec_landed, 16)

        @block.sync
        def _(sp):
            w_ada = t["w_ada"][0]
            sp.dma_start(ident_slots[:, :], t["shape_table"][:, 0:P + 68]).then_inc(ident_landed, 16)
            load_vectors(sp, VECTORS[:4])
            for n, use in enumerate(raw_uses):
                kind, part = use
                if n >= RAW:
                    was, was_part = raw_uses[n - RAW]
                    if was == "ada":
                        sp.wait_ge(ada_used, was_part + 1)
                    elif was == "row":
                        sp.wait_ge(rows_summed, was_part + 1)
                    else:
                        sp.wait_ge(lo_made, parts(number_of[was], was_part))
                slot = raw_slot(use)
                if kind == "ada":
                    sp.dma_start(slot, w_ada[part * P:(part + 1) * P, 0:2 * D]).then_inc(raw_landed[n % RAW], 16)
                elif kind == "row":
                    k, side = part % K, part // K
                    sp.dma_start(slot, w_ada[k * P:(k + 1) * P, 2 * D * (1 + side):2 * D * (2 + side)])\
                        .then_inc(raw_landed[n % RAW], 16)
                else:
                    _, w, first = GROUP_LIST[number_of[kind]]
                    rows = w[part * 4 * P:(part + 1) * 4 * P, first:first + 512].rearrange("(k p) n -> p k n", p=P)
                    sp.dma_start(slot.rearrange("p (k n) -> p k n", k=4), rows).then_inc(raw_landed[n % RAW], 16)

            def load_chunk(i, c):
                pair, m = c // CHUNKS, c % CHUNKS
                for e in range(2):
                    sp.dma_start(ring[c % RING][:, e, :, :], expert_w[m // 4][4 * i + (2 * pair + e), m % 4])\
                        .then_inc(ring_landed[c % RING], 16)

            for c in range(2 * CHUNKS):
                if c == 0:
                    wait_full(sp, ("gb1", 3))
                    sp.wait_ge(ln1_landed, 32)
                if c == 3:
                    wait_full(sp, ("wo1", 3))
                if c == 6:
                    sp.wait_ge(h2_made, T - 1)
                    sp.wait_ge(h2_last, 1)
                if c == 7:
                    sp.wait_ge(h2_split, T)
                    wait_full(sp, ("h2T", T - 1, 1))
                if c >= RING:
                    sp.wait_ge(chunk_used, c - RING + 1)
                load_chunk(0, c)
            with sp.Fori(1, PAIRS // 2) as i:
                for c in range(2 * CHUNKS):
                    sp.wait_ge(chunk_used, 2 * CHUNKS * i + (c - RING + 1))
                    load_chunk(i, c)
            sp.wait_ge(chunk_used, CHUNKS * PAIRS - RING + 1)
            for j, row in enumerate((t["ln2_w"][0], t["ln2_b"][0])):
                sp.dma_start(ln2_rows[:, j, :], row.partition_broadcast(P)).then_inc(ln2_landed, 16)
            out_v = out_d.rearrange("b (t p) d -> (b t) p d", p=P)
            for i in range(T):
                if i < T - 1:
                    sp.wait_ge(out_ready, i + 1)
                else:
                    sp.wait_ge(last_ready, 1)
                sp.dma_start(out_v[i], xa[:, i, :]).then_inc(stored, 16)
            sp.wait_ge(stored, 16 * T)

        @block.gpsimd
        def _(pool):
            pool_e.memset(ones[:, :], 1.0).then_inc(set_up, 1)
            pool_e.memset(powers[:, :], -0.5).then_inc(set_up, 1)
            pool.wait_ge(set_up, 2)
            turn = [0]

            def rsqrt(out, var, n):
                turn[0] += 1
                pool.wait_ge(var_ready, turn[0])
                pool_e.tensor_scalar(out, var, LN_EPS, None, ALU.add).then_inc(eps_added, 1)
                pool.wait_ge(eps_added, turn[0])
                pool_e.tensor_tensor(out, out, powers[:, 0:n], ALU.pow).then_inc(rstd_ready, 1)

            for i in range(T + C):
                rsqrt(rstd[:, i:i + 1], moments[:, i, 1:2], 1)
            pool.wait_ge(ada_used, K - 2)
            pool.dma_start(tables[:, :], t["shape_table"][:, P + 68:]).then_inc(tables_landed, 16)
            pool.dma_start(decay[:, 0:HEADS], t["ret_decay_f"][0].partition_broadcast(P)).then_inc(decay_landed, 16)
            pool.dma_start(decay[:, HEADS:], t["ret_decay_b"][0].partition_broadcast(P)).then_inc(decay_landed, 16)
            pool.dma_start(b_row[:, :], t["b_in"][0, 0:OFF_G].partition_broadcast(P)).then_inc(b_row_landed, 16)
            pool.dma_start(rope[:, :, :, :].rearrange("p t a d -> p t (a d)"),
                           t["rope"].rearrange("t p a d -> p t (a d)")).then_inc(rope_landed, 16)
            pool.dma_start(w_router[:, :, :], t["w_router"][0].rearrange("(k p) e -> p k e", p=P)).then_inc(router_landed, 16)
            pool.dma_start(b_router[:, :], t["b_router"].rearrange("o e -> e o")).then_inc(router_landed, 16)
            rsqrt(o_rstd[:, :], o_moments[:, :, 1], T * HEADS)
            wait_full(pool, ("oT", 3))
            pool_e.memset(mod_rows[:, :], 0.0).then_inc(rows_zeroed, 1)
            pool.wait_ge(rows_zeroed, 1)
            pool.dma_start(mod_rows[0:1, :], t["b_ada"][:, 2 * D:6 * D]).then_inc(rows_started, 16)
            wait_full(pool, ("oT", 7))
            for j, row in enumerate((t["b_in"][0, OFF_VS:OFF_VS + D], t["sgu_ln_w"][0], t["sgu_ln_b"][0])):
                pool.dma_start(vs_rows[:, j, :], row.partition_broadcast(P)).then_inc(vs_rows_landed, 16)
            pool.dma_start(sw_in[:, :, :], t["sgu_w"][0].rearrange("g p q -> p g q")).then_inc(sw_landed, 16)
            pool.wait_ge(vs_rows_landed, 48)
            for i in range(T + 1):
                if i < T:
                    rsqrt(v_rstd[:, i:i + 1], v_moments[:, i, 1:2], 1)
                if i >= 1:
                    pool.wait_ge(vs_scaled, i)
                    pool_e.tensor_tensor(vs_s[:, i - 1, :], vs_s[:, i - 1, :], vs_rows[:, 2, :], ALU.add)\
                        .then_inc(vs_made, 1)
            pool.wait_ge(vs_made, T)
            pool.dma_start(sgu_b[:, :, :].rearrange("p g q -> p (g q)"),
                           t["sgu_b"][0].rearrange("g q -> (g q)").partition_broadcast(P)).then_inc(sgu_b_landed, 16)
            wait_full(pool, ("pb1", 3))
            pool.dma_start(b_o[:, :], t["b_o"][0].partition_broadcast(P)).then_inc(b_o_landed, 16)
            pool.wait_ge(y_made, K)
            pool.dma_start(xa[:, :, :], x_d[0].rearrange("(t p) d -> p t d", p=P)).then_inc(xa_landed, 16)
            for j, row in enumerate((t["ln1_w"][0], t["ln1_b"][0])):
                pool.dma_start(ln_rows[:, j, :], row.partition_broadcast(P)).then_inc(ln1_landed, 16)

            def ln1_rsqrt(i):
                rsqrt(l_rstd[:, 2 * i:2 * i + 1], l_moments[:, 2 * i, 1:2], 1)

            def h2_rsqrt(i):
                rsqrt(l_rstd[:, 2 * i + 1:2 * i + 2], l_moments[:, 2 * i + 1, 1:2], 1)

            def ln1_bias(i):
                pool.wait_ge(w_applied, i + 1)
                pool_e.tensor_tensor(xa[:, i, :], xa[:, i, :], ln_rows[:, 1, :], ALU.add).then_inc(b_applied, 1)

            def h2_shift(i):
                pool.wait_ge(sc_applied, i + 1)
                pool_e.tensor_tensor(h2[:, i, :], h2[:, i, :], mod_rows[:, D:2 * D], ALU.add).then_inc(h2_made, 1)

            pool.wait_ge(ln1_landed, 32)
            for i in range(T + 2):
                if i < T:
                    ln1_rsqrt(i)
                if 1 <= i <= T:
                    h2_rsqrt(i - 1)
                if 2 <= i <= T:
                    h2_shift(i - 2)
                if i < T:
                    ln1_bias(i)
            wait_full(pool, ("wo1", 3))
            for i in range(T):
                pool.wait_ge(h2_copied, i + 1)
                pool_e.tensor_tensor(h2_lo[:, i, :], h2[:, i, :], h2_hi[:, i, :], ALU.subtract).then_inc(h2_split, 1)
            pool.wait_ge(ln2_landed, 32)
            for i in range(T):
                rsqrt(l_rstd[:, 2 * T + i:2 * T + i + 1], l_moments[:, 2 * T + i, 1:2], 1)
                if i >= 1:
                    pool.wait_ge(w_applied, T + i)
                    pool_e.tensor_tensor(xa[:, i - 1, :], xa[:, i - 1, :], ln2_rows[:, 1, :], ALU.add)\
                        .then_inc(out_ready, 1)

        @block.scalar
        def _(act):
            load_vectors(act, VECTORS[4:])
            for i in range(T + C):
                src = x_d[0, i * P:(i + 1) * P, :] if i < T else ctx_d[0, (i - T) * P:(i - T + 1) * P, :]
                act.dma_start(x_in[:, i, :], src).then_inc(x_landed[i], 16)

            act.wait_ge(vec_landed, 16 * len(VECTORS))
            act_e.activation(vec_rows[0:16, :], vec_rows[0:16, :], ACT.Silu).then_inc(silu_c, 1)
            wait_full(act, "cols")
            act_e.activation(cols[:, :], bank("cols")[:, 0:80], ACT.Copy).then_inc(act_drained, 1)
            for i in range(T + C):
                for h in range(2):
                    wait_full(act, ("xT", i, h))
                    act_e.activation(xn_t[:, 4 * h:4 * h + 4, i * P:(i + 1) * P],
                                     bank(("xT", i, h)).rearrange("p (k n) -> p k n", k=4), ACT.Copy)\
                        .then_inc(act_drained, 1)

            def high_part(gi, half):
                use = (ORDER[gi], half)
                wait_raw(act, use)
                wait_weights_free(act, gi, half)
                act_e.activation(w_hi[:, half, :], raw_slot(use), ACT.Copy).then_inc(hi_made, 1)

            wait_full(act, "modrow")
            act_e.activation(mod_t[:, :], bank("modrow"), ACT.Copy).then_inc(act_drained, 1)
            wait_drained(act, "mod")
            wait_drained(act, ("xT", T + C - 1, 1))
            for k in range(K):
                if k >= 2:
                    act.wait_ge(h_split, k - 1)
                for j, (lo, hi) in enumerate(((0, SEQ), (SEQ, SEQ + CTX))):
                    act_e.activation(h_tmp[:, k % 2, lo:hi], xn_t[:, k, lo:hi], ACT.Identity,
                                     scale=mod[:, 8 + k, j:j + 1], bias=mod[:, k, j:j + 1]).then_inc(h_made, 1)
                if k % 4 == 0:
                    wait_raw(act, (ORDER[0], k // 4))
                cut = slice((k % 4) * 512, (k % 4 + 1) * 512)
                act_e.activation(w_hi[:, k // 4, cut], raw_slot((ORDER[0], k // 4))[:, cut], ACT.Copy).then_inc(hi_made, 1)

            def exps():
                act.wait_ge(exp_in, 1)
                act_e.activation(decay_w[:, 1, :], decay_w[:, 0, :], ACT.Exp).then_inc(exp_out, 1)
                act.wait_ge(exp_in, 2)
                act_e.activation(zeta[:, :, :], zeta_arg[:, :, :], ACT.Exp).then_inc(exp_out, 1)
                act.wait_ge(tables_landed, 16)
                for s in range(2):
                    for h in range(HEADS):
                        act_e.activation(xi[:, s, h, :], tables[:, (4 + s) * P:(5 + s) * P], ACT.Exp,
                                         scale=log_gamma[:, s * HEADS + h:s * HEADS + h + 1]).then_inc(exp_out, 1)
                for h in range(HEADS):
                    act_e.activation(mask[:, h, :], tables[:, 0:P], ACT.Exp,
                                     scale=log_gamma[:, h:h + 1]).then_inc(exp_out, 1)
                    act_e.activation(o_s[:, 0, h * P:(h + 1) * P], tables[:, P:2 * P], ACT.Exp,
                                     scale=log_gamma[:, HEADS + h:HEADS + h + 1]).then_inc(exp_out, 1)

            def retention():
                def transposed(h):
                    for name, dst in (("qT", q_t), ("kT", k_t)):
                        wait_full(act, (name, h))
                        act_e.activation(dst[:, h % 2, :], bank((name, h)), ACT.Copy).then_inc(act_drained, 1)

                def first_state(h):
                    wait_full(act, ("kv0", h))
                    act_e.activation(state[:, :, 0, :], bank(("kv0", h)).rearrange("p (s v) -> p s v", s=2),
                                     ACT.Copy).then_inc(act_drained, 1)

                transposed(0)
                first_state(0)
                high_part(number_of["g0"], 1)
                for h in range(HEADS):
                    if h + 1 < HEADS:
                        transposed(h + 1)
                    if h == 0:
                        act.wait_ge(masks_made, 1)
                    for j in range(2):
                        wait_full(act, ("o", h, j))
                        act_e.activation(o_s[:, 2 * j:2 * j + 2, h * DV:(h + 1) * DV],
                                         bank(("o", h, j)).rearrange("p (n v) -> p n v", n=2),
                                         ACT.Copy).then_inc(act_drained, 1)
                    if h + 1 < HEADS:
                        first_state(h + 1)

            gates_seen = [0]

            def drain(g):
                half = int(g[-1])
                for j in range(4):
                    c = 4 * half + j
                    wait_full(act, (g, j))
                    if g in ("g0", "g1"):
                        act_e.activation(g_t[:, c, :], bank((g, j)), ACT.Silu,
                                         bias=cols[:, 32 + c:33 + c]).then_inc(act_drained, 1)
                    elif g in ("pa0", "pa1"):
                        act_e.activation(ya[:, c, :], bank((g, j)), ACT.Copy).then_inc(act_drained, 1)
                    elif g in ("pb0", "pb1"):
                        if half:
                            act.wait_ge(y_made, j + 1)
                        else:
                            act.wait_ge(sgu_made, K)
                        act_e.activation(pb_s[:, j, :], bank((g, j)), ACT.Copy).then_inc(act_drained, 1)
                    elif g in ("u0", "u1"):
                        if half:
                            act.wait_ge(sgu_made, c - 3)
                        act_e.activation(u_t[:, j, :], bank((g, j)), ACT.Gelu_apprx_tanh,
                                         bias=cols[:, 40 + c:41 + c]).then_inc(act_drained, 1)
                    else:
                        n = gates_seen[0]
                        gates_seen[0] += 1
                        if n >= 2:
                            act.wait_ge(gated, n - 1)
                        first = 48 if g.startswith("ga") else 56
                        act_e.activation(gate_s[:, n % 2, :], bank((g, j)), ACT.Sigmoid,
                                         bias=cols[:, first + c:first + c + 1]).then_inc(act_drained, 1)

            def gelu_vs(half):
                for i in range(T):
                    wait_drained(act, (f"vs{half}", i))
                    v = vs_s[:, i, half * 512:(half + 1) * 512]
                    act_e.activation(v, v, ACT.Gelu_apprx_tanh).then_inc(gelu_done, 1)

            for gi, g in enumerate(ORDER):
                if gi + 1 < len(ORDER):
                    high_part(gi + 1, 0)
                if J.drainer[(g, 0)] == "act":
                    drain(g)
                if gi + 1 < len(ORDER) and g != "v1":
                    high_part(gi + 1, 1)
                if g == "k":
                    exps()
                if g == "v1":
                    retention()
                if g == "ga1":
                    wait_full(act, "swT")
                    act_e.activation(sw_t[:, :, :], bank("swT").rearrange("p (g q) -> p g q", g=GROUPS),
                                     ACT.Copy).then_inc(act_drained, 1)
                if g in ("vs0", "vs1"):
                    gelu_vs(int(g[-1]))
                if g == "u1":
                    for i in range(8):
                        wait_full(act, ("row", i))
                        act_e.activation(mod_rows[:, i * 512:(i + 1) * 512], bank(("row", i)), ACT.Copy,
                                         bias=1.0 if i in (4, 5) else 0.0).then_inc(act_drained, 1)

            def normalise(n, dst, src):
                act.wait_ge(nmr_made, LATE.index(n) + 1)
                act_e.activation(dst, src, ACT.Identity, scale=l_rstd[:, n:n + 1], bias=l_nmr[:, n:n + 1])\
                    .then_inc(normed, 1)

            def router_logits(i):
                for h in range(2):
                    wait_full(act, ("h2T", i, h))
                    act_e.activation(h2_t[:, i % 2, 4 * h:4 * h + 4, :],
                                     bank(("h2T", i, h)).rearrange("p (k n) -> p k n", k=4), ACT.Copy)\
                        .then_inc(act_drained, 1)
                wait_full(act, ("lg", i))
                act_e.activation(logits_t[:, i * P:(i + 1) * P], bank(("lg", i))[0:NE, 0:P], ACT.Identity,
                                 bias=b_router[:, :]).then_inc(act_drained, 1)

            act.wait_ge(router_landed, 32)
            for i in range(T + 3):
                if i < T:
                    normalise(2 * i, xa[:, i, :], xa[:, i, :])
                if 1 <= i <= T:
                    normalise(2 * i - 1, h2[:, i - 1, :], xa[:, i - 1, :])
                if i >= 3:
                    router_logits(i - 3)
            wait_drained(act, "lgT")
            act_e.activation(logits[:, :, :], logits[:, :, :], ACT.Exp).then_inc(exp_out, 1)
            wait_full(act, "affT")
            act_e.activation(aff_t[:, :], bank("affT")[0:NE, :], ACT.Copy).then_inc(act_drained, 1)
            for i in range(T):
                act_e.activation(h2_hi[:, i, :], h2[:, i, :], ACT.Copy).then_inc(h2_copied, 1)
            for i in range(T):
                act_e.activation(xa[:, i, :], xa[:, i, :], ACT.Copy, scale=ALPHA).then_inc(acc_scaled, 1)

            def pair_of_experts(i, pair):
                full, dve_side = 32 * i + 16 * pair, 32 * i + 16 * pair
                for h in range(2):
                    act.wait_ge(pair_full, full + (1 + h))
                    act_e.activation(x_rows[:, h * 512:(h + 1) * 512], ps[:, 4 + h, :], ACT.Copy)\
                        .then_inc(pair_act, 1)
                for h in range(2):
                    act.wait_ge(pair_full, full + (3 + h))
                    act_e.activation(xs[:, 4 * h:4 * h + 4, :], ps[:, 2 + h, :].rearrange("p (k n) -> p k n", k=4),
                                     ACT.Copy).then_inc(pair_act, 1)
                act.wait_ge(pair_full, full + 5)
                act_e.activation(sel_t[:, :], ps[:, 6, :], ACT.Copy).then_inc(pair_act, 1)
                act.wait_ge(chunk_used, 24 * i + (12 * pair + 4))
                for h in range(2):
                    act_e.activation(silu_s[:, h * 512:(h + 1) * 512], ps[:, h, :], ACT.Silu).then_inc(pair_act, 1)
                for h in range(2):
                    act.wait_ge(pair_full, full + (7 + h))
                    act_e.activation(hid_t[:, 4 * h:4 * h + 4, :], ps[:, 4 + h, :].rearrange("p (k n) -> p k n", k=4),
                                     ACT.Copy).then_inc(pair_act, 1)
                for h in range(2):
                    act.wait_ge(pair_dve, dve_side + (5 + h))
                    act_e.activation(ye_hi[:, h * 512:(h + 1) * 512], ye[:, h * 512:(h + 1) * 512], ACT.Copy)\
                        .then_inc(pair_act, 1)

            with act.Fori(0, PAIRS // 2) as i:
                pair_of_experts(i, 0)
                pair_of_experts(i, 1)
            for i in range(T):
                normalise(2 * T + i, xa[:, i, :], xa[:, i, :])

        @block.vector
        def _(dve):
            steps = [0]

            def step(ins):
                steps[0] += 1
                ins.then_inc(dve_step, 1)
                dve.wait_ge(dve_step, steps[0])

            def moments_of(src, st, mo):
                n = src.shape[1] // 512 or 1
                for j in range(n):
                    ins = vec.bn_stats(st[:, j, :] if n > 1 else st, src[:, j * 512:(j + 1) * 512])
                step(ins)
                vec.bn_aggr(mo, st.rearrange("p a b -> p (a b)") if n > 1 else st).then_inc(var_ready, 1)

            groups_of_var = [0]

            def normalise(dst, src, mo, rs):
                groups_of_var[0] += 1
                dve.wait_ge(rstd_ready, groups_of_var[0])
                return vec.tensor_scalar(dst, src, mo[:, 0:1], rs, ALU.subtract, ALU.mult)

            wait_drained(dve, "cols")
            vec.tensor_copy(c_wide[:, :, :].rearrange("p k (x n) -> p k x n", x=2),
                            cols[:, 0:16].rearrange("p (x k) -> p k x", x=2).unsqueeze(3)
                            .broadcast_to([P, K, 2, 16])).then_inc(c_spread, 1)
            for i in range(T + C + 1):
                if i < T + C:
                    dve.wait_ge(x_landed[i], 16)
                    moments_of(x_in[:, i, :], stats[:, i, :, :], moments[:, i, :])
                if i >= 1:
                    normalise(x_in[:, i - 1, :], x_in[:, i - 1, :], moments[:, i - 1, :],
                              rstd[:, i - 1:i]).then_inc(x_normed, 1)

            def log_gammas():
                dve.wait_ge(decay_landed, 32)
                step(vec.tensor_scalar(decay_w[:, 2, :], decay[:, :], -1.0, None, ALU.mult))
                vec.tensor_tensor(decay_w[:, 0, :], decay[:, :], decay_w[:, 2, :], ALU.min).then_inc(exp_in, 1)
                dve.wait_ge(exp_out, 1)
                y, s, s2, q = (decay_w[:, j, :] for j in (1, 2, 3, 0))
                step(vec.tensor_scalar(s, y, 2.0, None, ALU.add))
                step(vec.reciprocal(s2, s))
                step(vec.tensor_tensor(s, y, s2, ALU.mult))
                step(vec.tensor_tensor(s2, s, s, ALU.mult))
                step(vec.tensor_scalar(q, s2, 1.0 / 17.0, None, ALU.mult))
                for n in (15, 13, 11, 9, 7, 5, 3):
                    step(vec.scalar_tensor_tensor(q, q, 1.0 / n, s2, ALU.add, ALU.mult))
                step(vec.scalar_tensor_tensor(q, q, 1.0, s, ALU.add, ALU.mult))
                step(vec.tensor_scalar(s, decay[:, :], 0.0, None, ALU.min))
                step(vec.scalar_tensor_tensor(log_gamma[:, :], q, -2.0, s, ALU.mult, ALU.add))
                f, b = log_gamma[:, 0:HEADS], log_gamma[:, HEADS:]
                for j, (g, by) in enumerate(((f, ramps[:, 0:1]), (b, ramps[:, 1:2]), (f, ramps[:, 2:3]),
                                             (b, ramps[:, 3:4]), (f, float(P)), (b, float(P)))):
                    ins = vec.tensor_scalar(zeta_arg[:, j, :], g, by, None, ALU.mult)
                ins.then_inc(exp_in, 1)
                dve.wait_ge(exp_out, 2)
                for j, s in enumerate((2, 0, 1, 3)):
                    step(vec.tensor_scalar(zeta_ctx[:, j, :], zeta[:, s, :], float(DK) ** -0.5, None, ALU.mult))

            def masks():
                dve.wait_ge(exp_out, 2 + 4 * HEADS)
                back = o_s[:, 0, 0:HEADS * P].rearrange("p (h n) -> p h n", h=HEADS)
                tri_f = tables[:, 2 * P:3 * P].unsqueeze(1).broadcast_to([P, HEADS, P])
                tri_b = tables[:, 3 * P:4 * P].unsqueeze(1).broadcast_to([P, HEADS, P])
                step(vec.tensor_tensor(mask[:, :, :], mask[:, :, :], tri_f, ALU.mult))
                step(vec.tensor_tensor(back, back, tri_b, ALU.mult))
                vec.tensor_tensor(mask[:, :, :], mask[:, :, :], back, ALU.add).then_inc(masks_made, 1)

            wait_full(dve, "mod")
            step(vec.tensor_tensor(mod[:, :, :].rearrange("p (j b) x -> p b j x", b=4),
                                   bank("mod").rearrange("p (b j x n) -> p b j x n", b=4, j=4, x=2)[:, :, :, :, 0],
                                   cols[:, 16:32].rearrange("p (j b) -> p b j", b=4).unsqueeze(3)
                                   .broadcast_to([P, 4, 4, 2]), ALU.add))
            vec.tensor_scalar(mod[:, 8:16, :], mod[:, 8:16, :], 1.0, None, ALU.add).then_inc(dve_drained, 1)

            def low_part(gi, half):
                use = (ORDER[gi], half)
                wait_raw(dve, use)
                wait_weights_free(dve, gi, half)
                dve.wait_ge(hi_made, parts(gi, half))
                vec.tensor_tensor(w_lo[:, half, :], raw_slot(use), w_hi[:, half, :], ALU.subtract).then_inc(lo_made, 1)

            def split(hi, lo, src):
                step(vec.tensor_copy(hi, src))
                return vec.tensor_tensor(lo, src, hi, ALU.subtract)

            for k in range(K):
                dve.wait_ge(h_made, 2 * k + 2)
                vec.tensor_copy(h_hi[:, k, :], h_tmp[:, k % 2, 0:SEQ])
                step(vec.tensor_copy(hc_hi[:, k, :], h_tmp[:, k % 2, SEQ:]))
                vec.tensor_tensor(h_lo[:, k, :], h_tmp[:, k % 2, 0:SEQ], h_hi[:, k, :], ALU.subtract)
                vec.tensor_tensor(hc_lo[:, k, :], h_tmp[:, k % 2, SEQ:], hc_hi[:, k, :], ALU.subtract)\
                    .then_inc(h_split, 1)
                cut = slice((k % 4) * 512, (k % 4 + 1) * 512)
                if k % 4 == 0:
                    wait_raw(dve, (ORDER[0], k // 4))
                dve.wait_ge(hi_made, k + 1)
                vec.tensor_tensor(w_lo[:, k // 4, cut], raw_slot((ORDER[0], k // 4))[:, cut], w_hi[:, k // 4, cut],
                                  ALU.subtract).then_inc(lo_made, 1)

            def add_bias(g):
                dve.wait_ge(b_row_landed, 16)
                for j in range(T + (C if g in WITH_CTX else 0)):
                    if g == "k":
                        dst = k_s[:, j, :] if j < T else kc_s[:, j - T, :]
                        row = b_row[:, OFF_K:OFF_K + QW]
                    elif g == "q":
                        dst, row = q_s[:, j, :], b_row[:, OFF_Q:OFF_Q + QW]
                    else:
                        lo = 512 * int(g[1])
                        dst = v_s[:, j, lo:lo + 512] if j < T else vc_s[:, j - T, lo:lo + 512]
                        row = b_row[:, OFF_V + lo:OFF_V + lo + 512]
                    wait_full(dve, (g, j))
                    vec.tensor_tensor(dst, bank((g, j)), row, ALU.add).then_inc(dve_drained, 1)

            def turn(z, which, g):
                dve.wait_ge(rope_landed, 16)
                wait_drained(dve, last_job(g))
                for i in range(T):
                    if i:
                        dve.wait_ge(roped, (0 if g == "k" else T) + i)
                    c = rope[:, i, 2 * which, :].unsqueeze(1).broadcast_to([P, HEADS, DK])
                    s = rope[:, i, 2 * which + 1, :].rearrange("p (a j n) -> p j a n", a=2, j=2)
                    x = z[:, i, :].rearrange("p (h d) -> p h d", h=HEADS)
                    halves = z[:, i, :].rearrange("p (h a j n) -> p j h a n", h=HEADS, a=2, j=2)
                    turned = rope_tmp[:, 1, :].rearrange("p (h a j n) -> p j h a n", h=HEADS, a=2, j=2)
                    for j in range(2):
                        vec.tensor_tensor(turned[:, j], halves[:, 1 - j],
                                          s[:, j].unsqueeze(1).broadcast_to([P, HEADS, 2, DK // 4]), ALU.mult)
                    step(vec.tensor_tensor(rope_tmp[:, 0, :].rearrange("p (h d) -> p h d", h=HEADS), x, c, ALU.mult))
                    vec.tensor_tensor(z[:, i, :], rope_tmp[:, 0, :], rope_tmp[:, 1, :], ALU.add).then_inc(roped, 1)

            def weigh_keys(h):
                cut = slice(h * DK, (h + 1) * DK)
                if h == 0:
                    dve.wait_ge(roped, 2 * T)
                    dve.wait_ge(masks_made, 1)
                vec.tensor_scalar(kz[:, h % 2, 0], k_s[:, 0:T - 1, cut], zeta[:, 0, h:h + 1], None, ALU.mult)
                vec.tensor_scalar(kz[:, h % 2, 1], k_s[:, 1:T, cut], zeta[:, 1, h:h + 1], None, ALU.mult)
                for s in range(2):
                    for i in range(C):
                        ins = vec.tensor_scalar(kcz[:, h % 2, s, i], kc_s[:, i, cut],
                                                zeta_ctx[:, 2 * s + i, h:h + 1], None, ALU.mult)
                ins.then_inc(kz_made, 1)

            def retention():
                def weigh_queries(h):
                    wait_drained(dve, ("qT", h))
                    q = q_t[:, h % 2, :].rearrange("p (n l) -> p n l", n=T)
                    for s, dst in ((0, q_f), (1, q_b)):
                        ins = vec.tensor_tensor(dst[:, h % 2, :].rearrange("p (n l) -> p n l", n=T), q,
                                                xi[:, s, h, :].unsqueeze(1).broadcast_to([P, T, P]), ALU.mult)
                    ins.then_inc(q_made, 1)

                def states(h):
                    wait_drained(dve, ("kv0", h))
                    for j in range(T - 1):
                        if j:
                            wait_drained(dve, ("kv", h, j - 1))
                        wait_full(dve, ("kv", h, j))
                        for s in range(2):
                            ins = vec.scalar_tensor_tensor(
                                state[:, s, j + 1, :], state[:, s, j, :], zeta[:, 4 + s, h:h + 1],
                                bank(("kv", h, j))[:, s * DV:(s + 1) * DV], ALU.mult, ALU.add)
                        ins.then_inc(dve_drained, 1)
                    wait_full(dve, ("sc", h))
                    vec.tensor_tensor(sm[:, h % 2, :].rearrange("p (n l) -> p n l", n=T),
                                      bank(("sc", h)).rearrange("p (n l) -> p n l", n=T),
                                      mask[:, h, :].unsqueeze(1).broadcast_to([P, T, P]), ALU.mult)\
                        .then_inc(dve_drained, 1)

                weigh_queries(0)
                states(0)
                low_part(number_of["g0"], 1)
                for h in range(1, HEADS):
                    weigh_keys(h)
                    weigh_queries(h)
                    states(h)

            def o_moments_made():
                wait_drained(dve, ("o", HEADS - 1, 1))
                for i in range(T):
                    for h in range(HEADS):
                        ins = vec.bn_stats(o_stats[:, i * HEADS + h, :], o_s[:, i, h * DV:(h + 1) * DV])
                step(ins)
                for n in range(T * HEADS):
                    ins = vec.bn_aggr(o_moments[:, n, :], o_stats[:, n, :])
                ins.then_inc(var_ready, 1)

            def o_normalised():
                groups_of_var[0] += 1
                dve.wait_ge(rstd_ready, groups_of_var[0])
                for i in range(T):
                    for h in range(HEADS):
                        n = i * HEADS + h
                        o = o_s[:, i, h * DV:(h + 1) * DV]
                        ins = vec.tensor_scalar(o, o, o_moments[:, n, 0:1], o_rstd[:, n:n + 1],
                                                ALU.subtract, ALU.mult)
                ins.then_inc(o_normed, 1)

            def gated_retention(c):
                if c >= 2:
                    dve.wait_ge(ret_made, c - 1)
                wait_full(dve, ("oT", c))
                vec.tensor_scalar(prod[:, c % 2, :], bank(("oT", c)), cols[:, 64 + c:65 + c], cols[:, 72 + c:73 + c],
                                  ALU.mult, ALU.add).then_inc(dve_drained, 1)
                wait_drained(dve, ("oT", c))
                wait_drained(dve, (f"g{c // 4}", c % 4))
                step(vec.tensor_tensor(prod[:, c % 2, :], prod[:, c % 2, :], g_t[:, c, :], ALU.mult))
                split(r_hi[:, c, :], r_lo[:, c, :], prod[:, c % 2, :]).then_inc(ret_made, 1)

            def row_chunks(first, n):
                for m in range(first, first + n):
                    k, side = m % K, m // K
                    acc = mod_rows[:, 2 * D * side:2 * D * (side + 1)]
                    if m == 0:
                        dve.wait_ge(rows_started, 16)
                    else:
                        dve.wait_ge(rows_summed, m)
                    wait_raw(dve, ("row", m))
                    vec.scalar_tensor_tensor(acc, raw_slot(("row", m)), cols[:, k:k + 1], acc,
                                             ALU.mult, ALU.add).then_inc(rows_summed, 1)

            def gate_retention(half):
                for j in range(4):
                    wait_drained(dve, (f"ga{half}", j))
                    wait_drained(dve, (f"pa{half}", j))
                    c = 4 * half + j
                    vec.tensor_tensor(ya[:, c, :], ya[:, c, :], gate_s[:, c % 2, :], ALU.mult).then_inc(gated, 1)

            def vs_biased(half):
                dve.wait_ge(vs_rows_landed, 48)
                for i in range(T):
                    wait_full(dve, (f"vs{half}", i))
                    vec.tensor_tensor(vs_s[:, i, half * 512:(half + 1) * 512], bank((f"vs{half}", i)),
                                      vs_rows[:, 0, half * 512:(half + 1) * 512], ALU.add).then_inc(dve_drained, 1)

            def vs_normalised():
                for i in range(T + 1):
                    if i < T:
                        dve.wait_ge(gelu_done, T + i + 1)
                        moments_of(vs_s[:, i, :], v_stats[:, i, :, :], v_moments[:, i, :])
                    if i >= 1:
                        v = vs_s[:, i - 1, :]
                        step(normalise(v, v, v_moments[:, i - 1, :], v_rstd[:, i - 1:i]))
                        vec.tensor_tensor(v, v, vs_rows[:, 1, :], ALU.mult).then_inc(vs_scaled, 1)

            def gated_spatial(c):
                if c == 0:
                    dve.wait_ge(sgu_b_landed, 16)
                if c >= 2:
                    dve.wait_ge(sgu_made, c - 1)
                wait_full(dve, ("sp", c))
                vec.tensor_tensor(prod[:, c % 2, :].rearrange("p (n l) -> p n l", n=T),
                                  bank(("sp", c)).rearrange("p (n l) -> p n l", n=T),
                                  sgu_b[:, c // 2, :].unsqueeze(1).broadcast_to([P, T, P]), ALU.add)\
                    .then_inc(dve_drained, 1)
                wait_drained(dve, ("sp", c))
                wait_drained(dve, (f"u{c // 4}", c % 4))
                step(vec.tensor_tensor(prod[:, c % 2, :], prod[:, c % 2, :], u_t[:, c % 4, :], ALU.mult))
                split(s_hi[:, c, :], s_lo[:, c, :], prod[:, c % 2, :]).then_inc(sgu_made, 1)

            def mixed(half):
                for j in range(4):
                    c = 4 * half + j
                    if c >= 2:
                        dve.wait_ge(y_made, c - 1)
                    wait_drained(dve, (f"gb{half}", j))
                    wait_drained(dve, (f"pb{half}", j))
                    step(vec.tensor_tensor(prod[:, c % 2, :], pb_s[:, j, :], gate_s[:, c % 2, :], ALU.mult))
                    step(vec.tensor_tensor(prod[:, c % 2, :], prod[:, c % 2, :], ya[:, c, :], ALU.add))
                    vec.tensor_copy(y_hi[:, c, :], prod[:, c % 2, :]).then_inc(gated, 1)
                    dve.wait_ge(gated, K + c + 1)
                    vec.tensor_tensor(y_lo[:, c, :], prod[:, c % 2, :], y_hi[:, c, :], ALU.subtract).then_inc(y_made, 1)

            def residual():
                dve.wait_ge(b_o_landed, 16)
                wait_drained(dve, ("row", 7))
                step(vec.tensor_tensor(b_o[:, :], b_o[:, :], mod_rows[:, 0:D], ALU.mult))
                dve.wait_ge(xa_landed, 16)
                for i in range(T):
                    ins = vec.scalar_tensor_tensor(xa[:, i, :], xa[:, i, :], ALPHA, b_o[:, :], ALU.mult, ALU.add)
                step(ins)

            def mixed_out(g, i):
                half = int(g[-1])
                cut = slice(half * 512, (half + 1) * 512)
                wait_full(dve, (g, i))
                vec.tensor_tensor(ln_tmp[:, i % 2, cut], bank((g, i)), mod_rows[:, cut], ALU.mult)\
                    .then_inc(dve_drained, 1)
                wait_drained(dve, (g, i))
                step(vec.tensor_tensor(xa[:, i, cut], xa[:, i, cut], ln_tmp[:, i % 2, cut], ALU.add))

            def ln_stats(n, src):
                moments_of(src, l_stats[:, n, :, :], l_moments[:, n, :])

            def ln_bias(n):
                groups_of_var[0] += 1
                dve.wait_ge(rstd_ready, groups_of_var[0])
                vec.scalar_tensor_tensor(l_nmr[:, n:n + 1], l_moments[:, n, 0:1], -1.0, l_rstd[:, n:n + 1],
                                         ALU.mult, ALU.mult).then_inc(nmr_made, 1)

            def ln1_scaled(i):
                dve.wait_ge(ln1_landed, 32)
                dve.wait_ge(normed, LATE.index(2 * i) + 1)
                vec.tensor_tensor(xa[:, i, :], xa[:, i, :], ln_rows[:, 0, :], ALU.mult).then_inc(w_applied, 1)

            def h2_scaled(i):
                dve.wait_ge(normed, LATE.index(2 * i + 1) + 1)
                ins = vec.tensor_tensor(h2[:, i, :], h2[:, i, :], mod_rows[:, 2 * D:3 * D], ALU.mult)
                if i < T - 1:
                    ins.then_inc(sc_applied, 1)
                else:
                    step(ins)
                    vec.tensor_tensor(h2[:, i, :], h2[:, i, :], mod_rows[:, D:2 * D], ALU.add).then_inc(h2_last, 1)

            for gi, g in enumerate(ORDER):
                if g == "g0":
                    o_moments_made()
                if gi + 1 < len(ORDER):
                    low_part(gi + 1, 0)
                if g == "g0":
                    o_normalised()
                if g == "v1":
                    weigh_keys(0)
                if g in ("k", "q", "v0", "v1"):
                    add_bias(g)
                if g in ("vs0", "vs1"):
                    vs_biased(int(g[-1]))
                if g in ("ga0", "ga1"):
                    gate_retention(int(g[-1]))
                if g in ("gb0", "gb1"):
                    mixed(int(g[-1]))
                if g == "wo0":
                    residual()
                if gi + 1 < len(ORDER) and g != "v1":
                    low_part(gi + 1, 1)
                if g == "k":
                    log_gammas()
                    turn(k_s, 1, "k")
                if g == "q":
                    turn(q_s, 0, "q")
                    masks()
                if g == "v1":
                    retention()
                if g in ("g0", "g1"):
                    for c in range(4 * int(g[1]), 4 * int(g[1]) + 4):
                        gated_retention(c)
                if g in ROW_CHUNKS_AFTER:
                    row_chunks(4 * list(ROW_CHUNKS_AFTER).index(g), 4)
                if g == "vs1":
                    vs_normalised()
                if g in ("u0", "u1"):
                    for c in range(4 * int(g[1]), 4 * int(g[1]) + 4):
                        gated_spatial(c)
                if g == "wo0":
                    for i in range(T):
                        mixed_out(g, i)
            for i in range(T + 2):
                if i < T:
                    mixed_out("wo1", i)
                    ln_stats(2 * i, xa[:, i, :])
                if 1 <= i <= T:
                    dve.wait_ge(b_applied, i)
                    ln_stats(2 * i - 1, xa[:, i - 1, :])
                if i < T:
                    ln_bias(2 * i)
                if i >= 2:
                    h2_scaled(i - 2)
                if 1 <= i <= T:
                    ln_bias(2 * i - 1)
                if i < T:
                    ln1_scaled(i)

            wait_full(dve, "lgT")
            lg = bank("lgT")[:, 0:T * NE].rearrange("p (t e) -> p t e", t=T)
            step(vec.tensor_reduce(soft[:, 0, :], lg, AX_X, ALU.max))
            vec.tensor_tensor(logits[:, :, :], lg, soft[:, 0, :].unsqueeze(2).broadcast_to([P, T, NE]),
                              ALU.subtract).then_inc(dve_drained, 1)
            dve.wait_ge(exp_out, 3 + 4 * HEADS)
            step(vec.tensor_reduce(soft[:, 1, :], logits[:, :, :], AX_X, ALU.add))
            step(vec.reciprocal(soft[:, 2, :], soft[:, 1, :]))
            vec.tensor_tensor(aff[:, :, :], logits[:, :, :], soft[:, 2, :].unsqueeze(2).broadcast_to([P, T, NE]),
                              ALU.mult).then_inc(exp_in, 1)
            wait_drained(dve, "affT")
            for n in range(CAP // 8):
                src = aff_t if n == 0 else work
                step(vec.max(top8[:, n % 2, :], src[:, :]))
                step(vec.match_replace(work[:, :], top8[:, n % 2, :], src[:, :], -1.0))
            step(vec.tensor_scalar(picked[:, :], work[:, :], 0.0, None, ALU.is_lt))
            step(vec.tensor_tensor_scan(rank[:, :], picked[:, :], picked[:, :], 0.0, ALU.add, ALU.max))
            step(vec.tensor_tensor(rank[:, :], rank[:, :], picked[:, :], ALU.mult))
            vec.tensor_scalar(rank[:, :], rank[:, :], -1.0, None, ALU.add).then_inc(exp_in, 1)
            wait_full(dve, "posT")
            vec.tensor_copy(pos_t[:, :, :], bank("posT")[:, 0:T * NE].rearrange("p (t e) -> p t e", t=T))\
                .then_inc(dve_drained, 1)
            wait_drained(dve, "posT")
            dve.wait_ge(acc_scaled, T)

            def expert_outputs(i, pair):
                full, own, act_side = 32 * i + 16 * pair, 32 * i + 16 * pair, 22 * i + 11 * pair
                vec.tensor_tensor(sel[:, :, :].rearrange("p t (j s) -> p t j s", j=2),
                                  slot_ramp.unsqueeze(1).unsqueeze(1).broadcast_to([P, T, 2, CAP]),
                                  pos_t[:, :, bass.ds(4 * i + 2 * pair, 2)].unsqueeze(3).broadcast_to([P, T, 2, CAP]),
                                  ALU.is_equal).then_inc(pair_dve, 1)
                dve.wait_ge(pair_full, full + 6)
                dve.wait_ge(pair_dve, own + 1)
                vec.tensor_copy(gate_col[0:CAP, :], ps[0:CAP, 7, 0:1])
                vec.tensor_copy(gate_col[CAP:P, :], ps[CAP:P, 7, 1:2]).then_inc(pair_dve, 1)
                dve.wait_ge(chunk_used, 24 * i + (12 * pair + 8))
                for h in range(2):
                    dve.wait_ge(pair_act, act_side + (6 + h))
                    vec.tensor_tensor(hid[:, h * 512:(h + 1) * 512], ps[:, 2 + h, :],
                                      silu_s[:, h * 512:(h + 1) * 512], ALU.mult).then_inc(pair_dve, 1)
                dve.wait_ge(chunk_used, 24 * i + (12 * pair + 12))
                dve.wait_ge(pair_dve, own + 4)
                for h in range(2):
                    cut = slice(h * 512, (h + 1) * 512)
                    vec.scalar_tensor_tensor(ye[:, cut], ps[:, 6 + h, :], gate_col[:, 0:1],
                                             mod_rows[:, 3 * D + h * 512:3 * D + (h + 1) * 512],
                                             ALU.mult, ALU.mult).then_inc(pair_dve, 1)
                for h in range(2):
                    cut = slice(h * 512, (h + 1) * 512)
                    dve.wait_ge(pair_act, act_side + (10 + h))
                    vec.tensor_tensor(ye_lo[:, cut], ye[:, cut], ye_hi[:, cut], ALU.subtract).then_inc(pair_dve, 1)

            def add_outputs(i, pair, s):
                dst = xa[:, s // 2, (s % 2) * 512:(s % 2 + 1) * 512]
                dve.wait_ge(pair_full, 32 * i + (16 * pair + 9 + s))
                vec.tensor_tensor(dst, dst, ps[:, SCATTER_BANK[s], :], ALU.add).then_inc(pair_dve, 1)

            def two_pairs(i, last):
                for pair in range(2):
                    expert_outputs(i, pair)
                    if not (last and pair):
                        for s in range(8):
                            add_outputs(i, pair, s)

            with dve.Fori(0, PAIRS // 2 - 1) as i:
                two_pairs(i, False)
            two_pairs(PAIRS // 2 - 1, True)

            def ln2_scaled(i):
                dve.wait_ge(normed, 2 * T + i + 1)
                return vec.tensor_tensor(xa[:, i, :], xa[:, i, :], ln2_rows[:, 0, :], ALU.mult)

            dve.wait_ge(ln2_landed, 32)
            for i in range(T + 1):
                if i < T:
                    for h in range(2):
                        add_outputs(PAIRS // 2 - 1, 1, 2 * i + h)
                    dve.wait_ge(pair_dve, 16 * (PAIRS - 1) + 8 + 2 * (i + 1))
                if i >= 1:
                    ln_bias(2 * T + i - 1)
                if i < T:
                    ln_stats(2 * T + i, xa[:, i, :])
                if 1 <= i < T:
                    ln2_scaled(i - 1).then_inc(w_applied, 1)
            step(ln2_scaled(T - 1))
            vec.tensor_tensor(xa[:, T - 1, :], xa[:, T - 1, :], ln2_rows[:, 1, :], ALU.add).then_inc(last_ready, 1)

        @block.tensor
        def _(pe):
            mm, flip = nc.tensor.matmul, nc.tensor.transpose

            def begin(job):
                if J.before(job):
                    wait_drained(pe, J.before(job))

            pe.wait_ge(ident_landed, 16)
            pe.wait_ge(vec_landed, 16 * len(VECTORS))
            pe.wait_ge(silu_c, 1)
            begin("cols")
            flip(bank("cols")[:, 0:80], vec_rows[:, :], ident[0:80, 0:80]).then_inc(bank_full, 1)
            wait_drained(pe, "cols")
            pe.wait_ge(c_spread, 1)
            def modulation(k):
                wait_raw(pe, ("ada", k))
                w = raw_slot(("ada", k))
                for c in range(4):
                    ins = mm(bank("modrow")[32 * c:32 * c + 32, :], c_wide[:, k, :], w[:, c * 512:(c + 1) * 512],
                             start=(k == 0), stop=(k == K - 1))
                ins.then_inc(ada_used, 1)

            pe.wait_ge(set_up, 2)
            for i in range(T + C):
                pe.wait_ge(x_normed, i + 1)
                for h in range(2):
                    begin(("xT", i, h))
                    for k in range(4):
                        ins = flip(bank(("xT", i, h))[:, k * P:(k + 1) * P],
                                   x_in[:, i, (4 * h + k) * P:(4 * h + k + 1) * P], ident)
                    ins.then_inc(bank_full, 1)
                modulation(i)
            for k in range(T + C, K):
                modulation(k)
            pe.wait_ge(ada_used, K)
            pe.nop().then_inc(bank_full, 1)
            begin("mod")
            wait_drained(pe, "modrow")
            for c in range(4):
                ins = flip(bank("mod")[:, c * P:(c + 1) * P], mod_t[:, c * P:(c + 1) * P], ident)
            ins.then_inc(bank_full, 1)

            def product(job, a_hi, a_lo, b_hi, b_lo, first, last):
                o = bank(job)
                mm(o, a_hi, b_hi, start=first, stop=False)
                mm(o, a_hi, b_lo, start=False, stop=False)
                return mm(o, a_lo, b_hi, start=False, stop=last)

            def group(g, hi, lo, ready=None):
                gi = number_of[g]
                jobs = [(g, j) for j in range(4 + (C if g in WITH_CTX else 0))]
                for half in range(2):
                    if gi:
                        pe.wait_ge(lo_made, parts(gi, half))
                    for kk in range(4):
                        k = 4 * half + kk
                        if gi == 0:
                            pe.wait_ge(lo_made, k + 1)
                        if ready:
                            ready(k)
                        w = [x[:, half, kk * 512:(kk + 1) * 512] for x in (w_hi, w_lo)]
                        for j, job in enumerate(jobs):
                            if k == 0:
                                begin(job)
                            cut = slice(j * P, (j + 1) * P)
                            if g in WIDE:
                                ins = product(job, w[0][:, cut], w[1][:, cut], hi[:, k, :], lo[:, k, :],
                                              k == 0, k == K - 1)
                            elif j < T:
                                ins = product(job, hi[:, k, cut], lo[:, k, cut], w[0], w[1], k == 0, k == K - 1)
                            else:
                                cut = slice((j - T) * P, (j - T + 1) * P)
                                ins = product(job, hc_hi[:, k, cut], hc_lo[:, k, cut], w[0], w[1],
                                              k == 0, k == K - 1)
                            if k == K - 1:
                                ins.then_inc(bank_full, 1)
                        if k == 3:
                            ins.then_inc(half_used, 1)

            def h_ready(k):
                pe.wait_ge(h_split, k + 1)

            group("k", h_hi, h_lo, h_ready)
            group("q", h_hi, h_lo)
            group("v0", h_hi, h_lo)
            group("v1", h_hi, h_lo)

            pe.wait_ge(roped, 2 * T)

            def turn_heads(h):
                for name, src in (("qT", q_s), ("kT", k_s)):
                    begin((name, h))
                    for n in range(T):
                        ins = flip(bank((name, h))[:, n * P:(n + 1) * P], src[:, n, h * DK:(h + 1) * DK], ident)
                    ins.then_inc(bank_full, 1)

            def states(h):
                pe.wait_ge(kz_made, h + 1)
                wait_drained(pe, ("v1", T + C - 1))
                cut = slice(h * DV, (h + 1) * DV)
                begin(("kv0", h))
                for s in range(2):
                    for i in range(C):
                        ins = mm(bank(("kv0", h))[:, s * DV:(s + 1) * DV], kcz[:, h % 2, s, i, :], vc_s[:, i, cut],
                                 start=(i == 0), stop=(i == C - 1))
                ins.then_inc(bank_full, 1)
                for j in range(T - 1):
                    begin(("kv", h, j))
                    o = bank(("kv", h, j))
                    mm(o[:, 0:DV], kz[:, h % 2, 0, j, :], v_s[:, j, cut], start=True, stop=True)
                    mm(o[:, DV:2 * DV], kz[:, h % 2, 1, T - 2 - j, :], v_s[:, T - 1 - j, cut],
                       start=True, stop=True).then_inc(bank_full, 1)
                begin(("sc", h))
                wait_drained(pe, ("kT", h))
                for n in range(T):
                    cut = slice(n * P, (n + 1) * P)
                    ins = mm(bank(("sc", h))[:, cut], k_t[:, h % 2, cut], q_t[:, h % 2, cut], start=True, stop=True)
                ins.then_inc(bank_full, 1)

            def outputs(h):
                wait_drained(pe, ("sc", h))
                pe.wait_ge(q_made, h + 1)
                for j in range(2):
                    begin(("o", h, j))
                    for n in (2 * j, 2 * j + 1):
                        o = bank(("o", h, j))[:, (n % 2) * DV:(n % 2 + 1) * DV]
                        cut = slice(n * P, (n + 1) * P)
                        mm(o, sm[:, h % 2, cut], v_s[:, n, h * DV:(h + 1) * DV], start=True, stop=False)
                        mm(o, q_f[:, h % 2, cut], state[:, 0, n, :], start=False, stop=False)
                        ins = mm(o, q_b[:, h % 2, cut], state[:, 1, T - 1 - n, :], start=False, stop=True)
                    ins.then_inc(bank_full, 1)

            turn_heads(0)
            states(0)
            for h in range(HEADS):
                if h + 1 < HEADS:
                    turn_heads(h + 1)
                outputs(h)
                if h + 1 < HEADS:
                    states(h + 1)

            for half in range(2):
                group(f"g{half}", h_hi, h_lo)
                pe.wait_ge(o_normed, 1)
                for c in range(4 * half, 4 * half + 4):
                    begin(("oT", c))
                    for n in range(T):
                        ins = flip(bank(("oT", c))[:, n * P:(n + 1) * P], o_s[:, n, c * P:(c + 1) * P], ident)
                    ins.then_inc(bank_full, 1)

            def ret_ready(k):
                pe.wait_ge(ret_made, k + 1)

            group("pa0", r_hi, r_lo, ret_ready)
            group("ga0", h_hi, h_lo)
            group("pa1", r_hi, r_lo)
            group("ga1", h_hi, h_lo)
            begin("swT")
            pe.wait_ge(sw_landed, 16)
            for g in range(GROUPS):
                ins = flip(bank("swT")[:, g * P:(g + 1) * P], sw_in[:, g, :], ident)
            ins.then_inc(bank_full, 1)
            group("vs0", h_hi, h_lo)
            group("vs1", h_hi, h_lo)
            for half in range(2):
                group(f"u{half}", h_hi, h_lo)
                if half == 0:
                    pe.wait_ge(vs_made, T)
                    wait_drained(pe, "swT")
                for c in range(4 * half, 4 * half + 4):
                    begin(("sp", c))
                    for n in range(T):
                        ins = mm(bank(("sp", c))[:, n * P:(n + 1) * P], vs_s[:, n, c * P:(c + 1) * P],
                                 sw_t[:, c // 2, :], start=True, stop=True)
                    ins.then_inc(bank_full, 1)

            def sgu_ready(k):
                pe.wait_ge(sgu_made, k + 1)

            pe.wait_ge(rows_summed, 2 * K)
            for i in range(8):
                begin(("row", i))
                mm(bank(("row", i)), ones[:, :], mod_rows[:, i * 512:(i + 1) * 512], start=True, stop=True)\
                    .then_inc(bank_full, 1)
            group("pb0", s_hi, s_lo, sgu_ready)
            group("gb0", h_hi, h_lo)
            group("pb1", s_hi, s_lo)
            group("gb1", h_hi, h_lo)

            def y_ready(k):
                pe.wait_ge(y_made, k + 1)

            def out_tile(g, j, half):
                cut = slice(j * P, (j + 1) * P)
                for k in range(4 * half, 4 * half + 4):
                    w = [x[:, half, (k % 4) * 512:(k % 4 + 1) * 512] for x in (w_hi, w_lo)]
                    ins = product((g, j), y_hi[:, k, cut], y_lo[:, k, cut], w[0], w[1], k == 0, k == K - 1)
                return ins

            pe.wait_ge(lo_made, parts(number_of["wo0"], 0))
            for k in range(4):
                y_ready(k)
            for j in range(T):
                begin(("wo0", j))
                ins = out_tile("wo0", j, 0)
            ins.then_inc(half_used, 1)
            pe.wait_ge(lo_made, parts(number_of["wo0"], 1))
            for k in range(4, K):
                y_ready(k)
            for j in range(T):
                out_tile("wo0", j, 1).then_inc(bank_full, 1)
            pe.wait_ge(lo_made, parts(number_of["wo1"], 0))
            for j, half in ((0, 0), (1, 0), (0, 1), (1, 1), (2, 0), (2, 1), (3, 0), (3, 1)):
                if half == 0:
                    begin(("wo1", j))
                    out_tile("wo1", j, 0)
                else:
                    pe.wait_ge(lo_made, parts(number_of["wo1"], 1))
                    out_tile("wo1", j, 1).then_inc(bank_full, 1)

            pe.wait_ge(router_landed, 32)
            for i in range(T):
                if i < T - 1:
                    pe.wait_ge(h2_made, i + 1)
                else:
                    pe.wait_ge(h2_last, 1)
                for h in range(2):
                    begin(("h2T", i, h))
                    for k in range(4):
                        ins = flip(bank(("h2T", i, h))[:, k * P:(k + 1) * P],
                                   h2[:, i, (4 * h + k) * P:(4 * h + k + 1) * P], ident)
                    ins.then_inc(bank_full, 1)
                begin(("lg", i))
                for k in range(K):
                    if k % 4 == 0:
                        wait_drained(pe, ("h2T", i, k // 4))
                    ins = mm(bank(("lg", i))[0:NE, 0:P], w_router[:, k, :], h2_t[:, i % 2, k, :],
                             start=(k == 0), stop=(k == K - 1))
                ins.then_inc(bank_full, 1)
            begin("lgT")
            for i in range(T):
                wait_drained(pe, ("lg", i))
                ins = flip(bank("lgT")[:, i * NE:(i + 1) * NE], logits_t[:, i * P:(i + 1) * P], ident[0:NE, 0:NE])
            ins.then_inc(bank_full, 1)
            begin("affT")
            pe.wait_ge(exp_in, 3)
            for i in range(T):
                ins = mm(bank("affT")[0:NE, i * P:(i + 1) * P], aff[:, i, :], ident, start=True, stop=True)
            ins.then_inc(bank_full, 1)
            begin("posT")
            pe.wait_ge(exp_in, 4)
            for i in range(T):
                ins = flip(bank("posT")[:, i * NE:(i + 1) * NE], rank[:, i * P:(i + 1) * P], ident[0:NE, 0:NE])
            ins.then_inc(bank_full, 1)

            pe.wait_ge(h2_split, T)
            def pair_of_experts(i, pair):
                dve_side, act_side = 32 * i + 16 * pair, 22 * i + 11 * pair
                pe.wait_ge(pair_dve, dve_side + 1)
                for h in range(2):
                    for n in range(T):
                        for part in (h2_hi, h2_lo):
                            ins = mm(ps[:, 4 + h, :], sel[:, n, :], part[:, n, h * 512:(h + 1) * 512],
                                     start=(n == 0 and part is h2_hi), stop=(n == T - 1 and part is h2_lo))
                    ins.then_inc(pair_full, 1)
                for h in range(2):
                    pe.wait_ge(pair_act, act_side + (1 + h))
                    for k in range(4 * h, 4 * h + 4):
                        ins = flip(ps[:, 2 + h, (k % 4) * P:(k % 4 + 1) * P], x_rows[:, k * P:(k + 1) * P], ident)
                    ins.then_inc(pair_full, 1)
                for n in range(T):
                    ins = flip(ps[:, 6, n * P:(n + 1) * P], sel[:, n, :].bitcast(F32), ident)
                ins.then_inc(pair_full, 1)
                for n in range(T):
                    ins = mm(ps[:, 7, 0:2], sel[:, n, :].bitcast(F32), aff[:, n, bass.ds(4 * i + 2 * pair, 2)],
                             start=(n == 0), stop=(n == T - 1))
                ins.then_inc(pair_full, 1)

                def expert_product(first_chunk, first_bank, operand, ready):
                    for c in range(first_chunk, first_chunk + 4):
                        g = CHUNKS * pair + c
                        pe.wait_ge(ring_landed[g % RING], 96 * i + 32 * (g // RING + 1))
                        for kk in range(2):
                            k = 2 * (c % 4) + kk
                            if k % 4 == 0:
                                pe.wait_ge(pair_act, act_side + ready[k // 4])
                            for f in range(2):
                                for e in range(2):
                                    ins = mm(ps[e * CAP:(e + 1) * CAP, first_bank + f, :],
                                             operand[:, k, e * CAP:(e + 1) * CAP],
                                             ring[g % RING][:, e, kk, f * 512:(f + 1) * 512],
                                             start=(k == 0), stop=(k == K - 1))
                        ins.then_inc(chunk_used, 1)

                expert_product(0, 0, xs, (3, 4))
                expert_product(4, 2, xs, (3, 4))
                for h in range(2):
                    pe.wait_ge(pair_dve, dve_side + (3 + h))
                    for k in range(4 * h, 4 * h + 4):
                        ins = flip(ps[:, 4 + h, (k % 4) * P:(k % 4 + 1) * P], hid[:, k * P:(k + 1) * P], ident)
                    ins.then_inc(pair_full, 1)
                expert_product(8, 6, hid_t, (8, 9))
                pe.wait_ge(pair_dve, dve_side + 7)
                for s in range(8):
                    n, h = s // 2, s % 2
                    if s == 1:
                        pe.wait_ge(pair_dve, dve_side + 8)
                    if s >= 6:
                        pe.wait_ge(pair_dve, dve_side + (9 + s - 6))
                    mm(ps[:, SCATTER_BANK[s], :], sel_t[:, n * P:(n + 1) * P], ye_hi[:, h * 512:(h + 1) * 512],
                       start=True, stop=False)
                    mm(ps[:, SCATTER_BANK[s], :], sel_t[:, n * P:(n + 1) * P], ye_lo[:, h * 512:(h + 1) * 512],
                       start=False, stop=True).then_inc(pair_full, 1)

            with pe.Fori(0, PAIRS // 2) as i:
                pair_of_experts(i, 0)
                pair_of_experts(i, 1)


_INS = ["x", "c", "ctx", "c_ctx", "w_ada", "b_ada", "w_in", "b_in", "ret_decay_f", "ret_decay_b", "ret_gn_w",
        "ret_gn_b", "sgu_ln_w", "sgu_ln_b", "sgu_w", "sgu_b", "w_pa", "w_pb", "w_o", "b_o", "ln1_w", "ln1_b",
        "w_router", "b_router", "w_gate", "w_up", "w_down", "ln2_w", "ln2_b"]


def kernel(**inputs):
    import concourse.bacc as _bacc
    from concourse.bass_utils import run_bass_kernel_spmd as _run

    nc = _bacc.Bacc("TRN2", target_bir_lowering=False, num_devices=1)
    arrays, tensors = {}, {}
    for name in _INS:
        a = np.ascontiguousarray(inputs[name])
        arrays[f"in_{name}"] = a
        tensors[name] = nc.dram_tensor(f"in_{name}", a.shape, mybir.dt.from_np(a.dtype), kind="ExternalInput").ap()
    seq, d_model = inputs["x"].shape[1:]
    shape_table, rope = shape_constants(seq, 128)
    for name, a in (("shape_table", shape_table), ("rope", rope)):
        arrays[f"in_{name}"] = a
        tensors[name] = nc.dram_tensor(f"in_{name}", a.shape, F32, kind="ExternalInput").ap()
    tensors["out"] = nc.dram_tensor("out_0", (1, seq, d_model), F32, kind="ExternalOutput").ap()
    mixer_and_experts(nc, tensors)
    r = _run(nc, [arrays], core_ids=[0])
    return r.results[0]["out_0"]
```

```python
from contextlib import ExitStack

import numpy as np

import concourse.bass as bass
from concourse import mybir

F32 = mybir.dt.float32
F32R = mybir.dt.float32r
ALU = mybir.AluOpType
ACT = mybir.ActivationFunctionType
AX_X = mybir.AxisListType.X

P = 128
BANKS = 8
BANK = 512
GRID_W = 64
ROPE_THETA = 10000.0
LN_EPS = 1e-6
DEPTH = 1
ALPHA = (2.0 * DEPTH) ** 0.25
CAPACITY_FACTOR = 2

SBUF_START = 16512
AREA = 7680


def place(kib):
    return SBUF_START + AREA + int((kib - 8) * 1024)


class Jobs:

    def __init__(self):
        self.number, self.bank, self.drainer = {}, {}, {}
        self.names, self.turn = [], 0

    def add(self, name, drainer, bank=None, banks=BANKS):
        if bank is None:
            bank = self.turn % banks
            self.turn = bank + 1
        self.number[name] = len(self.names) + 1
        self.bank[name], self.drainer[name] = bank, drainer
        self.names.append(name)

    def full(self, name):
        return self.number[name]

    def drained(self, name):
        return sum(self.drainer[n] == self.drainer[name] for n in self.names[:self.number[name]])

    def before(self, name):
        found = [n for n in self.names[:self.number[name] - 1] if self.bank[n] == self.bank[name]]
        return found[-1] if found else None


def shape_constants(seq, heads_dim):
    m, l = np.meshgrid(np.arange(P), np.arange(P), indexing="ij")
    p = np.arange(P)[:, None]
    ramps = np.concatenate([P - 1 - p, p, 2 * P - 1 - p, P + p], 1)
    slots = np.broadcast_to(np.arange(64)[None], (P, 64))
    table = np.concatenate([np.eye(P), slots, ramps, np.maximum(l - m, 0), np.maximum(m - l, 0),
                            l >= m, m >= l, l + 1, P - l], 1).astype(np.float32)
    t = np.arange(seq)
    n_freq = heads_dim // 4
    inv = (np.float32(ROPE_THETA) ** (-np.arange(n_freq, dtype=np.float32) / np.float32(n_freq))).astype(np.float32)
    pos = np.stack([t // GRID_W, t % GRID_W], -1).astype(np.float32)
    ang = (pos[..., None] * inv).astype(np.float32)
    cos, sin = np.cos(ang).astype(np.float32), np.sin(ang).astype(np.float32)
    both = np.stack([cos, cos], 2).reshape(seq, heads_dim)
    turn = np.stack([-sin, sin], 2).reshape(seq, heads_dim)
    scale = np.float32(heads_dim ** -0.5)
    rope = np.stack([both, turn, both * scale, turn * scale], 1).astype(np.float32)
    return table, np.ascontiguousarray(rope.reshape(seq // P, P, 4, heads_dim))


def mixer_and_experts(nc, t):
    x_d, ctx_d, out_d = t["x"], t["ctx"], t["out"]
    _, SEQ, D = x_d.shape
    CTX = ctx_d.shape[1]
    HEADS = t["ret_decay_f"].shape[1]
    D_IN = t["w_in"].shape[2]
    NE = t["w_gate"].shape[1]
    FE = t["w_gate"].shape[3]
    DK = 128
    DV = t["ret_gn_w"].shape[1] // HEADS
    QW, VW = HEADS * DK, HEADS * DV
    GROUPS = t["sgu_w"].shape[1]
    T, C, K = SEQ // P, CTX // P, D // P
    CAP = CAPACITY_FACTOR * SEQ // NE
    PAIRS = NE // 2
    CHUNKS = 3 * K
    assert (T, C, K, CAP, QW, VW, FE) == (4, 2, 8, 64, 512, 1024, 1024)
    OFF_Q, OFF_K, OFF_V = 0, QW, 2 * QW
    OFF_G = OFF_V + VW
    OFF_U, OFF_VS, OFF_GA, OFF_GB = OFF_G + VW, OFF_G + VW + D, OFF_G + VW + 2 * D, OFF_G + VW + 3 * D
    assert OFF_GB + D == D_IN

    w_in, w_pa, w_pb, w_o = (t[n][0] for n in ("w_in", "w_pa", "w_pb", "w_o"))
    GROUP_LIST = [("k", w_in, OFF_K), ("q", w_in, OFF_Q), ("v0", w_in, OFF_V), ("v1", w_in, OFF_V + 512),
                  ("g0", w_in, OFF_G), ("g1", w_in, OFF_G + 512),
                  ("pa0", w_pa, 0), ("ga0", w_in, OFF_GA), ("pa1", w_pa, 512), ("ga1", w_in, OFF_GA + 512),
                  ("vs0", w_in, OFF_VS), ("vs1", w_in, OFF_VS + 512), ("u0", w_in, OFF_U), ("u1", w_in, OFF_U + 512),
                  ("pb0", w_pb, 0), ("gb0", w_in, OFF_GB), ("pb1", w_pb, 512), ("gb1", w_in, OFF_GB + 512),
                  ("wo0", w_o, 0), ("wo1", w_o, 512)]
    ORDER = [g[0] for g in GROUP_LIST]
    number_of = {name: i for i, name in enumerate(ORDER)}
    WITH_CTX = {"k", "v0", "v1"}
    WIDE = {"g0", "g1", "pa0", "ga0", "pa1", "ga1", "u0", "u1", "pb0", "gb0", "pb1", "gb1"}
    ROW_CHUNKS_AFTER = {"pa0": 4, "ga0": 4, "pa1": 4, "ga1": 4}

    ROW_JOBS = (0, 1, 6, 7)

    J = Jobs()
    J.add("cols", "act", banks=7)
    for i in range(T + C):
        for h in range(2):
            J.add(("xT", i, h), "act", banks=7)
    J.add("modrow", "act", bank=7)
    J.add("mod", "dve", bank=6)
    J.turn = 0

    def group_jobs(g):
        who = "act" if g.rstrip("01") in ("g", "pa", "ga", "pb", "gb", "u") else "dve"
        for j in range(4):
            J.add((g, j), who)
        if g in WITH_CTX:
            for j in range(C):
                J.add((g, T + j), who)

    def state_jobs(h):
        J.add(("kv0", h), "act")
        for j in range(T - 1):
            J.add(("kv", h, j), "dve")
        J.add(("sc", h), "dve")

    for g in ("k", "q", "v0", "v1"):
        group_jobs(g)
    J.add(("qT", 0), "act")
    J.add(("kT", 0), "act")
    state_jobs(0)
    for h in range(HEADS):
        if h + 1 < HEADS:
            J.add(("qT", h + 1), "act")
            J.add(("kT", h + 1), "act")
        J.add(("o", h, 0), "act")
        J.add(("o", h, 1), "act")
        if h + 1 < HEADS:
            state_jobs(h + 1)
    for half in range(2):
        group_jobs(f"g{half}")
        for c in range(4 * half, 4 * half + 4):
            J.add(("oT", c), "dve")
    for g in ("pa0", "ga0", "pa1", "ga1"):
        group_jobs(g)
    J.add("swT", "act")
    group_jobs("vs0")
    group_jobs("vs1")
    for half in range(2):
        group_jobs(f"u{half}")
        for c in range(4 * half, 4 * half + 4):
            J.add(("sp", c), "dve")
    for i in ROW_JOBS:
        J.add(("row", i), "act")
    J.add("cols2", "act", bank=J.bank["row", 0])
    for j in range(4):
        J.add(("pb0", j), "act", bank=(J.bank["row", 0] + 1 + j) % BANKS)
    J.turn = J.bank["pb0", 3] + 1
    for g in ("gb0", "pb1", "gb1", "wo0", "wo1"):
        group_jobs(g)
    early = [J.bank["wo0", j] for j in range(T)]
    for i in range(T):
        for h in range(2):
            J.add(("h2T", i, h), "dve" if h and i >= T - 2 else "act", bank=early[h])
        J.add(("lg", i), "act", bank=early[2 + i % 2])
    J.add("lgT", "dve", bank=early[0])
    J.add("affT", "dve")
    J.add("posT", "dve")

    RAW = 3
    raw_uses = [("ada", k) for k in range(K)]
    rows_left = [("row", n) for n in range(2 * K)]
    raw_uses += [(ORDER[0], 0), (ORDER[0], 1)]
    for gi, g in enumerate(ORDER):
        if gi + 1 < len(ORDER):
            raw_uses += [(ORDER[gi + 1], 0), (ORDER[gi + 1], 1)]
        for _ in range(ROW_CHUNKS_AFTER.get(g, 0)):
            raw_uses.append(rows_left.pop(0))
    assert not rows_left
    raw_at = {u: n for n, u in enumerate(raw_uses)}

    with ExitStack() as ctx:
        small_at = [SBUF_START]

        def small(name, shape, dt=F32):
            n = int(np.prod(shape[1:])) * 4
            a = nc.alloc_sbuf_tensor_at(name, list(shape), dt, offset=small_at[0])
            small_at[0] += (n + 31) // 32 * 32
            assert small_at[0] <= SBUF_START + AREA
            return a

        def at(kib, name, shape, dt=F32):
            return nc.alloc_sbuf_tensor_at(name, list(shape), dt, offset=place(kib))

        def sem(name):
            return ctx.enter_context(nc.semaphore(name))

        ps = ctx.enter_context(nc.psum_tensor("banks", [P, BANKS, BANK], F32))

        ident_slots = small("ident_slots", [P, P + 64 + 4])
        ident = ident_slots[:, 0:P]
        slot_ramp = ident_slots[:, P:P + 64]
        ramps = ident_slots[:, P + 64:P + 68]
        ones = small("ones", [P, P])
        vec_rows = small("vec_rows", [80, P])
        cols = small("cols", [P, 80])
        c_wide = small("c_wide", [P, K, 32])
        mod = small("mod", [P, 16, 2])
        mod2 = small("mod2", [P, 16])
        stats = small("stats", [P, 6, 2, 6])
        moments = small("moments", [P, 6, 2])
        rstd = small("rstd", [P, 6])
        o_stats = small("o_stats", [P, T * HEADS, 6])
        o_moments = small("o_moments", [P, T * HEADS, 2])
        o_rstd = small("o_rstd", [P, T * HEADS])
        v_stats = small("v_stats", [P, T, 2, 6])
        v_moments = small("v_moments", [P, T, 2])
        v_rstd = small("v_rstd", [P, T])
        l_stats = small("l_stats", [P, 3 * T, 2, 6])
        l_moments = small("l_moments", [P, 3 * T, 2])
        l_rstd = small("l_rstd", [P, 3 * T])
        l_nmr = small("l_nmr", [P, 3 * T])
        powers = small("powers", [P, 16])
        decay = small("decay", [P, 2 * HEADS])
        decay_w = small("decay_w", [P, 4, 2 * HEADS])
        log_gamma = small("log_gamma", [P, 2 * HEADS])
        zeta_arg = small("zeta_arg", [P, 6, HEADS])
        zeta = small("zeta", [P, 6, HEADS])
        zeta_ctx = small("zeta_ctx", [P, 4, HEADS])
        b_router = small("b_router_s", [P, 1])
        logits = small("logits", [P, T, NE])
        aff = small("aff", [P, T, NE])
        soft = small("soft", [P, 3, T])
        pos_t = small("pos_t", [P, T, NE])
        top8 = small("top8", [NE, 2, 8])
        gate_col = small("gate_col", [P, 1])

        raw = at(8, "raw", [P, RAW, 2048])
        w_hi = at(32, "w_hi", [P, 2, 2048], F32R)
        w_lo = at(48, "w_lo", [P, 2, 2048], F32R)
        h_hi = at(64, "h_hi", [P, K, SEQ], F32R)
        h_lo = at(80, "h_lo", [P, K, SEQ], F32R)
        x_in = at(96, "x_in", [P, T + C, D])
        xn_t = at(120, "xn_t", [P, K, SEQ + CTX])
        mod_t = at(188, "mod_t", [P, 512])
        hc_hi = at(144, "hc_hi", [P, K, CTX], F32R)
        hc_lo = at(152, "hc_lo", [P, K, CTX], F32R)
        h_tmp = at(182, "h_tmp", [P, 2, SEQ + CTX])
        tables = at(202, "tables", [P, 6 * P])
        k_s = at(96, "k_s", [P, T, QW])
        q_s = at(104, "q_s", [P, T, QW])
        v_s = at(112, "v_s", [P, T, VW])
        kc_s = at(128, "kc_s", [P, C, QW])
        vc_s = at(132, "vc_s", [P, C, VW])
        b_row = at(160, "b_row", [P, 2 * QW + VW])
        rope = at(168, "rope", [P, T, 4, DK])
        rope_tmp = at(176, "rope_tmp", [P, 2, QW])
        mask = at(180, "mask", [P, HEADS, P])
        q_t = at(152, "q_t", [P, 2, SEQ])
        k_t = at(156, "k_t", [P, 2, SEQ])
        q_f = at(160, "q_f", [P, 2, SEQ])
        q_b = at(164, "q_b", [P, 2, SEQ])
        kz = at(168, "kz", [P, 2, 2, T - 1, DK])
        kcz = at(140, "kcz", [P, 2, 2, C, DK])
        sm = at(176, "sm", [P, 2, SEQ])
        state = at(144, "state", [P, 2, T, DV])
        xi = at(182, "xi_rows", [P, 2, HEADS, P])
        o_s = at(186, "o_s", [P, T, VW])
        g_t = at(96, "g_t", [P, K, SEQ])
        r_hi = at(112, "r_hi", [P, K, SEQ], F32R)
        r_lo = at(128, "r_lo", [P, K, SEQ], F32R)
        prod = at(144, "prod", [P, 2, SEQ])
        ya = at(96, "ya", [P, K, SEQ])
        gate_s = at(148, "gate_s", [P, 2, SEQ])
        mod_rows = at(152, "mod_rows", [P, 4 * D])
        gate_b = at(156, "gate_b", [P, 4, SEQ])
        vs_s = at(168, "vs_s", [P, T, D])
        vs_rows = at(184, "vs_rows", [P, 3, D])
        u_t = at(196, "u_t", [P, 4, SEQ])
        sw_in = at(204, "sw_in", [P, GROUPS, P])
        sw_t = at(206, "sw_t", [P, GROUPS, P])
        sgu_b = at(184, "sgu_b_s", [P, GROUPS, P])
        s_hi = at(112, "s_hi", [P, K, SEQ], F32R)
        s_lo = at(128, "s_lo", [P, K, SEQ], F32R)
        pb_s = at(200, "pb_s", [P, 4, SEQ])
        y_hi = at(168, "y_hi", [P, K, SEQ], F32R)
        y_lo = at(184, "y_lo", [P, K, SEQ], F32R)
        xa = at(96, "xa", [P, T, D])
        b_o = at(112, "b_o_s", [P, D])
        ln_rows = at(200, "ln_rows", [P, 2, D])
        h2 = at(112, "h2", [P, T, D])
        h2_hi = at(8, "h2_hi", [P, T, D], F32R)
        h2_lo = at(32, "h2_lo", [P, T, D], F32R)
        h2_t = at(24, "h2_t", [P, 2, K, P])
        logits_t = at(32, "logits_t", [P, SEQ])
        work = at(26, "work", [NE, SEQ])
        picked = at(28, "picked", [NE, SEQ])
        rank = at(30, "rank", [NE, SEQ])
        w_router = at(160, "w_router_s", [P, K, 32])
        RING = 16
        ring_at = (64, 80, 128, 48, 168, 184, 144, 112)
        ring = [at(ring_at[n // 2] + 8 * (n % 2), f"ring{n}", [P, 2, FE]) for n in range(RING)]
        sel = at(24, "sel", [P, T, P], F32R)
        sel_t = at(26, "sel_t", [P, SEQ], F32R)
        silu_s = at(28, "silu_s", [P, FE])
        ye = at(28, "ye", [P, D])
        x_rows = at(160, "x_rows", [P, D])
        hid = at(160, "hid", [P, FE])
        ye_hi = at(160, "ye_hi", [P, D], F32R)
        xs = at(200, "xs", [P, K, P])
        hid_t = at(200, "hid_t", [P, K, P])
        ye_lo = at(200, "ye_lo", [P, D], F32R)
        ln2_rows = at(64, "ln2_rows", [P, 2, D])

        raw_landed = [sem(f"raw_landed{i}") for i in range(RAW)]
        ring_landed = [sem(f"ring_landed{i}") for i in range(RING)]
        vec_landed = sem("vec_landed")
        x_landed = [sem(f"x_landed{i}") for i in range(T + C)]
        ident_landed = sem("ident_landed")
        tables_landed = sem("tables_landed")
        decay_landed = sem("decay_landed")
        b_row_landed = sem("b_row_landed")
        rope_landed = sem("rope_landed")
        router_landed = sem("router_landed")
        router_zeroed = sem("router_zeroed")
        vs_rows_landed = sem("vs_rows_landed")
        sw_landed = sem("sw_landed")
        sgu_b_landed = sem("sgu_b_landed")
        rows_zeroed = sem("rows_zeroed")
        rows_started = sem("rows_started")
        xa_landed = sem("xa_landed")
        b_o_landed = sem("b_o_landed")
        ln1_landed = sem("ln1_landed")
        ln2_landed = sem("ln2_landed")
        stored = sem("stored")
        bank_full = sem("bank_full")
        act_drained = sem("act_drained")
        dve_drained = sem("dve_drained")
        set_up = sem("set_up")
        silu_c = sem("silu_c")
        var_ready = sem("var_ready")
        rstd_ready = sem("rstd_ready")
        eps_added = sem("eps_added")
        x_normed = sem("x_normed")
        rounds_near_end = sem("rounds_near_end")
        pb_gated = sem("pb_gated")
        raw_scaled = sem("raw_scaled")
        ada_used = sem("ada_used")
        c_spread = sem("c_spread")
        h_made = sem("h_made")
        h_split = sem("h_split")
        hi_made = sem("hi_made")
        lo_made = sem("lo_made")
        half_used = sem("half_used")
        exp_in = sem("exp_in")
        exp_out = sem("exp_out")
        masks_made = sem("masks_made")
        roped = sem("roped")
        kz_made = sem("kz_made")
        q_made = sem("q_made")
        o_normed = sem("o_normed")
        ret_made = sem("ret_made")
        gated = sem("gated")
        gelu_done = sem("gelu_done")
        vs_scaled = sem("vs_scaled")
        vs_made = sem("vs_made")
        sgu_made = sem("sgu_made")
        y_made = sem("y_made")
        rows_summed = sem("rows_summed")
        w_applied = sem("w_applied")
        b_applied = sem("b_applied")
        nmr_made = sem("nmr_made")
        normed = sem("normed")
        h2_copied = sem("h2_copied")
        acc_scaled = sem("acc_scaled")
        h2_split = sem("h2_split")
        out_ready = sem("out_ready")
        last_ready = sem("last_ready")
        dve_step = sem("dve_step")
        chunk_used = sem("chunk_used")
        pair_full = sem("pair_full")
        pair_act = sem("pair_act")
        pair_dve = sem("pair_dve")

        LATE = [0] + [n for i in range(1, T) for n in (2 * i, 2 * i - 1)] + [2 * T - 1] + [2 * T + i for i in range(T)]
        SCATTER_BANK = (0, 1, 2, 3, 4, 5, 0, 1)
        LAST_BANK = (0, 1, 2, 3, 4, 5, 6, 7)

        def last_sum(i):
            return ps[:, LAST_BANK[2 * i]:LAST_BANK[2 * i] + 2, :].rearrange("p b n -> p (b n)")

        drained_by = {"act": act_drained, "dve": dve_drained}

        def wait_full(eng, job):
            eng.wait_ge(bank_full, J.full(job))

        def wait_drained(eng, job):
            eng.wait_ge(drained_by[J.drainer[job]], J.drained(job))

        def bank(job):
            return ps[:, J.bank[job], :]

        def last_job(g):
            return (g, T + C - 1) if g in WITH_CTX else (g, 3)

        def wait_raw(eng, use):
            n = raw_at[use]
            eng.wait_ge(raw_landed[n % RAW], 16 * (n // RAW + 1))

        def raw_slot(use):
            return raw[:, raw_at[use] % RAW, :]

        OUT_USES = [(g, half) for g in ("wo0", "wo1") for half in range(2)]

        def wait_scaled(eng, use):
            if use in OUT_USES:
                eng.wait_ge(raw_scaled, OUT_USES.index(use) + 1)

        def parts(gi, half):
            return 4 * (half + 1) if gi == 0 else K + 2 * (gi - 1) + half + 1

        def wait_weights_free(eng, gi, half):
            if gi == 0:
                return
            if half == 0:
                eng.wait_ge(half_used, gi)
            else:
                wait_full(eng, last_job(ORDER[gi - 1]))

        vec = nc.vector
        act_e = nc.scalar
        pool_e = nc.gpsimd
        block = ctx.enter_context(nc.Block())

        expert_w = [t[n].rearrange("l e (k p) f -> (l k) p e f", p=P) for n in ("w_gate", "w_up", "w_down")]

        VECTORS = ((0, t["c"][0]), (8, t["c_ctx"]), (16, t["b_ada"][0, 0:2 * D]), (32, t["b_in"][0, OFF_G:OFF_G + 2 * D]),
                   (48, t["b_in"][0, OFF_GA:OFF_GA + 2 * D]), (64, t["ret_gn_w"][0]), (72, t["ret_gn_b"][0]))

        def load_vectors(eng, vectors):
            for first, v in vectors:
                n = v.shape[0] // P
                eng.dma_start(vec_rows[first:first + n, :], v.rearrange("(r n) -> r n", n=P)).then_inc(vec_landed, 16)

        @block.sync
        def _(sp):
            w_ada = t["w_ada"][0]
            sp.dma_start(ident_slots[:, :], t["shape_table"][:, 0:P + 68]).then_inc(ident_landed, 16)
            load_vectors(sp, VECTORS[:4])
            for n, use in enumerate(raw_uses):
                kind, part = use
                if n >= RAW:
                    was, was_part = raw_uses[n - RAW]
                    if was == "ada":
                        sp.wait_ge(ada_used, was_part + 1)
                    elif was == "row":
                        sp.wait_ge(rows_summed, was_part + 1)
                    else:
                        sp.wait_ge(lo_made, parts(number_of[was], was_part))
                slot = raw_slot(use)
                if kind == "ada":
                    sp.dma_start(slot, w_ada[part * P:(part + 1) * P, 0:2 * D]).then_inc(raw_landed[n % RAW], 16)
                elif kind == "row":
                    k, side = part % K, part // K
                    sp.dma_start(slot, w_ada[k * P:(k + 1) * P, 2 * D * (1 + side):2 * D * (2 + side)])\
                        .then_inc(raw_landed[n % RAW], 16)
                else:
                    _, w, first = GROUP_LIST[number_of[kind]]
                    rows = w[part * 4 * P:(part + 1) * 4 * P, first:first + 512].rearrange("(k p) n -> p k n", p=P)
                    sp.dma_start(slot.rearrange("p (k n) -> p k n", k=4), rows).then_inc(raw_landed[n % RAW], 16)

            def load_chunk(i, c):
                pair, m = c // CHUNKS, c % CHUNKS
                sp.dma_start(ring[c % RING][:, :, :], expert_w[m // K][m % K][:, bass.ds(4 * i + 2 * pair, 2), :])\
                    .then_inc(ring_landed[c % RING], 16)

            for c in range(2 * CHUNKS):
                if c == 0:
                    wait_full(sp, ("gb1", 3))
                    sp.wait_ge(ln1_landed, 32)
                if c == 2:
                    sp.wait_ge(router_landed, 32)
                if c == 6:
                    wait_full(sp, ("wo1", 3))
                if c == 12:
                    sp.wait_ge(var_ready, T + C + 1 + T + LATE.index(2 * T - 2) + 1)
                if c == 14:
                    sp.wait_ge(h2_split, T)
                    wait_full(sp, ("h2T", T - 1, 1))
                if c >= RING:
                    sp.wait_ge(chunk_used, c - RING + 1)
                load_chunk(0, c)
            with sp.Fori(1, PAIRS // 2) as i:
                for c in range(2 * CHUNKS):
                    sp.wait_ge(chunk_used, 2 * CHUNKS * i + (c - RING + 1))
                    load_chunk(i, c)
            sp.wait_ge(chunk_used, CHUNKS * PAIRS - RING + 1)
            for j, row in enumerate((t["ln2_w"][0], t["ln2_b"][0])):
                sp.dma_start(ln2_rows[:, j, :], row.partition_broadcast(P)).then_inc(ln2_landed, 16)
            out_v = out_d.rearrange("b (t p) d -> (b t) p d", p=P)
            for i in range(T - 1):
                sp.wait_ge(out_ready, i + 1)
                sp.dma_start(out_v[i], xa[:, i, :]).then_inc(stored, 16)
            for h in range(2):
                cut = slice(h * 512, (h + 1) * 512)
                sp.wait_ge(last_ready, h + 1)
                sp.dma_start(out_v[T - 1][:, cut], xa[:, T - 1, cut]).then_inc(stored, 16)
            sp.wait_ge(stored, 16 * (T + 1))

        @block.gpsimd
        def _(pool):
            pool_e.memset(ones[:, :], 1.0).then_inc(set_up, 1)
            pool_e.memset(powers[:, :], -0.5).then_inc(set_up, 1)
            pool.wait_ge(set_up, 2)
            turn = [0]

            def rsqrt(out, var, n):
                turn[0] += 1
                pool.wait_ge(var_ready, turn[0])
                pool_e.tensor_scalar(out, var, LN_EPS, None, ALU.add).then_inc(eps_added, 1)
                pool.wait_ge(eps_added, turn[0])
                pool_e.tensor_tensor(out, out, powers[:, 0:n], ALU.pow).then_inc(rstd_ready, 1)

            for i in range(T + C):
                rsqrt(rstd[:, i:i + 1], moments[:, i, 1:2], 1)
            pool.wait_ge(ada_used, K - 2)
            pool.dma_start(tables[:, :], t["shape_table"][:, P + 68:]).then_inc(tables_landed, 16)
            pool.dma_start(decay[:, 0:HEADS], t["ret_decay_f"][0].partition_broadcast(P)).then_inc(decay_landed, 16)
            pool.dma_start(decay[:, HEADS:], t["ret_decay_b"][0].partition_broadcast(P)).then_inc(decay_landed, 16)
            pool.dma_start(b_row[:, :], t["b_in"][0, 0:OFF_G].partition_broadcast(P)).then_inc(b_row_landed, 16)
            pool.dma_start(rope[:, :, :, :].rearrange("p t a d -> p t (a d)"),
                           t["rope"].rearrange("t p a d -> p t (a d)")).then_inc(rope_landed, 16)
            pool_e.memset(b_router[:, :], 0.0).then_inc(router_zeroed, 1)
            pool.wait_ge(router_zeroed, 1)
            pool.dma_start(b_router[0:NE, :], t["b_router"].rearrange("o e -> e o")).then_inc(router_landed, 16)
            rsqrt(o_rstd[:, :], o_moments[:, :, 1], T * HEADS)
            wait_full(pool, ("oT", 3))
            pool_e.memset(mod_rows[:, :], 0.0).then_inc(rows_zeroed, 1)
            pool.wait_ge(rows_zeroed, 1)
            pool.dma_start(mod_rows[0:1, :], t["b_ada"][:, 2 * D:6 * D]).then_inc(rows_started, 16)
            wait_full(pool, ("oT", 7))
            for j, row in enumerate((t["b_in"][0, OFF_VS:OFF_VS + D], t["sgu_ln_w"][0], t["sgu_ln_b"][0])):
                pool.dma_start(vs_rows[:, j, :], row.partition_broadcast(P)).then_inc(vs_rows_landed, 16)
            pool.dma_start(sw_in[:, :, :], t["sgu_w"][0].rearrange("g p q -> p g q")).then_inc(sw_landed, 16)
            pool.wait_ge(vs_rows_landed, 48)
            for i in range(T + 1):
                if i < T:
                    rsqrt(v_rstd[:, i:i + 1], v_moments[:, i, 1:2], 1)
                if i >= 1:
                    pool.wait_ge(vs_scaled, i)
                    pool_e.tensor_tensor(vs_s[:, i - 1, :], vs_s[:, i - 1, :], vs_rows[:, 2, :], ALU.add)\
                        .then_inc(vs_made, 1)
            pool.wait_ge(vs_made, T)
            pool.dma_start(sgu_b[:, :, :].rearrange("p g q -> p (g q)"),
                           t["sgu_b"][0].rearrange("g q -> (g q)").partition_broadcast(P)).then_inc(sgu_b_landed, 16)

            def scale_out_weights(use):
                wait_raw(pool, use)
                w = raw_slot(use).rearrange("p (k n) -> p k n", k=4)
                first = 512 * int(use[0][-1])
                g1 = mod_rows[:, first:first + 512].unsqueeze(1).broadcast_to([P, 4, 512])
                pool_e.tensor_tensor(w, w, g1, ALU.mult).then_inc(raw_scaled, 1)

            def gate_spatial(half):
                for j in range(4):
                    wait_drained(pool, (f"gb{half}", j))
                    wait_drained(pool, (f"pb{half}", j))
                    pool_e.tensor_tensor(pb_s[:, j, :], pb_s[:, j, :], gate_b[:, j, :], ALU.mult).then_inc(pb_gated, 1)

            gate_spatial(0)
            wait_full(pool, ("pb1", 3))
            pool.dma_start(b_o[:, :], t["b_o"][0].partition_broadcast(P)).then_inc(b_o_landed, 16)
            wait_drained(pool, ("row", 1))
            for use in OUT_USES[:3]:
                scale_out_weights(use)
            gate_spatial(1)
            pool.wait_ge(y_made, K)
            pool.dma_start(xa[:, :, :], x_d[0].rearrange("(t p) d -> p t d", p=P)).then_inc(xa_landed, 16)
            for j, row in enumerate((t["ln1_w"][0], t["ln1_b"][0])):
                pool.dma_start(ln_rows[:, j, :], row.partition_broadcast(P)).then_inc(ln1_landed, 16)

            scale_out_weights(OUT_USES[3])
            pool_e.memset(w_router[:, :, :], 0.0).then_inc(router_zeroed, 1)
            pool.wait_ge(router_zeroed, 2)
            pool.dma_start(w_router[:, :, 0:NE], t["w_router"][0].rearrange("(k p) e -> p k e", p=P)).then_inc(router_landed, 16)

            def ln1_rsqrt(i):
                rsqrt(l_rstd[:, 2 * i:2 * i + 1], l_moments[:, 2 * i, 1:2], 1)

            def h2_rsqrt(i):
                rsqrt(l_rstd[:, 2 * i + 1:2 * i + 2], l_moments[:, 2 * i + 1, 1:2], 1)

            def ln1_bias(i):
                pool.wait_ge(w_applied, i + 1)
                pool_e.tensor_tensor(xa[:, i, 512:], xa[:, i, 512:], ln_rows[:, 1, 512:], ALU.add).then_inc(b_applied, 1)

            pool.wait_ge(ln1_landed, 32)
            for i in range(T + 1):
                if i < T:
                    ln1_rsqrt(i)
                if i >= 1:
                    h2_rsqrt(i - 1)
                if i < T:
                    ln1_bias(i)
            wait_full(pool, ("wo1", 3))
            for i in range(T):
                pool.wait_ge(h2_copied, i + 1)
                pool_e.tensor_tensor(h2_lo[:, i, :], h2[:, i, :], h2_hi[:, i, :], ALU.subtract).then_inc(h2_split, 1)
            pool.wait_ge(ln2_landed, 32)
            for i in range(T):
                rsqrt(l_rstd[:, 2 * T + i:2 * T + i + 1], l_moments[:, 2 * T + i, 1:2], 1)
                if i >= 1:
                    pool.wait_ge(w_applied, T + i)
                    pool_e.tensor_tensor(xa[:, i - 1, :], xa[:, i - 1, :], ln2_rows[:, 1, :], ALU.add)\
                        .then_inc(out_ready, 1)

        @block.scalar
        def _(act):
            load_vectors(act, VECTORS[4:])
            for i in range(T + C):
                src = x_d[0, i * P:(i + 1) * P, :] if i < T else ctx_d[0, (i - T) * P:(i - T + 1) * P, :]
                act.dma_start(x_in[:, i, :], src).then_inc(x_landed[i], 16)

            act.wait_ge(vec_landed, 16 * len(VECTORS))
            act_e.activation(vec_rows[0:16, :], vec_rows[0:16, :], ACT.Silu).then_inc(silu_c, 1)
            wait_full(act, "cols")
            act_e.activation(cols[:, :], bank("cols")[:, 0:80], ACT.Copy).then_inc(act_drained, 1)
            for i in range(T + C):
                for h in range(2):
                    wait_full(act, ("xT", i, h))
                    act_e.activation(xn_t[:, 4 * h:4 * h + 4, i * P:(i + 1) * P],
                                     bank(("xT", i, h)).rearrange("p (k n) -> p k n", k=4), ACT.Copy)\
                        .then_inc(act_drained, 1)

            def high_part(gi, half):
                use = (ORDER[gi], half)
                wait_raw(act, use)
                wait_scaled(act, use)
                wait_weights_free(act, gi, half)
                act_e.activation(w_hi[:, half, :], raw_slot(use), ACT.Copy).then_inc(hi_made, 1)

            wait_full(act, "modrow")
            act_e.activation(mod_t[:, :], bank("modrow"), ACT.Copy).then_inc(act_drained, 1)
            wait_drained(act, "mod")
            wait_drained(act, ("xT", T + C - 1, 1))
            for k in range(K):
                if k >= 2:
                    act.wait_ge(h_split, k - 1)
                for j, (lo, hi) in enumerate(((0, SEQ), (SEQ, SEQ + CTX))):
                    act_e.activation(h_tmp[:, k % 2, lo:hi], xn_t[:, k, lo:hi], ACT.Identity,
                                     scale=mod[:, 8 + k, j:j + 1], bias=mod[:, k, j:j + 1]).then_inc(h_made, 1)
                if k % 4 == 0:
                    wait_raw(act, (ORDER[0], k // 4))
                cut = slice((k % 4) * 512, (k % 4 + 1) * 512)
                act_e.activation(w_hi[:, k // 4, cut], raw_slot((ORDER[0], k // 4))[:, cut], ACT.Copy).then_inc(hi_made, 1)

            def exps():
                act.wait_ge(exp_in, 1)
                act_e.activation(decay_w[:, 1, :], decay_w[:, 0, :], ACT.Exp).then_inc(exp_out, 1)
                act.wait_ge(exp_in, 2)
                act_e.activation(zeta[:, :, :], zeta_arg[:, :, :], ACT.Exp).then_inc(exp_out, 1)
                act.wait_ge(tables_landed, 16)
                for s in range(2):
                    for h in range(HEADS):
                        act_e.activation(xi[:, s, h, :], tables[:, (4 + s) * P:(5 + s) * P], ACT.Exp,
                                         scale=log_gamma[:, s * HEADS + h:s * HEADS + h + 1]).then_inc(exp_out, 1)
                for h in range(HEADS):
                    act_e.activation(mask[:, h, :], tables[:, 0:P], ACT.Exp,
                                     scale=log_gamma[:, h:h + 1]).then_inc(exp_out, 1)
                    act_e.activation(o_s[:, 0, h * P:(h + 1) * P], tables[:, P:2 * P], ACT.Exp,
                                     scale=log_gamma[:, HEADS + h:HEADS + h + 1]).then_inc(exp_out, 1)

            def retention():
                def transposed(h):
                    for name, dst in (("qT", q_t), ("kT", k_t)):
                        wait_full(act, (name, h))
                        act_e.activation(dst[:, h % 2, :], bank((name, h)), ACT.Copy).then_inc(act_drained, 1)

                def first_state(h):
                    wait_full(act, ("kv0", h))
                    act_e.activation(state[:, :, 0, :], bank(("kv0", h)).rearrange("p (s v) -> p s v", s=2),
                                     ACT.Copy).then_inc(act_drained, 1)

                transposed(0)
                first_state(0)
                high_part(number_of["g0"], 1)
                for h in range(HEADS):
                    if h + 1 < HEADS:
                        transposed(h + 1)
                    if h == 0:
                        act.wait_ge(masks_made, 1)
                    for j in range(2):
                        wait_full(act, ("o", h, j))
                        act_e.activation(o_s[:, 2 * j:2 * j + 2, h * DV:(h + 1) * DV],
                                         bank(("o", h, j)).rearrange("p (n v) -> p n v", n=2),
                                         ACT.Copy).then_inc(act_drained, 1)
                    if h + 1 < HEADS:
                        first_state(h + 1)

            def drain(g):
                half = int(g[-1])
                for j in range(4):
                    c = 4 * half + j
                    wait_full(act, (g, j))
                    if g in ("g0", "g1"):
                        act_e.activation(g_t[:, c, :], bank((g, j)), ACT.Silu,
                                         bias=cols[:, 32 + c:33 + c]).then_inc(act_drained, 1)
                    elif g in ("pa0", "pa1"):
                        act_e.activation(ya[:, c, :], bank((g, j)), ACT.Copy).then_inc(act_drained, 1)
                    elif g in ("pb0", "pb1"):
                        if half:
                            act.wait_ge(y_made, j + 1)
                        else:
                            act.wait_ge(sgu_made, K)
                        act_e.activation(pb_s[:, j, :], bank((g, j)), ACT.Copy).then_inc(act_drained, 1)
                    elif g in ("u0", "u1"):
                        if half:
                            act.wait_ge(sgu_made, c - 3)
                        act_e.activation(u_t[:, j, :], bank((g, j)), ACT.Gelu_apprx_tanh,
                                         bias=cols[:, 40 + c:41 + c]).then_inc(act_drained, 1)
                    elif g in ("ga0", "ga1"):
                        if c >= 2:
                            act.wait_ge(gated, c - 1)
                        act_e.activation(gate_s[:, c % 2, :], bank((g, j)), ACT.Sigmoid,
                                         bias=cols[:, 48 + c:49 + c]).then_inc(act_drained, 1)
                    else:
                        if half:
                            act.wait_ge(pb_gated, j + 1)
                        act_e.activation(gate_b[:, j, :], bank((g, j)), ACT.Sigmoid,
                                         bias=cols[:, 56 + c:57 + c]).then_inc(act_drained, 1)

            def gelu_vs(half):
                for i in range(T):
                    wait_drained(act, (f"vs{half}", i))
                    v = vs_s[:, i, half * 512:(half + 1) * 512]
                    act_e.activation(v, v, ACT.Gelu_apprx_tanh).then_inc(gelu_done, 1)

            for gi, g in enumerate(ORDER):
                if gi + 1 < len(ORDER):
                    high_part(gi + 1, 0)
                if J.drainer[(g, 0)] == "act":
                    drain(g)
                if gi + 1 < len(ORDER) and g != "v1":
                    high_part(gi + 1, 1)
                if g == "k":
                    exps()
                if g == "v1":
                    retention()
                if g == "ga1":
                    wait_full(act, "swT")
                    act_e.activation(sw_t[:, :, :], bank("swT").rearrange("p (g q) -> p g q", g=GROUPS),
                                     ACT.Copy).then_inc(act_drained, 1)
                if g in ("vs0", "vs1"):
                    gelu_vs(int(g[-1]))
                if g == "u1":
                    for i in ROW_JOBS:
                        wait_full(act, ("row", i))
                        act_e.activation(mod_rows[:, i * 512:(i + 1) * 512], bank(("row", i)), ACT.Copy)\
                            .then_inc(act_drained, 1)
                    wait_full(act, "cols2")
                    act_e.activation(mod2[:, 0:8], bank("cols2")[:, 0:8], ACT.Copy)
                    act_e.activation(mod2[:, 8:16], bank("cols2")[:, 8:16], ACT.Copy, bias=1.0)\
                        .then_inc(act_drained, 1)

            def normalise(n, dst, src):
                act.wait_ge(nmr_made, LATE.index(n) + 1)
                act_e.activation(dst, src, ACT.Identity, scale=l_rstd[:, n:n + 1], bias=l_nmr[:, n:n + 1])\
                    .then_inc(normed, 1)

            def modulated(dst, src, k):
                return act_e.activation(dst, src, ACT.Identity, scale=mod2[:, 8 + k:9 + k], bias=mod2[:, k:k + 1])

            def router_operand(i):
                for h in range(2 if i < T - 2 else 1):
                    wait_full(act, ("h2T", i, h))
                    for k in range(4):
                        ins = modulated(h2_t[:, i % 2, 4 * h + k, :], bank(("h2T", i, h))[:, k * P:(k + 1) * P], 4 * h + k)
                    ins.then_inc(act_drained, 1)

            def router_logits(i):
                wait_full(act, ("lg", i))
                act_e.activation(logits_t[:, i * P:(i + 1) * P], bank(("lg", i))[:, 0:P], ACT.Identity,
                                 bias=b_router[:, :]).then_inc(act_drained, 1)

            act.wait_ge(router_landed, 32)
            wait_drained(act, "cols2")
            act_e.activation(l_nmr[:, 3 * T - 1:3 * T], powers[:, 0:1], ACT.Exp)
            for i in range(T + 2):
                if i < T:
                    normalise(2 * i, xa[:, i, :], xa[:, i, :])
                if i >= 2:
                    router_operand(i - 2)
                if 1 <= i <= T:
                    normalise(2 * i - 1, h2[:, i - 1, :], xa[:, i - 1, :])
                if i >= 2:
                    router_logits(i - 2)
            act.wait_ge(exp_in, 3)
            act_e.activation(logits[:, :, :], logits[:, :, :], ACT.Exp).then_inc(exp_out, 1)
            for i in range(T):
                act_e.activation(h2_hi[:, i, :], h2[:, i, :], ACT.Copy).then_inc(h2_copied, 1)
            for i in range(T):
                act_e.activation(xa[:, i, :], xa[:, i, :], ACT.Copy, scale=ALPHA).then_inc(acc_scaled, 1)

            def pair_of_experts(i, pair, last=False):
                full, dve_side = 34 * i + 17 * pair, 34 * i + 17 * pair
                for h in range(2):
                    act.wait_ge(pair_full, full + (1 + h))
                    act_e.activation(x_rows[:, h * 512:(h + 1) * 512], ps[:, 4 + h, :], ACT.Copy)\
                        .then_inc(pair_act, 1)
                act.wait_ge(pair_full, full + 3)
                for k in range(4):
                    ins = modulated(xs[:, k, :], ps[:, 2, k * P:(k + 1) * P], k)
                    if k % 2:
                        ins.then_inc(pair_act, 1)
                act.wait_ge(pair_full, full + 5)
                act_e.activation(sel_t[:, :], ps[:, 6, :], ACT.Copy).then_inc(pair_act, 1)
                act.wait_ge(chunk_used, 48 * i + (24 * pair + 8))
                for h in range(2):
                    act_e.activation(silu_s[:, h * 512:(h + 1) * 512], ps[:, h, :], ACT.Silu).then_inc(pair_act, 1)
                for h in range(2):
                    act.wait_ge(pair_full, full + (7 + h))
                    act_e.activation(hid_t[:, 4 * h:4 * h + 4, :], ps[:, 4 + h, :].rearrange("p (k n) -> p k n", k=4),
                                     ACT.Copy).then_inc(pair_act, 1)
                for h in range(0 if last else 2):
                    act.wait_ge(pair_dve, dve_side + (6 + 2 * h))
                    act_e.activation(ye_hi[:, h * 512:(h + 1) * 512], ye[:, h * 512:(h + 1) * 512], ACT.Copy)\
                        .then_inc(pair_act, 1)

            with act.Fori(0, PAIRS // 2 - 1) as i:
                pair_of_experts(i, 0)
                pair_of_experts(i, 1)
            pair_of_experts(PAIRS // 2 - 1, 0)
            pair_of_experts(PAIRS // 2 - 1, 1, last=True)
            for i in range(T - 1):
                normalise(2 * T + i, xa[:, i, :], last_sum(i))
            for h in range(2):
                cut = slice(h * 512, (h + 1) * 512)
                normalise(3 * T - 1, xa[:, T - 1, cut], last_sum(T - 1)[:, cut])

        @block.vector
        def _(dve):
            steps = [0]

            def step(ins):
                steps[0] += 1
                ins.then_inc(dve_step, 1)
                dve.wait_ge(dve_step, steps[0])

            def moments_of(src, st, mo):
                n = src.shape[1] // 512 or 1
                for j in range(n):
                    ins = vec.bn_stats(st[:, j, :] if n > 1 else st, src[:, j * 512:(j + 1) * 512])
                step(ins)
                vec.bn_aggr(mo, st.rearrange("p a b -> p (a b)") if n > 1 else st).then_inc(var_ready, 1)

            groups_of_var = [0]

            def normalise(dst, src, mo, rs):
                groups_of_var[0] += 1
                dve.wait_ge(rstd_ready, groups_of_var[0])
                return vec.tensor_scalar(dst, src, mo[:, 0:1], rs, ALU.subtract, ALU.mult)

            wait_drained(dve, "cols")
            vec.tensor_copy(c_wide[:, :, :].rearrange("p k (x n) -> p k x n", x=2),
                            cols[:, 0:16].rearrange("p (x k) -> p k x", x=2).unsqueeze(3)
                            .broadcast_to([P, K, 2, 16])).then_inc(c_spread, 1)
            for i in range(T + C + 1):
                if i < T + C:
                    dve.wait_ge(x_landed[i], 16)
                    moments_of(x_in[:, i, :], stats[:, i, :, :], moments[:, i, :])
                if i >= 1:
                    normalise(x_in[:, i - 1, :], x_in[:, i - 1, :], moments[:, i - 1, :],
                              rstd[:, i - 1:i]).then_inc(x_normed, 1)

            def log_gammas():
                dve.wait_ge(decay_landed, 32)
                step(vec.tensor_scalar(decay_w[:, 2, :], decay[:, :], -1.0, None, ALU.mult))
                vec.tensor_tensor(decay_w[:, 0, :], decay[:, :], decay_w[:, 2, :], ALU.min).then_inc(exp_in, 1)
                dve.wait_ge(exp_out, 1)
                y, s, s2, q = (decay_w[:, j, :] for j in (1, 2, 3, 0))
                step(vec.tensor_scalar(s, y, 2.0, None, ALU.add))
                step(vec.reciprocal(s2, s))
                step(vec.tensor_tensor(s, y, s2, ALU.mult))
                step(vec.tensor_tensor(s2, s, s, ALU.mult))
                step(vec.tensor_scalar(q, s2, 1.0 / 17.0, None, ALU.mult))
                for n in (15, 13, 11, 9, 7, 5, 3):
                    step(vec.scalar_tensor_tensor(q, q, 1.0 / n, s2, ALU.add, ALU.mult))
                step(vec.scalar_tensor_tensor(q, q, 1.0, s, ALU.add, ALU.mult))
                step(vec.tensor_scalar(s, decay[:, :], 0.0, None, ALU.min))
                step(vec.scalar_tensor_tensor(log_gamma[:, :], q, -2.0, s, ALU.mult, ALU.add))
                f, b = log_gamma[:, 0:HEADS], log_gamma[:, HEADS:]
                for j, (g, by) in enumerate(((f, ramps[:, 0:1]), (b, ramps[:, 1:2]), (f, ramps[:, 2:3]),
                                             (b, ramps[:, 3:4]), (f, float(P)), (b, float(P)))):
                    ins = vec.tensor_scalar(zeta_arg[:, j, :], g, by, None, ALU.mult)
                ins.then_inc(exp_in, 1)
                dve.wait_ge(exp_out, 2)
                for j, s in enumerate((2, 0, 1, 3)):
                    step(vec.tensor_scalar(zeta_ctx[:, j, :], zeta[:, s, :], float(DK) ** -0.5, None, ALU.mult))

            def masks():
                dve.wait_ge(exp_out, 2 + 4 * HEADS)
                back = o_s[:, 0, 0:HEADS * P].rearrange("p (h n) -> p h n", h=HEADS)
                tri_f = tables[:, 2 * P:3 * P].unsqueeze(1).broadcast_to([P, HEADS, P])
                tri_b = tables[:, 3 * P:4 * P].unsqueeze(1).broadcast_to([P, HEADS, P])
                step(vec.tensor_tensor(mask[:, :, :], mask[:, :, :], tri_f, ALU.mult))
                step(vec.tensor_tensor(back, back, tri_b, ALU.mult))
                vec.tensor_tensor(mask[:, :, :], mask[:, :, :], back, ALU.add).then_inc(masks_made, 1)

            wait_full(dve, "mod")
            step(vec.tensor_tensor(mod[:, :, :].rearrange("p (j b) x -> p b j x", b=4),
                                   bank("mod").rearrange("p (b j x n) -> p b j x n", b=4, j=4, x=2)[:, :, :, :, 0],
                                   cols[:, 16:32].rearrange("p (j b) -> p b j", b=4).unsqueeze(3)
                                   .broadcast_to([P, 4, 4, 2]), ALU.add))
            vec.tensor_scalar(mod[:, 8:16, :], mod[:, 8:16, :], 1.0, None, ALU.add).then_inc(dve_drained, 1)

            def low_part(gi, half):
                use = (ORDER[gi], half)
                wait_raw(dve, use)
                wait_scaled(dve, use)
                wait_weights_free(dve, gi, half)
                dve.wait_ge(hi_made, parts(gi, half))
                vec.tensor_tensor(w_lo[:, half, :], raw_slot(use), w_hi[:, half, :], ALU.subtract).then_inc(lo_made, 1)

            def split(hi, lo, src):
                step(vec.tensor_copy(hi, src))
                return vec.tensor_tensor(lo, src, hi, ALU.subtract)

            for k in range(K):
                dve.wait_ge(h_made, 2 * k + 2)
                vec.tensor_copy(h_hi[:, k, :], h_tmp[:, k % 2, 0:SEQ])
                step(vec.tensor_copy(hc_hi[:, k, :], h_tmp[:, k % 2, SEQ:]))
                vec.tensor_tensor(h_lo[:, k, :], h_tmp[:, k % 2, 0:SEQ], h_hi[:, k, :], ALU.subtract)
                vec.tensor_tensor(hc_lo[:, k, :], h_tmp[:, k % 2, SEQ:], hc_hi[:, k, :], ALU.subtract)\
                    .then_inc(h_split, 1)
                cut = slice((k % 4) * 512, (k % 4 + 1) * 512)
                if k % 4 == 0:
                    wait_raw(dve, (ORDER[0], k // 4))
                dve.wait_ge(hi_made, k + 1)
                vec.tensor_tensor(w_lo[:, k // 4, cut], raw_slot((ORDER[0], k // 4))[:, cut], w_hi[:, k // 4, cut],
                                  ALU.subtract).then_inc(lo_made, 1)

            def add_bias(g):
                dve.wait_ge(b_row_landed, 16)
                for j in range(T + (C if g in WITH_CTX else 0)):
                    if g == "k":
                        dst = k_s[:, j, :] if j < T else kc_s[:, j - T, :]
                        row = b_row[:, OFF_K:OFF_K + QW]
                    elif g == "q":
                        dst, row = q_s[:, j, :], b_row[:, OFF_Q:OFF_Q + QW]
                    else:
                        lo = 512 * int(g[1])
                        dst = v_s[:, j, lo:lo + 512] if j < T else vc_s[:, j - T, lo:lo + 512]
                        row = b_row[:, OFF_V + lo:OFF_V + lo + 512]
                    wait_full(dve, (g, j))
                    vec.tensor_tensor(dst, bank((g, j)), row, ALU.add).then_inc(dve_drained, 1)

            def turn(z, which, g):
                dve.wait_ge(rope_landed, 16)
                wait_drained(dve, last_job(g))
                for i in range(T):
                    if i:
                        dve.wait_ge(roped, (0 if g == "k" else T) + i)
                    c = rope[:, i, 2 * which, :].unsqueeze(1).broadcast_to([P, HEADS, DK])
                    s = rope[:, i, 2 * which + 1, :].rearrange("p (a j n) -> p j a n", a=2, j=2)
                    x = z[:, i, :].rearrange("p (h d) -> p h d", h=HEADS)
                    halves = z[:, i, :].rearrange("p (h a j n) -> p j h a n", h=HEADS, a=2, j=2)
                    turned = rope_tmp[:, 1, :].rearrange("p (h a j n) -> p j h a n", h=HEADS, a=2, j=2)
                    for j in range(2):
                        vec.tensor_tensor(turned[:, j], halves[:, 1 - j],
                                          s[:, j].unsqueeze(1).broadcast_to([P, HEADS, 2, DK // 4]), ALU.mult)
                    step(vec.tensor_tensor(rope_tmp[:, 0, :].rearrange("p (h d) -> p h d", h=HEADS), x, c, ALU.mult))
                    vec.tensor_tensor(z[:, i, :], rope_tmp[:, 0, :], rope_tmp[:, 1, :], ALU.add).then_inc(roped, 1)

            def weigh_keys(h):
                cut = slice(h * DK, (h + 1) * DK)
                if h == 0:
                    dve.wait_ge(roped, 2 * T)
                    dve.wait_ge(masks_made, 1)
                vec.tensor_scalar(kz[:, h % 2, 0], k_s[:, 0:T - 1, cut], zeta[:, 0, h:h + 1], None, ALU.mult)
                vec.tensor_scalar(kz[:, h % 2, 1], k_s[:, 1:T, cut], zeta[:, 1, h:h + 1], None, ALU.mult)
                for s in range(2):
                    for i in range(C):
                        ins = vec.tensor_scalar(kcz[:, h % 2, s, i], kc_s[:, i, cut],
                                                zeta_ctx[:, 2 * s + i, h:h + 1], None, ALU.mult)
                ins.then_inc(kz_made, 1)

            def retention():
                def weigh_queries(h):
                    wait_drained(dve, ("qT", h))
                    q = q_t[:, h % 2, :].rearrange("p (n l) -> p n l", n=T)
                    for s, dst in ((0, q_f), (1, q_b)):
                        ins = vec.tensor_tensor(dst[:, h % 2, :].rearrange("p (n l) -> p n l", n=T), q,
                                                xi[:, s, h, :].unsqueeze(1).broadcast_to([P, T, P]), ALU.mult)
                    ins.then_inc(q_made, 1)

                def states(h):
                    wait_drained(dve, ("kv0", h))
                    for j in range(T - 1):
                        if j:
                            wait_drained(dve, ("kv", h, j - 1))
                        wait_full(dve, ("kv", h, j))
                        for s in range(2):
                            ins = vec.scalar_tensor_tensor(
                                state[:, s, j + 1, :], state[:, s, j, :], zeta[:, 4 + s, h:h + 1],
                                bank(("kv", h, j))[:, s * DV:(s + 1) * DV], ALU.mult, ALU.add)
                        ins.then_inc(dve_drained, 1)
                    wait_full(dve, ("sc", h))
                    vec.tensor_tensor(sm[:, h % 2, :].rearrange("p (n l) -> p n l", n=T),
                                      bank(("sc", h)).rearrange("p (n l) -> p n l", n=T),
                                      mask[:, h, :].unsqueeze(1).broadcast_to([P, T, P]), ALU.mult)\
                        .then_inc(dve_drained, 1)

                weigh_queries(0)
                states(0)
                low_part(number_of["g0"], 1)
                for h in range(1, HEADS):
                    weigh_keys(h)
                    weigh_queries(h)
                    states(h)

            def o_moments_made():
                wait_drained(dve, ("o", HEADS - 1, 1))
                for i in range(T):
                    for h in range(HEADS):
                        ins = vec.bn_stats(o_stats[:, i * HEADS + h, :], o_s[:, i, h * DV:(h + 1) * DV])
                step(ins)
                for n in range(T * HEADS):
                    ins = vec.bn_aggr(o_moments[:, n, :], o_stats[:, n, :])
                ins.then_inc(var_ready, 1)

            def o_normalised():
                groups_of_var[0] += 1
                dve.wait_ge(rstd_ready, groups_of_var[0])
                for i in range(T):
                    for h in range(HEADS):
                        n = i * HEADS + h
                        o = o_s[:, i, h * DV:(h + 1) * DV]
                        ins = vec.tensor_scalar(o, o, o_moments[:, n, 0:1], o_rstd[:, n:n + 1],
                                                ALU.subtract, ALU.mult)
                ins.then_inc(o_normed, 1)

            def gated_retention(c):
                if c >= 2:
                    dve.wait_ge(ret_made, c - 1)
                wait_full(dve, ("oT", c))
                vec.tensor_scalar(prod[:, c % 2, :], bank(("oT", c)), cols[:, 64 + c:65 + c], cols[:, 72 + c:73 + c],
                                  ALU.mult, ALU.add).then_inc(dve_drained, 1)
                wait_drained(dve, ("oT", c))
                wait_drained(dve, (f"g{c // 4}", c % 4))
                step(vec.tensor_tensor(prod[:, c % 2, :], prod[:, c % 2, :], g_t[:, c, :], ALU.mult))
                split(r_hi[:, c, :], r_lo[:, c, :], prod[:, c % 2, :]).then_inc(ret_made, 1)

            def row_chunks(first, n):
                for m in range(first, first + n):
                    k, side = m % K, m // K
                    acc = mod_rows[:, 2 * D * side:2 * D * (side + 1)]
                    if m == 0:
                        dve.wait_ge(rows_started, 16)
                    else:
                        dve.wait_ge(rows_summed, m)
                    wait_raw(dve, ("row", m))
                    vec.scalar_tensor_tensor(acc, raw_slot(("row", m)), cols[:, k:k + 1], acc,
                                             ALU.mult, ALU.add).then_inc(rows_summed, 1)

            def gate_retention(half):
                for j in range(4):
                    wait_drained(dve, (f"ga{half}", j))
                    wait_drained(dve, (f"pa{half}", j))
                    c = 4 * half + j
                    vec.tensor_tensor(ya[:, c, :], ya[:, c, :], gate_s[:, c % 2, :], ALU.mult).then_inc(gated, 1)

            def vs_biased(half):
                dve.wait_ge(vs_rows_landed, 48)
                for i in range(T):
                    wait_full(dve, (f"vs{half}", i))
                    vec.tensor_tensor(vs_s[:, i, half * 512:(half + 1) * 512], bank((f"vs{half}", i)),
                                      vs_rows[:, 0, half * 512:(half + 1) * 512], ALU.add).then_inc(dve_drained, 1)

            def vs_normalised():
                for i in range(T + 1):
                    if i < T:
                        dve.wait_ge(gelu_done, T + i + 1)
                        moments_of(vs_s[:, i, :], v_stats[:, i, :, :], v_moments[:, i, :])
                    if i >= 1:
                        v = vs_s[:, i - 1, :]
                        step(normalise(v, v, v_moments[:, i - 1, :], v_rstd[:, i - 1:i]))
                        vec.tensor_tensor(v, v, vs_rows[:, 1, :], ALU.mult).then_inc(vs_scaled, 1)

            def gated_spatial(c):
                if c == 0:
                    dve.wait_ge(sgu_b_landed, 16)
                if c >= 2:
                    dve.wait_ge(sgu_made, c - 1)
                wait_full(dve, ("sp", c))
                vec.tensor_tensor(prod[:, c % 2, :].rearrange("p (n l) -> p n l", n=T),
                                  bank(("sp", c)).rearrange("p (n l) -> p n l", n=T),
                                  sgu_b[:, c // 2, :].unsqueeze(1).broadcast_to([P, T, P]), ALU.add)\
                    .then_inc(dve_drained, 1)
                wait_drained(dve, ("sp", c))
                wait_drained(dve, (f"u{c // 4}", c % 4))
                step(vec.tensor_tensor(prod[:, c % 2, :], prod[:, c % 2, :], u_t[:, c % 4, :], ALU.mult))
                split(s_hi[:, c, :], s_lo[:, c, :], prod[:, c % 2, :]).then_inc(sgu_made, 1)

            def mixed(half, first, last):
                for j in range(first, last):
                    c = 4 * half + j
                    if c >= 2:
                        dve.wait_ge(y_made, c - 1)
                    dve.wait_ge(pb_gated, c + 1)
                    step(vec.tensor_tensor(prod[:, c % 2, :], pb_s[:, j, :], ya[:, c, :], ALU.add))
                    split(y_hi[:, c, :], y_lo[:, c, :], prod[:, c % 2, :]).then_inc(y_made, 1)

            def residual():
                dve.wait_ge(b_o_landed, 16)
                wait_drained(dve, "cols2")
                step(vec.tensor_tensor(b_o[:, :], b_o[:, :], mod_rows[:, 0:D], ALU.mult))
                dve.wait_ge(xa_landed, 16)
                for i in range(T):
                    ins = vec.scalar_tensor_tensor(xa[:, i, :], xa[:, i, :], ALPHA, b_o[:, :], ALU.mult, ALU.add)
                step(ins)

            def mixed_out(g, i):
                half = int(g[-1])
                cut = slice(half * 512, (half + 1) * 512)
                wait_full(dve, (g, i))
                vec.tensor_tensor(xa[:, i, cut], xa[:, i, cut], bank((g, i)), ALU.add).then_inc(dve_drained, 1)
                wait_drained(dve, (g, i))
                ins = vec.bn_stats(l_stats[:, 2 * i, half, :], xa[:, i, cut])
                if half:
                    step(ins)
                    vec.bn_aggr(l_moments[:, 2 * i, :], l_stats[:, 2 * i].rearrange("p a b -> p (a b)"))\
                        .then_inc(var_ready, 1)

            def ln_stats(n, src):
                moments_of(src, l_stats[:, n, :, :], l_moments[:, n, :])

            def ln_bias(n):
                groups_of_var[0] += 1
                dve.wait_ge(rstd_ready, groups_of_var[0])
                vec.scalar_tensor_tensor(l_nmr[:, n:n + 1], l_moments[:, n, 0:1], -1.0, l_rstd[:, n:n + 1],
                                         ALU.mult, ALU.mult).then_inc(nmr_made, 1)

            def ln1_scaled(i):
                dve.wait_ge(ln1_landed, 32)
                dve.wait_ge(normed, LATE.index(2 * i) + 1)
                vec.tensor_tensor(xa[:, i, :], xa[:, i, :], ln_rows[:, 0, :], ALU.mult).then_inc(w_applied, 1)

            def ln1_bias_half(i):
                dve.wait_ge(w_applied, i + 1)
                step(vec.tensor_tensor(xa[:, i, 0:512], xa[:, i, 0:512], ln_rows[:, 1, 0:512], ALU.add))

            for gi, g in enumerate(ORDER):
                if g == "g0":
                    o_moments_made()
                if gi + 1 < len(ORDER):
                    low_part(gi + 1, 0)
                if g == "g0":
                    o_normalised()
                if g == "v1":
                    weigh_keys(0)
                if g in ("k", "q", "v0", "v1"):
                    add_bias(g)
                if g in ("vs0", "vs1"):
                    vs_biased(int(g[-1]))
                if g in ("ga0", "ga1"):
                    gate_retention(int(g[-1]))
                if g in ("gb0", "gb1"):
                    mixed(int(g[-1]), 0, 2)
                if g == "wo0":
                    residual()
                if gi + 1 < len(ORDER) and g != "v1":
                    low_part(gi + 1, 1)
                if g in ("gb0", "gb1"):
                    mixed(int(g[-1]), 2, 4)
                if g == "k":
                    log_gammas()
                    turn(k_s, 1, "k")
                if g == "q":
                    turn(q_s, 0, "q")
                    masks()
                if g == "v1":
                    retention()
                if g in ("g0", "g1"):
                    for c in range(4 * int(g[1]), 4 * int(g[1]) + 4):
                        gated_retention(c)
                if g in ROW_CHUNKS_AFTER:
                    row_chunks(4 * list(ROW_CHUNKS_AFTER).index(g), 4)
                if g == "vs1":
                    vs_normalised()
                if g in ("u0", "u1"):
                    for c in range(4 * int(g[1]), 4 * int(g[1]) + 4):
                        gated_spatial(c)
                if g == "wo0":
                    for i in range(T):
                        mixed_out(g, i)
            for i in range(T + 1):
                if i < T:
                    mixed_out("wo1", i)
                if i >= 1:
                    behind = l_stats[:, 2 * i - 1]
                    vec.bn_stats(behind[:, 0, :], xa[:, i - 1, 0:512])
                if i < T:
                    ln_bias(2 * i)
                if i >= 1:
                    dve.wait_ge(b_applied, i)
                    step(vec.bn_stats(behind[:, 1, :], xa[:, i - 1, 512:]))
                    vec.bn_aggr(l_moments[:, 2 * i - 1, :], behind.rearrange("p a b -> p (a b)")).then_inc(var_ready, 1)
                if i < T:
                    ln1_scaled(i)
                if i >= 1:
                    ln_bias(2 * i - 1)
                if i < T:
                    ln1_bias_half(i)

            for i in (T - 2, T - 1):
                wait_full(dve, ("h2T", i, 1))
                for k in range(4, K):
                    ins = vec.tensor_scalar(h2_t[:, i % 2, k, :], bank(("h2T", i, 1))[:, (k - 4) * P:(k - 3) * P],
                                            mod2[:, 8 + k:9 + k], mod2[:, k:k + 1], ALU.mult, ALU.add)
                ins.then_inc(dve_drained, 1)
            wait_full(dve, "lgT")
            vec.tensor_reduce(logits[:, :, :], bank("lgT").rearrange("p (t g e) -> p t e g", t=T, g=4)[:, :, 0:NE, :],
                              AX_X, ALU.add).then_inc(dve_drained, 1)
            wait_drained(dve, "lgT")
            step(vec.tensor_reduce(soft[:, 0, :], logits[:, :, :], AX_X, ALU.max))
            vec.tensor_tensor(logits[:, :, :], logits[:, :, :], soft[:, 0, :].unsqueeze(2).broadcast_to([P, T, NE]),
                              ALU.subtract).then_inc(exp_in, 1)
            dve.wait_ge(exp_out, 3 + 4 * HEADS)
            step(vec.tensor_reduce(soft[:, 1, :], logits[:, :, :], AX_X, ALU.add))
            step(vec.reciprocal(soft[:, 2, :], soft[:, 1, :]))
            vec.tensor_tensor(aff[:, :, :], logits[:, :, :], soft[:, 2, :].unsqueeze(2).broadcast_to([P, T, NE]),
                              ALU.mult).then_inc(exp_in, 1)
            wait_full(dve, "affT")
            for n in range(CAP // 8):
                src = bank("affT")[0:NE, :] if n == 0 else work[:, :]
                step(vec.max(top8[:, n % 2, :], src))
                ins = vec.match_replace(work[:, :], top8[:, n % 2, :], src, -1.0)
                if n == CAP // 8 - 3:
                    ins.then_inc(rounds_near_end, 1)
                    dve.wait_ge(rounds_near_end, 1)
                elif n:
                    step(ins)
                else:
                    ins.then_inc(dve_drained, 1)
                    wait_drained(dve, "affT")
            step(vec.tensor_scalar(picked[:, :], work[:, :], 0.0, None, ALU.is_lt))
            step(vec.tensor_tensor_scan(rank[:, :], picked[:, :], picked[:, :], 0.0, ALU.add, ALU.max))
            vec.tensor_tensor(rank[:, :], rank[:, :], picked[:, :], ALU.mult).then_inc(exp_in, 1)
            wait_full(dve, "posT")
            vec.tensor_scalar(pos_t[:, :, :], bank("posT")[:, 0:T * NE].rearrange("p (t e) -> p t e", t=T),
                              -1.0, None, ALU.add).then_inc(dve_drained, 1)
            wait_drained(dve, "posT")
            dve.wait_ge(acc_scaled, T)

            def expert_outputs(i, pair, last=False):
                full, own, act_side = 34 * i + 17 * pair, 34 * i + 17 * pair, 22 * i + 11 * pair
                vec.tensor_tensor(sel[:, :, :].rearrange("p t (j s) -> p t j s", j=2),
                                  slot_ramp.unsqueeze(1).unsqueeze(1).broadcast_to([P, T, 2, CAP]),
                                  pos_t[:, :, bass.ds(4 * i + 2 * pair, 2)].unsqueeze(3).broadcast_to([P, T, 2, CAP]),
                                  ALU.is_equal).then_inc(pair_dve, 1)
                dve.wait_ge(pair_full, full + 4)
                for k in range(4, 8):
                    ins = vec.tensor_scalar(xs[:, k, :], ps[:, 3, (k - 4) * P:(k - 3) * P], mod2[:, 8 + k:9 + k],
                                            mod2[:, k:k + 1], ALU.mult, ALU.add)
                ins.then_inc(pair_dve, 1)
                dve.wait_ge(pair_full, full + 6)
                dve.wait_ge(pair_dve, own + 1)
                vec.tensor_copy(gate_col[0:CAP, :], ps[0:CAP, 7, 0:1])
                vec.tensor_copy(gate_col[CAP:P, :], ps[CAP:P, 7, 1:2]).then_inc(pair_dve, 1)
                dve.wait_ge(chunk_used, 48 * i + (24 * pair + 16))
                for h in range(2):
                    dve.wait_ge(pair_act, act_side + (6 + h))
                    vec.tensor_tensor(hid[:, h * 512:(h + 1) * 512], ps[:, 2 + h, :],
                                      silu_s[:, h * 512:(h + 1) * 512], ALU.mult).then_inc(pair_dve, 1)
                dve.wait_ge(pair_dve, own + 5)
                for h in range(2):
                    if h == 0:
                        dve.wait_ge(pair_full, full + 9)
                    else:
                        dve.wait_ge(chunk_used, 48 * i + (24 * pair + 24))
                    cut = slice(h * 512, (h + 1) * 512)
                    vec.scalar_tensor_tensor(ye[:, cut], ps[:, 6 + h, :], gate_col[:, 0:1],
                                             mod_rows[:, 3 * D + h * 512:3 * D + (h + 1) * 512],
                                             ALU.mult, ALU.mult).then_inc(pair_dve, 1)
                    if not last:
                        dve.wait_ge(pair_act, act_side + (10 + h))
                        vec.tensor_tensor(ye_lo[:, cut], ye[:, cut], ye_hi[:, cut], ALU.subtract).then_inc(pair_dve, 1)

            def add_outputs(i, pair, s):
                dst = xa[:, s // 2, (s % 2) * 512:(s % 2 + 1) * 512]
                dve.wait_ge(pair_full, 34 * i + (17 * pair + 10 + s))
                vec.tensor_tensor(dst, dst, ps[:, SCATTER_BANK[s], :], ALU.add).then_inc(pair_dve, 1)

            def two_pairs(i, last):
                for pair in range(2):
                    expert_outputs(i, pair, last and pair == 1)
                    if not (last and pair):
                        for s in range(8):
                            add_outputs(i, pair, s)

            with dve.Fori(0, PAIRS // 2 - 1) as i:
                two_pairs(i, False)
            two_pairs(PAIRS // 2 - 1, True)

            for i in range(T + 1):
                if i >= 1:
                    ln_bias(2 * T + i - 1)
                if i < T:
                    dve.wait_ge(pair_full, 17 * (PAIRS - 1) + 10 + 2 * i + 1)
                    ln_stats(2 * T + i, last_sum(i))
                if i == 1:
                    dve.wait_ge(ln2_landed, 32)
                if 1 <= i < T:
                    dve.wait_ge(normed, 2 * T + i)
                    vec.tensor_tensor(xa[:, i - 1, :], xa[:, i - 1, :], ln2_rows[:, 0, :], ALU.mult).then_inc(w_applied, 1)
            for h in range(2):
                cut = slice(h * 512, (h + 1) * 512)
                dve.wait_ge(normed, 3 * T + h)
                step(vec.tensor_tensor(xa[:, T - 1, cut], xa[:, T - 1, cut], ln2_rows[:, 0, cut], ALU.mult))
                vec.tensor_tensor(xa[:, T - 1, cut], xa[:, T - 1, cut], ln2_rows[:, 1, cut], ALU.add)\
                    .then_inc(last_ready, 1)

        @block.tensor
        def _(pe):
            mm, flip = nc.tensor.matmul, nc.tensor.transpose

            def begin(job):
                if J.before(job):
                    wait_drained(pe, J.before(job))

            def warm_up(to, times):
                for _ in range(times):
                    mm(to[:, 0:P], ones[:, :], ones[:, :], start=True, stop=True)

            pe.wait_ge(ident_landed, 16)
            pe.wait_ge(vec_landed, 16 * len(VECTORS))
            pe.wait_ge(silu_c, 1)
            begin("cols")
            flip(bank("cols")[:, 0:80], vec_rows[:, :], ident[0:80, 0:80]).then_inc(bank_full, 1)
            wait_drained(pe, "cols")
            pe.wait_ge(c_spread, 1)
            def modulation(k):
                wait_raw(pe, ("ada", k))
                w = raw_slot(("ada", k))
                for c in range(4):
                    ins = mm(bank("modrow")[32 * c:32 * c + 32, :], c_wide[:, k, :], w[:, c * 512:(c + 1) * 512],
                             start=(k == 0), stop=(k == K - 1))
                ins.then_inc(ada_used, 1)

            pe.wait_ge(set_up, 2)
            for i in range(T + C):
                pe.wait_ge(x_normed, i + 1)
                for h in range(2):
                    begin(("xT", i, h))
                    for k in range(4):
                        ins = flip(bank(("xT", i, h))[:, k * P:(k + 1) * P],
                                   x_in[:, i, (4 * h + k) * P:(4 * h + k + 1) * P], ident)
                    ins.then_inc(bank_full, 1)
                modulation(i)
            for k in range(T + C, K):
                modulation(k)
            pe.wait_ge(ada_used, K)
            pe.nop().then_inc(bank_full, 1)
            begin("mod")
            wait_drained(pe, "modrow")
            for c in range(4):
                ins = flip(bank("mod")[:, c * P:(c + 1) * P], mod_t[:, c * P:(c + 1) * P], ident)
            ins.then_inc(bank_full, 1)

            warm_up(bank("modrow"), 10)

            def product(job, a_hi, a_lo, b_hi, b_lo, first, last):
                o = bank(job)
                mm(o, a_hi, b_hi, start=first, stop=False)
                mm(o, a_hi, b_lo, start=False, stop=False)
                return mm(o, a_lo, b_hi, start=False, stop=last)

            def group(g, hi, lo, ready=None):
                gi = number_of[g]
                jobs = [(g, j) for j in range(4 + (C if g in WITH_CTX else 0))]
                for half in range(2):
                    if gi:
                        pe.wait_ge(lo_made, parts(gi, half))
                    for kk in range(4):
                        k = 4 * half + kk
                        if gi == 0:
                            pe.wait_ge(lo_made, k + 1)
                        if ready:
                            ready(k)
                        w = [x[:, half, kk * 512:(kk + 1) * 512] for x in (w_hi, w_lo)]
                        for j, job in enumerate(jobs):
                            if k == 0:
                                begin(job)
                            cut = slice(j * P, (j + 1) * P)
                            if g in WIDE:
                                ins = product(job, w[0][:, cut], w[1][:, cut], hi[:, k, :], lo[:, k, :],
                                              k == 0, k == K - 1)
                            elif j < T:
                                ins = product(job, hi[:, k, cut], lo[:, k, cut], w[0], w[1], k == 0, k == K - 1)
                            else:
                                cut = slice((j - T) * P, (j - T + 1) * P)
                                ins = product(job, hc_hi[:, k, cut], hc_lo[:, k, cut], w[0], w[1],
                                              k == 0, k == K - 1)
                            if k == K - 1:
                                ins.then_inc(bank_full, 1)
                        if k == 3:
                            ins.then_inc(half_used, 1)

            def h_ready(k):
                pe.wait_ge(h_split, k + 1)

            group("k", h_hi, h_lo, h_ready)
            group("q", h_hi, h_lo)
            group("v0", h_hi, h_lo)
            group("v1", h_hi, h_lo)

            pe.wait_ge(roped, 2 * T)

            def turn_heads(h):
                for name, src in (("qT", q_s), ("kT", k_s)):
                    begin((name, h))
                    for n in range(T):
                        ins = flip(bank((name, h))[:, n * P:(n + 1) * P], src[:, n, h * DK:(h + 1) * DK], ident)
                    ins.then_inc(bank_full, 1)

            def states(h):
                pe.wait_ge(kz_made, h + 1)
                wait_drained(pe, ("v1", T + C - 1))
                cut = slice(h * DV, (h + 1) * DV)
                begin(("kv0", h))
                for s in range(2):
                    for i in range(C):
                        ins = mm(bank(("kv0", h))[:, s * DV:(s + 1) * DV], kcz[:, h % 2, s, i, :], vc_s[:, i, cut],
                                 start=(i == 0), stop=(i == C - 1))
                ins.then_inc(bank_full, 1)
                for j in range(T - 1):
                    begin(("kv", h, j))
                    o = bank(("kv", h, j))
                    mm(o[:, 0:DV], kz[:, h % 2, 0, j, :], v_s[:, j, cut], start=True, stop=True)
                    mm(o[:, DV:2 * DV], kz[:, h % 2, 1, T - 2 - j, :], v_s[:, T - 1 - j, cut],
                       start=True, stop=True).then_inc(bank_full, 1)
                begin(("sc", h))
                wait_drained(pe, ("kT", h))
                for n in range(T):
                    cut = slice(n * P, (n + 1) * P)
                    ins = mm(bank(("sc", h))[:, cut], k_t[:, h % 2, cut], q_t[:, h % 2, cut], start=True, stop=True)
                ins.then_inc(bank_full, 1)

            def outputs(h):
                wait_drained(pe, ("sc", h))
                pe.wait_ge(q_made, h + 1)
                for j in range(2):
                    begin(("o", h, j))
                    for n in (2 * j, 2 * j + 1):
                        o = bank(("o", h, j))[:, (n % 2) * DV:(n % 2 + 1) * DV]
                        cut = slice(n * P, (n + 1) * P)
                        mm(o, sm[:, h % 2, cut], v_s[:, n, h * DV:(h + 1) * DV], start=True, stop=False)
                        mm(o, q_f[:, h % 2, cut], state[:, 0, n, :], start=False, stop=False)
                        ins = mm(o, q_b[:, h % 2, cut], state[:, 1, T - 1 - n, :], start=False, stop=True)
                    ins.then_inc(bank_full, 1)

            turn_heads(0)
            states(0)
            for h in range(HEADS):
                if h + 1 < HEADS:
                    turn_heads(h + 1)
                outputs(h)
                if h + 1 < HEADS:
                    states(h + 1)

            for half in range(2):
                group(f"g{half}", h_hi, h_lo)
                pe.wait_ge(o_normed, 1)
                for c in range(4 * half, 4 * half + 4):
                    begin(("oT", c))
                    for n in range(T):
                        ins = flip(bank(("oT", c))[:, n * P:(n + 1) * P], o_s[:, n, c * P:(c + 1) * P], ident)
                    ins.then_inc(bank_full, 1)

            def ret_ready(k):
                pe.wait_ge(ret_made, k + 1)

            group("pa0", r_hi, r_lo, ret_ready)
            group("ga0", h_hi, h_lo)
            group("pa1", r_hi, r_lo)
            group("ga1", h_hi, h_lo)
            begin("swT")
            pe.wait_ge(sw_landed, 16)
            for g in range(GROUPS):
                ins = flip(bank("swT")[:, g * P:(g + 1) * P], sw_in[:, g, :], ident)
            ins.then_inc(bank_full, 1)
            group("vs0", h_hi, h_lo)
            group("vs1", h_hi, h_lo)
            for half in range(2):
                group(f"u{half}", h_hi, h_lo)
                if half == 0:
                    pe.wait_ge(vs_made, T)
                    wait_drained(pe, "swT")
                for c in range(4 * half, 4 * half + 4):
                    begin(("sp", c))
                    for n in range(T):
                        ins = mm(bank(("sp", c))[:, n * P:(n + 1) * P], vs_s[:, n, c * P:(c + 1) * P],
                                 sw_t[:, c // 2, :], start=True, stop=True)
                    ins.then_inc(bank_full, 1)

            def sgu_ready(k):
                pe.wait_ge(sgu_made, k + 1)

            pe.wait_ge(rows_summed, 2 * K)
            for i in ROW_JOBS:
                begin(("row", i))
                mm(bank(("row", i)), ones[:, :], mod_rows[:, i * 512:(i + 1) * 512], start=True, stop=True)\
                    .then_inc(bank_full, 1)
            begin("cols2")
            for k in range(16):
                ins = mm(bank("cols2")[:, k:k + 1], mod_rows[:, D + k * P:D + (k + 1) * P], ones[:, 0:1],
                         start=True, stop=True)
            ins.then_inc(bank_full, 1)
            group("pb0", s_hi, s_lo, sgu_ready)
            group("gb0", h_hi, h_lo)
            group("pb1", s_hi, s_lo)
            group("gb1", h_hi, h_lo)

            def y_ready(k):
                pe.wait_ge(y_made, k + 1)

            def out_tile(g, j, half):
                cut = slice(j * P, (j + 1) * P)
                for k in range(4 * half, 4 * half + 4):
                    w = [x[:, half, (k % 4) * 512:(k % 4 + 1) * 512] for x in (w_hi, w_lo)]
                    ins = product((g, j), y_hi[:, k, cut], y_lo[:, k, cut], w[0], w[1], k == 0, k == K - 1)
                return ins

            pe.wait_ge(lo_made, parts(number_of["wo0"], 0))
            for k in range(4):
                y_ready(k)
            for j in range(T):
                begin(("wo0", j))
                ins = out_tile("wo0", j, 0)
            ins.then_inc(half_used, 1)
            pe.wait_ge(lo_made, parts(number_of["wo0"], 1))
            for k in range(4, K):
                y_ready(k)
            for j in range(T):
                out_tile("wo0", j, 1).then_inc(bank_full, 1)
            pe.wait_ge(lo_made, parts(number_of["wo1"], 0))
            for j, half in ((0, 0), (1, 0), (0, 1), (1, 1), (2, 0), (2, 1), (3, 0), (3, 1)):
                if half == 0:
                    begin(("wo1", j))
                    out_tile("wo1", j, 0)
                else:
                    pe.wait_ge(lo_made, parts(number_of["wo1"], 1))
                    out_tile("wo1", j, 1).then_inc(bank_full, 1)

            pe.wait_ge(router_landed, 32)
            for i in range(T):
                pe.wait_ge(normed, LATE.index(2 * i + 1) + 1)
                for h in range(2):
                    begin(("h2T", i, h))
                    for k in range(4):
                        ins = flip(bank(("h2T", i, h))[:, k * P:(k + 1) * P],
                                   h2[:, i, (4 * h + k) * P:(4 * h + k + 1) * P], ident)
                    ins.then_inc(bank_full, 1)
                begin(("lg", i))
                for m in range(2):
                    wait_drained(pe, ("h2T", i, m))
                    for q in range(2):
                        for g in (0, 1):
                            part = 2 * g + m
                            k = 4 * m + 2 * g + q
                            ins = mm(bank(("lg", i))[32 * part:32 * part + 32, 0:P], w_router[:, k, :],
                                     h2_t[:, i % 2, k, :], start=(q == 0), stop=(q == 1))
                ins.then_inc(bank_full, 1)
            begin("lgT")
            for i in range(T):
                wait_drained(pe, ("lg", i))
                ins = flip(bank("lgT")[:, i * P:(i + 1) * P], logits_t[:, i * P:(i + 1) * P], ident)
            ins.then_inc(bank_full, 1)
            begin("affT")
            pe.wait_ge(exp_in, 4)
            for i in range(T):
                ins = flip(bank("affT")[0:NE, i * P:(i + 1) * P], aff[:, i, :], ident)
            ins.then_inc(bank_full, 1)
            begin("posT")
            pe.wait_ge(rounds_near_end, 1)
            warm_up(bank("posT"), 12)
            pe.wait_ge(exp_in, 5)
            for i in range(T):
                ins = flip(bank("posT")[:, i * NE:(i + 1) * NE], rank[:, i * P:(i + 1) * P], ident[0:NE, 0:NE])
            ins.then_inc(bank_full, 1)

            warm_up(bank("affT"), 6)
            pe.wait_ge(h2_split, T)
            def pair_of_experts(i, pair, last=False):
                dve_side, act_side = 34 * i + 17 * pair, 22 * i + 11 * pair
                pe.wait_ge(pair_dve, dve_side + 1)
                for h in range(2):
                    for n in range(T):
                        for part in (h2_hi, h2_lo):
                            ins = mm(ps[:, 4 + h, :], sel[:, n, :], part[:, n, h * 512:(h + 1) * 512],
                                     start=(n == 0 and part is h2_hi), stop=(n == T - 1 and part is h2_lo))
                    ins.then_inc(pair_full, 1)
                for h in range(2):
                    pe.wait_ge(pair_act, act_side + (1 + h))
                    for k in range(4 * h, 4 * h + 4):
                        ins = flip(ps[:, 2 + h, (k % 4) * P:(k % 4 + 1) * P], x_rows[:, k * P:(k + 1) * P], ident)
                    ins.then_inc(pair_full, 1)
                def so_far(s):
                    mm(ps[:, LAST_BANK[s], :], ident, xa[:, s // 2, (s % 2) * 512:(s % 2 + 1) * 512],
                       start=True, stop=False)

                def expert_product(first_chunk, first_bank, operand, ready):
                    for k in range(K):
                        ready(k)
                        g = CHUNKS * pair + first_chunk + k
                        pe.wait_ge(ring_landed[g % RING], 48 * i + 16 * (g // RING + 1))
                        for f in range(2):
                            for e in range(2):
                                ins = mm(ps[e * CAP:(e + 1) * CAP, first_bank + f, :],
                                         operand[:, k, e * CAP:(e + 1) * CAP],
                                         ring[g % RING][:, e, f * 512:(f + 1) * 512],
                                         start=(k == 0), stop=(k == K - 1))
                            if f == 0 and first_chunk + k == CHUNKS - 1:
                                ins.then_inc(pair_full, 1)
                        ins.then_inc(chunk_used, 1)
                        if last and first_chunk + k == 2 * K + 1:
                            ready(K - 1)
                            for s in range(6):
                                so_far(s)

                def tokens_ready(k):
                    if k in (0, 2):
                        pe.wait_ge(pair_act, act_side + (3 + k // 2))
                    elif k == K // 2:
                        pe.wait_ge(pair_dve, dve_side + 2)

                def hid_ready(k):
                    if k in (0, K // 2, K - 1):
                        pe.wait_ge(pair_act, act_side + (8 + k // (K // 2)))

                expert_product(0, 0, xs, tokens_ready)
                for n in range(T):
                    ins = flip(ps[:, 6, n * P:(n + 1) * P], sel[:, n, :].bitcast(F32), ident)
                ins.then_inc(pair_full, 1)
                for n in range(T):
                    ins = mm(ps[:, 7, 0:2], sel[:, n, :].bitcast(F32), aff[:, n, bass.ds(4 * i + 2 * pair, 2)],
                             start=(n == 0), stop=(n == T - 1))
                ins.then_inc(pair_full, 1)
                expert_product(K, 2, xs, tokens_ready)
                for h in range(2):
                    pe.wait_ge(pair_dve, dve_side + (4 + h))
                    for k in range(4 * h, 4 * h + 4):
                        ins = flip(ps[:, 4 + h, (k % 4) * P:(k % 4 + 1) * P], hid[:, k * P:(k + 1) * P], ident)
                    ins.then_inc(pair_full, 1)
                expert_product(2 * K, 6, hid_t, hid_ready)
                if last:
                    for s in range(8):
                        n, h = s // 2, s % 2
                        if s < 2:
                            pe.wait_ge(pair_dve, dve_side + (6 + s))
                        if s >= 6:
                            so_far(s)
                        mm(ps[:, LAST_BANK[s], :], sel_t[:, n * P:(n + 1) * P].bitcast(F32),
                           ye[:, h * 512:(h + 1) * 512], start=False, stop=True).then_inc(pair_full, 1)
                    return
                pe.wait_ge(pair_dve, dve_side + 7)
                for s in range(8):
                    n, h = s // 2, s % 2
                    if s == 1:
                        pe.wait_ge(pair_dve, dve_side + 9)
                    if s >= 6:
                        pe.wait_ge(pair_dve, dve_side + (10 + s - 6))
                    to = ps[:, SCATTER_BANK[s], :]
                    mm(to, sel_t[:, n * P:(n + 1) * P], ye_hi[:, h * 512:(h + 1) * 512],
                       start=True, stop=False)
                    mm(to, sel_t[:, n * P:(n + 1) * P], ye_lo[:, h * 512:(h + 1) * 512],
                       start=False, stop=True).then_inc(pair_full, 1)

            with pe.Fori(0, PAIRS // 2 - 1) as i:
                pair_of_experts(i, 0)
                pair_of_experts(i, 1)
            pair_of_experts(PAIRS // 2 - 1, 0)
            pair_of_experts(PAIRS // 2 - 1, 1, last=True)


_INS = ["x", "c", "ctx", "c_ctx", "w_ada", "b_ada", "w_in", "b_in", "ret_decay_f", "ret_decay_b", "ret_gn_w",
        "ret_gn_b", "sgu_ln_w", "sgu_ln_b", "sgu_w", "sgu_b", "w_pa", "w_pb", "w_o", "b_o", "ln1_w", "ln1_b",
        "w_router", "b_router", "w_gate", "w_up", "w_down", "ln2_w", "ln2_b"]


def kernel(**inputs):
    import concourse.bacc as _bacc
    from concourse.bass_utils import run_bass_kernel_spmd as _run

    nc = _bacc.Bacc("TRN2", target_bir_lowering=False, num_devices=1)
    arrays, tensors = {}, {}
    for name in _INS:
        a = np.ascontiguousarray(inputs[name])
        arrays[f"in_{name}"] = a
        tensors[name] = nc.dram_tensor(f"in_{name}", a.shape, mybir.dt.from_np(a.dtype), kind="ExternalInput").ap()
    seq, d_model = inputs["x"].shape[1:]
    shape_table, rope = shape_constants(seq, 128)
    for name, a in (("shape_table", shape_table), ("rope", rope)):
        arrays[f"in_{name}"] = a
        tensors[name] = nc.dram_tensor(f"in_{name}", a.shape, F32, kind="ExternalInput").ap()
    tensors["out"] = nc.dram_tensor("out_0", (1, seq, d_model), F32, kind="ExternalOutput").ap()
    mixer_and_experts(nc, tensors)
    r = _run(nc, [arrays], core_ids=[0])
    return r.results[0]["out_0"]
```
